# Optimizing a Trainium2 kernel written in Bass

```python
import functools
import jax, jax.numpy as jnp
from jax import lax
import numpy as np

D_MODEL = 1024
BATCH = 1
SEQ = 256
DEPTH = 2
DEC_BATCH = 8
DEC_SEQ = 1
PAST_LEN = 2048
PAGE_SIZE = 128

HEAD_DIM = 64
D_A = 3 * D_MODEL // 8
D_B = D_MODEL // 4
D_C = D_MODEL - D_A - D_B
N_HEADS_B = D_B // HEAD_DIM
CONV_A = 3
CONV_C = 31
CHUNK = 128
D_IN = 3 * D_A + 2 * D_B + 2 * D_C
D_PLE = 256
D_FF = 11 * D_MODEL // 4
N_EXPERTS = 8
TOP_K = 2
D_EXPERT = 2 * D_MODEL
N_DENSE = (DEPTH + 1) // 2
N_MOE = DEPTH // 2
EPS = 1e-6

kernel_name = 'hybrid_conv_chunkmlp_conformer_decoder_step'

def rmsnorm(x, g):
    xf = x.astype(jnp.float32)
    y = xf * lax.rsqrt(jnp.mean(xf * xf, axis=-1, keepdims=True) + EPS)
    return (y * g.astype(jnp.float32)).astype(x.dtype)

def layernorm(x, g, b):
    xf = x.astype(jnp.float32)
    mu = jnp.mean(xf, axis=-1, keepdims=True)
    xc = xf - mu
    var = jnp.mean(xc * xc, axis=-1, keepdims=True)
    y = xc * lax.rsqrt(var + EPS) * g.astype(jnp.float32) + b.astype(jnp.float32)
    return y.astype(x.dtype)

def causal_dwconv(x, prev, w):
    xp = jnp.concatenate([prev.astype(x.dtype), x], axis=1)
    y = lax.conv_general_dilated(
        xp, w[:, None, :].astype(x.dtype), window_strides=(1,), padding='VALID',
        dimension_numbers=('NWC', 'WIO', 'NWC'), feature_group_count=x.shape[-1])
    return y, xp[:, -(w.shape[0] - 1):]

def chunk_mix(v, w_s, b_s):
    n, length, _ = v.shape
    n_chunks = -(-length // CHUNK)
    pad = n_chunks * CHUNK - length
    vp = jnp.pad(v, ((0, 0), (0, pad), (0, 0))).reshape(n, n_chunks, CHUNK, N_HEADS_B, HEAD_DIM)
    mask = jnp.tril(jnp.ones((CHUNK, CHUNK), dtype=bool))
    wm = jnp.where(mask[None], w_s, jnp.zeros_like(w_s)).astype(v.dtype)
    s = jnp.einsum('hts,ncshd->ncthd', wm, vp) + b_s.T[None, None, :, :, None].astype(v.dtype)
    return s.reshape(n, n_chunks * CHUNK, D_B)[:, :length]

def swiglu(x, w_gate, w_up, w_down):
    return (jax.nn.silu(x @ w_gate) * (x @ w_up)) @ w_down

def moe_swiglu(x, w_router, w_gate, w_up, w_down):
    logits = (x @ w_router).astype(jnp.float32)
    top_v, top_i = lax.top_k(logits, TOP_K)
    top_w = jax.nn.softmax(top_v, axis=-1)
    gates = jnp.einsum('...k,...ke->...e', top_w,
                       jax.nn.one_hot(top_i, N_EXPERTS, dtype=jnp.float32)).astype(x.dtype)
    out = jnp.zeros_like(x)
    for e in range(N_EXPERTS):
        out = out + gates[..., e:e + 1] * swiglu(x, w_gate[e], w_up[e], w_down[e])
    return out

def hybrid_layer(h, p_i, prev_a, prev_c, g_mix, w_in, w_conv_a, w_s, b_s, g_ln_b, b_ln_b,
                 w_conv_c, b_conv_c, g_ln_c, b_ln_c, g_out, w_o, g_ffn, ffn,
                 g_ple, w_ple_gate, w_ple_proj):
    n = rmsnorm(h, g_mix)
    z = n @ w_in
    o1, o2, o3 = D_A, 2 * D_A, 3 * D_A
    o4 = o3 + 2 * D_B
    gate_b, gate_c, xa = z[..., :o1], z[..., o1:o2], z[..., o2:o3]
    conv_a, new_a = causal_dwconv(gate_c * xa, prev_a, w_conv_a)
    y_a = gate_b * conv_a
    zb = jax.nn.gelu(z[..., o3:o4])
    u = zb[..., :D_B]
    v = layernorm(zb[..., D_B:], g_ln_b, b_ln_b)
    y_b = u * chunk_mix(v, w_s, b_s)
    zc = z[..., o4:]
    glu = zc[..., :D_C] * jax.nn.sigmoid(zc[..., D_C:])
    conv_c, new_c = causal_dwconv(glu, prev_c, w_conv_c)
    y_c = jax.nn.silu(layernorm(conv_c + b_conv_c, g_ln_c, b_ln_c))
    y = jnp.concatenate([rmsnorm(y_a, g_out[:D_A]),
                         rmsnorm(y_b, g_out[D_A:D_A + D_B]),
                         rmsnorm(y_c, g_out[D_A + D_B:])], axis=-1)
    h = h + y @ w_o
    h = h + ffn(rmsnorm(h, g_ffn))
    h = h + jax.nn.sigmoid(rmsnorm(h, g_ple) @ w_ple_gate) * (p_i @ w_ple_proj)
    return h, new_a, new_c, v

def setup_inputs(seed: int = 0) -> dict:
    key = jax.random.key(seed)
    ks = iter(jax.random.split(key, 40))
    f32 = jnp.float32

    def nrm(shape, scale):
        return jax.random.normal(next(ks), shape, f32) * scale

    def gain(shape):
        return 1.0 + nrm(shape, 0.05)

    return {
        'x_prompt': nrm((BATCH, SEQ, D_MODEL), 1.0),
        'x_sample': nrm((DEC_BATCH, DEC_SEQ, D_MODEL), 1.0),
        'state_conv_a': nrm((DEPTH, DEC_BATCH, CONV_A - 1, D_A), 1.0),
        'state_conv_c': nrm((DEPTH, DEC_BATCH, CONV_C - 1, D_C), 1.0),
        'p_prompt': nrm((DEPTH, BATCH, SEQ, D_PLE), 1.0),
        'p_sample': nrm((DEPTH, DEC_BATCH, DEC_SEQ, D_PLE), 1.0),
        'g_mix': gain((DEPTH, D_MODEL)),
        'w_in': nrm((DEPTH, D_MODEL, D_IN), D_MODEL ** -0.5),
        'w_conv_a': nrm((DEPTH, CONV_A, D_A), CONV_A ** -0.5),
        'w_s': nrm((DEPTH, N_HEADS_B, CHUNK, CHUNK), CHUNK ** -0.5),
        'b_s': 1.0 + nrm((DEPTH, N_HEADS_B, CHUNK), 0.1),
        'g_ln_b': gain((DEPTH, D_B)),
        'b_ln_b': nrm((DEPTH, D_B), 0.02),
        'w_conv_c': nrm((DEPTH, CONV_C, D_C), CONV_C ** -0.5),
        'b_conv_c': nrm((DEPTH, D_C), 0.02),
        'g_ln_c': gain((DEPTH, D_C)),
        'b_ln_c': nrm((DEPTH, D_C), 0.02),
        'g_out': gain((DEPTH, D_MODEL)),
        'w_o': nrm((DEPTH, D_MODEL, D_MODEL), D_MODEL ** -0.5),
        'g_ffn': gain((DEPTH, D_MODEL)),
        'w_ff_gate': nrm((N_DENSE, D_MODEL, D_FF), D_MODEL ** -0.5),
        'w_ff_up': nrm((N_DENSE, D_MODEL, D_FF), D_MODEL ** -0.5),
        'w_ff_down': nrm((N_DENSE, D_FF, D_MODEL), D_FF ** -0.5),
        'w_router': nrm((N_MOE, D_MODEL, N_EXPERTS), D_MODEL ** -0.5),
        'w_ex_gate': nrm((N_MOE, N_EXPERTS, D_MODEL, D_EXPERT), D_MODEL ** -0.5),
        'w_ex_up': nrm((N_MOE, N_EXPERTS, D_MODEL, D_EXPERT), D_MODEL ** -0.5),
        'w_ex_down': nrm((N_MOE, N_EXPERTS, D_EXPERT, D_MODEL), D_EXPERT ** -0.5),
        'g_ple': gain((DEPTH, D_MODEL)),
        'w_ple_gate': nrm((DEPTH, D_MODEL, D_MODEL), D_MODEL ** -0.5),
        'w_ple_proj': nrm((DEPTH, D_PLE, D_MODEL), D_PLE ** -0.5),
        'g_final': gain((D_MODEL,)),
    }

def reference(x_prompt, x_sample, state_conv_a, state_conv_c, p_prompt, p_sample,
              g_mix, w_in, w_conv_a, w_s, b_s, g_ln_b, b_ln_b, w_conv_c, b_conv_c,
              g_ln_c, b_ln_c, g_out, w_o, g_ffn, w_ff_gate, w_ff_up, w_ff_down,
              w_router, w_ex_gate, w_ex_up, w_ex_down, g_ple, w_ple_gate, w_ple_proj,
              g_final):
    hp, hs = x_prompt, x_sample
    na_p, na_s, nc_p, nc_s, nv_s = [], [], [], [], []
    for i in range(DEPTH):
        j = i // 2
        if i % 2 == 0:
            ffn = functools.partial(swiglu, w_gate=w_ff_gate[j], w_up=w_ff_up[j],
                                    w_down=w_ff_down[j])
        else:
            ffn = functools.partial(moe_swiglu, w_router=w_router[j], w_gate=w_ex_gate[j],
                                    w_up=w_ex_up[j], w_down=w_ex_down[j])

        def run(h, p_i, prev_a, prev_c):
            return hybrid_layer(h, p_i, prev_a, prev_c, g_mix[i], w_in[i], w_conv_a[i],
                                w_s[i], b_s[i], g_ln_b[i], b_ln_b[i], w_conv_c[i],
                                b_conv_c[i], g_ln_c[i], b_ln_c[i], g_out[i], w_o[i],
                                g_ffn[i], ffn, g_ple[i], w_ple_gate[i], w_ple_proj[i])

        zeros_a = jnp.zeros((hp.shape[0], CONV_A - 1, D_A), hp.dtype)
        zeros_c = jnp.zeros((hp.shape[0], CONV_C - 1, D_C), hp.dtype)
        hp, a_p, c_p, _ = run(hp, p_prompt[i], zeros_a, zeros_c)
        hs, a_s, c_s, v_s = run(hs, p_sample[i], state_conv_a[i], state_conv_c[i])
        na_p.append(a_p)
        na_s.append(a_s)
        nc_p.append(c_p)
        nc_s.append(c_s)
        nv_s.append(v_s)
    y_prompt = rmsnorm(hp, g_final)
    y_sample = rmsnorm(hs, g_final)
    return (y_prompt, y_sample, jnp.stack(na_p), jnp.stack(na_s), jnp.stack(nc_p),
            jnp.stack(nc_s), jnp.stack(nv_s))


_drawn_inputs = setup_inputs


def setup_inputs(seed=0):
    import zlib

    import numpy as np

    out = dict(_drawn_inputs(seed))
    spreads = {}
    factors = {'b_ln_b': 2.878, 'b_ln_c': 2.879, 'g_ple': 5.619}
    for name, (base, spread) in spreads.items():
        noise = np.random.default_rng([zlib.crc32(name.encode()), seed]).standard_normal(out[name].shape)
        drawn = base * np.exp(spread * noise) if base else spread * noise
        out[name] = __import__('jax').numpy.asarray(drawn.astype(out[name].dtype))
    for name, factor in factors.items():
        out[name] = (out[name] * factor).astype(out[name].dtype)
    return out
```

```python
from contextlib import ExitStack

import concourse.bass as bass
from concourse import mybir

F32 = mybir.dt.float32
I32 = mybir.dt.int32
ALU = mybir.AluOpType
ACT = mybir.ActivationFunctionType
AX_X = mybir.AxisListType.X

P = 128
D_MODEL, SEQ, DEPTH, NB = 1024, 256, 2, 8
HEAD = 64
D_A, D_B = 3 * D_MODEL // 8, D_MODEL // 4
D_C = D_MODEL - D_A - D_B
TAPS_A, TAPS_C = 3, 31
D_PLE, D_FF, N_EXP, D_EXP = 256, 11 * D_MODEL // 4, 8, 2 * D_MODEL
EPS = 1e-6
T = SEQ + NB
KD = D_MODEL // P
CA, CB, CC = D_A // P, D_B // P, D_C // P
NHEAD = D_B // HEAD
CHUNKS = SEQ // P
KF, KE, KP = D_FF // P, D_EXP // P, D_PLE // P
TT = CHUNKS + 1
TOKS = [P] * CHUNKS + [NB]

CAP = 96
ROUNDS = -(-T // CAP)
UNITS = ROUNDS * N_EXP

WBLOCKS = 32
RING = 6
PRE_MOE = (2 * (KD * (3 * CA + 2 * CB + 2 * CC) + KP * KD + KD * KD) + 3 * KF * KD + KD * KD) // WBLOCKS
UNIT_SLOTS = 3 * KE * KD // WBLOCKS
GU_SLOTS = 2 * KE * KD // WBLOCKS
TAIL_SLOTS = KD * KD // WBLOCKS
SLOTS = PRE_MOE + N_EXP * UNIT_SLOTS + TAIL_SLOTS
assert UNIT_SLOTS % RING == 0

PAR = {}
_at = 0
for _name, _n in (("g_mix", KD), ("g_ln_b", CB), ("b_ln_b", CB), ("b_conv_c", CC), ("g_ln_c", CC),
                  ("b_ln_c", CC), ("g_out", KD), ("g_ffn", KD), ("g_ple", KD), ("g_final", KD),
                  ("w_conv_a", CA * TAPS_A), ("w_conv_c", CC * TAPS_C), ("b_s", CB * P), ("w00", CB),
                  ("w_sT", NHEAD * P), ("w_router", KD * N_EXP)):
    PAR[_name] = (_at, _n)
    _at += _n
NPAR = _at
NST_A, NST_C = CA * NB * (TAPS_A - 1), CC * NB * (TAPS_C - 1)

N_ZC, N_ZAB = 2 * CC, 3 * CA + 2 * CB
BASE = []
_at = 0
for _l in range(DEPTH):
    _b = {}
    for _name, _n in (("zc", N_ZC), ("zab", N_ZAB), ("pp", KD), ("wo", KD),
                      ("ff", 2 * KF if _l == 0 else 0), ("down", KD if _l == 0 else 0), ("ple", KD)):
        _b[_name] = _at
        _at += _n
    BASE.append(_b)
BANKS = 4


def build(nc, wstream, x_in, p_in, par_in, state_in, y_out, a_prompt, a_sample, c_prompt, c_sample, v_sample):
    with ExitStack() as ctx:
        def sb(name, shape, dt=F32):
            return ctx.enter_context(nc.sbuf_tensor(name, shape, dt))

        def sem(name):
            return ctx.enter_context(nc.semaphore(name))

        ring = sb("ring", [P, RING, WBLOCKS, P])
        h = sb("h", [P, KD, T])
        gh = sb("gh", [P, KD, T])
        sq = sb("sq", [P, KD, T])
        pp = sb("pp", [P, KD, T])
        work = sb("work", [P, KF * T])
        par = sb("par", [P, DEPTH, NPAR])
        pe_in = sb("pe_in", [P, DEPTH, KP, T])
        sta = sb("sta", [P, DEPTH, CA, NB, TAPS_A - 1])
        stc = sb("stc", [P, DEPTH, CC, NB, TAPS_C - 1])
        xa = sb("xa", [P, CA, NB, TAPS_A])
        xc = sb("xc", [P, CC, NB, TAPS_C])
        apad = sb("apad", [P, CA, TAPS_A - 1 + SEQ])
        cpad = sb("cpad", [P, CC, TAPS_C - 1 + SEQ])
        prod = sb("prod", [P, NB * TAPS_C])
        root = sb("root", [P, T])
        rstd = sb("rstd", [P, T])
        rstd2 = sb("rstd2", [P, T])
        vtok = sb("vtok", [P, CHUNKS, D_B])
        sig = sb("sig", [P, 2, T])
        up = sb("up", [P, 2, T])
        ones = {d: sb(f"ones_{d}", [P, P]) for d in (D_MODEL, D_A, D_B, 1)}
        before = sb("before", [P, P])
        ident = sb("ident", [P, P])
        eps = sb("eps", [P, 1])
        iota = sb("iota", [P, CAP])
        lt8 = sb("lt8", [P, N_EXP, N_EXP])

        yn = work[:, 0:KD * T].rearrange("p (c t) -> p c t", t=T)
        gh_mix = yn
        ycat = work[:, KD * T:2 * KD * T].rearrange("p (c t) -> p c t", t=T)
        zb = work[:, 2 * KD * T:2 * KD * T + 2 * CB * T].rearrange("p (c t) -> p c t", t=T)
        hid = work[:, :].rearrange("p (c t) -> p c t", t=T)
        ntok = work[:, 0:TT * D_MODEL].rearrange("p (j d) -> p j d", d=D_MODEL)
        _o = TT * D_MODEL
        xg = work[:, _o:_o + KD * CAP].rearrange("p (c t) -> p c t", t=CAP)
        _o += KD * CAP
        hexp = work[:, _o:_o + KE * CAP].rearrange("p (c t) -> p c t", t=CAP)
        cv = sb("cv", [P, CC, T])
        lnb = sb("lnb", [P, CB, T])
        small = sb("small", [P, 2048])
        yT = cv[:, :, :].rearrange("p c t -> p (c t)")[:, 0:KD * CAP].rearrange("p (c t) -> p c t", t=CAP)
        ytok = small[0:CAP, 0:D_MODEL]
        GT = rstd2
        onehot = vtok[:, :, :].rearrange("p j d -> p (j d)")[:, 0:TT * CAP].rearrange("p (j t) -> p j t", t=CAP)
        gated = sb("gated", [P, TT, CAP])
        _s = [D_MODEL]

        def cut(*shape):
            n = 1
            for k in shape:
                n *= k
            v = small[:, _s[0]:_s[0] + n]
            _s[0] += n
            return v if len(shape) == 1 else v.rearrange(
                "p (a b) -> p a b", b=shape[1]) if len(shape) == 2 else v.rearrange(
                "p (a b c) -> p a b c", b=shape[1], c=shape[2])

        logit = cut(TT, N_EXP)
        beats = cut(TT, N_EXP, N_EXP)
        ties = cut(TT, N_EXP, N_EXP)
        rank = cut(TT, N_EXP)
        first = cut(TT, N_EXP)
        second = cut(TT, N_EXP)
        tmp8 = cut(TT, N_EXP)
        gate = cut(TT, N_EXP)
        top = cut(5, TT)
        place = cut(TT, UNITS + 1)
        member = cut(TT, UNITS + 1)
        weight = cut(TT, UNITS + 1)
        most = cut(1)
        flag = sb("flag", [1, 1], I32)
        assert _s[0] <= 2048

        bank = [ctx.enter_context(nc.psum_tensor(f"bank{i}", [P, 512], F32)) for i in range(8)]

        def col(l, name, i=0):
            o = PAR[name][0] + i
            return par[:, l, o:o + 1]

        def cols(l, name):
            o, n = PAR[name]
            return par[:, l, o:o + n]

        consts = sem("consts_ready")
        loaded = [sem(f"layer_inputs_loaded_{l}") for l in range(DEPTH)]
        x_loaded = sem("x_loaded")
        landed = [sem(f"slot_landed_{i}") for i in range(RING)]
        slots_used = sem("slots_used")
        over_landed = [sem(f"overflow_slot_landed_{i}") for i in range(RING)]
        over_used = sem("overflow_slots_used")
        acc_ready = sem("acc_ready")
        acc_evac = sem("acc_evacuated")
        dve_step = sem("dve_step")
        stored = sem("stored")
        flag_ready = sem("flag_ready")

        L = [{n: sem(f"{n}_{l}") for n in (
            "gh_mix", "sq_mix", "ms_mix", "root_mix", "sigmoid_zc", "glu", "gelu", "taps",
            "mean_b", "xc_b", "sq_b", "var_b", "root_b", "rs_b", "ln_b", "vt", "vtok", "mixed",
            "mean_c", "xc_c", "sq_c", "var_c", "root_c", "rs_c", "y_c", "y_a", "y_b", "ys_sq",
            "y_ms", "y_root", "yn", "gh_ffn", "sq_ffn", "ms_ffn", "root_ffn", "silu", "hid",
            "gh_ple", "sq_ple", "ms_ple", "root_ple", "sig_ple", "tails", "w_sT", "y_fin_sq", "y_fin_h")}
            for l in range(DEPTH)]
        F = {n: sem(n) for n in ("ms_fin", "root_fin", "y_fin", "normed", "turned", "ntok", "logits",
                                 "exp_in", "exp_out", "member", "ranks")}
        M = [{n: sem(f"{n}_{k}") for n in (
            "onehot", "gated", "gathered", "xg", "gu_ready", "silu", "gu_free", "gt_turned", "gt", "down",
            "yT", "y_turned", "ytok", "sc_ready", "sc_free")} for k in ("moe", "over")]

        block = ctx.enter_context(nc.Block())

        @block.sync
        def _(sp):
            sp.dma_start(h[:, :, :], x_in).then_inc(x_loaded, 16)

            def layer_inputs(l):
                sp.dma_start(par[:, l, :], par_in[l]).then_inc(loaded[l], 16)
                sp.dma_start(sta[:, l], state_in[l, :, 0:NST_A].rearrange(
                    "p (c b k) -> p c b k", c=CA, b=NB)).then_inc(loaded[l], 16)
                sp.dma_start(stc[:, l], state_in[l, :, NST_A:NST_A + NST_C].rearrange(
                    "p (c b k) -> p c b k", c=CC, b=NB)).then_inc(loaded[l], 16)
                sp.dma_start(pe_in[:, l], p_in[l]).then_inc(loaded[l], 16)

            def load(slot, pos):
                sp.dma_start(ring[:, pos], wstream[slot].rearrange("p (w n) -> p w n", n=P)).then_inc(landed[pos], 16)

            layer_inputs(0)
            for s in range(RING):
                load(s, s)
            layer_inputs(1)
            turns = (PRE_MOE + N_EXP * UNIT_SLOTS) // RING
            with sp.Fori(1, turns) as n:
                for pos in range(RING):
                    sp.wait_ge(slots_used, n * RING + (pos + 1 - RING))
                    sp.dma_start(ring[:, pos], wstream[bass.ds(n * RING + pos, 1)].rearrange(
                        "s p (w n) -> p (s w) n", n=P)).then_inc(landed[pos], 16)
            for s in range(turns * RING, PRE_MOE + N_EXP * UNIT_SLOTS):
                sp.wait_ge(slots_used, s - RING + 1)
                load(s, s % RING)
            sp.wait_ge(flag_ready, 1)
            some = sp.value_load(flag[0:1, 0:1], min_val=0, max_val=1)
            with sp.If(some > 0):
                sp.wait_ge(slots_used, PRE_MOE + N_EXP * UNIT_SLOTS)
                with sp.Fori(0, ROUNDS - 1) as r:
                    with sp.Fori(0, N_EXP) as e:
                        for j in range(UNIT_SLOTS):
                            pos = (PRE_MOE + j) % RING
                            sp.wait_ge(over_used, r * (N_EXP * UNIT_SLOTS) + e * UNIT_SLOTS + (j + 1))
                            sp.dma_start(ring[:, pos], wstream[bass.ds(e * UNIT_SLOTS + (PRE_MOE + j), 1)].rearrange(
                                "s p (w n) -> p (s w) n", n=P)).then_inc(over_landed[pos], 16)
                sp.wait_ge(over_used, (ROUNDS - 1) * N_EXP * UNIT_SLOTS + RING)
            for s in range(SLOTS - TAIL_SLOTS, SLOTS):
                sp.wait_ge(slots_used, s - RING + 1)
                load(s, s % RING)


        @block.gpsimd
        def _(pool):
            for d, t in ones.items():
                pool.memset(t[:, :], 1.0 / d).then_inc(consts, 1)
            pool.memset(eps[:, :], EPS).then_inc(consts, 1)
            pool.memset(ident[:, :], 0.0).then_inc(consts, 1)
            pool.memset(before[:, :], 1.0).then_inc(consts, 1)
            pool.memset(lt8[:, :, :], 1.0).then_inc(consts, 1)
            pool.memset(apad[:, :, 0:TAPS_A - 1], 0.0).then_inc(consts, 1)
            pool.memset(cpad[:, :, 0:TAPS_C - 1], 0.0).then_inc(consts, 1)
            pool.iota(iota[:, :], [[1, CAP]], base=0, channel_multiplier=0,
                      allow_small_or_imprecise_dtypes=True).then_inc(consts, 1)
            n = len(ones) + 7
            pool.wait_ge(consts, n)
            pool.affine_select(out=ident[:, :], in_=ident[:, :], compare_op=ALU.not_equal, fill=1.0,
                               base=0, pattern=[[-1, P]], channel_multiplier=1).then_inc(consts, 1)
            pool.affine_select(out=before[:, :], in_=before[:, :], compare_op=ALU.is_gt, fill=0.0,
                               base=0, pattern=[[1, P]], channel_multiplier=-1).then_inc(consts, 1)
            pool.affine_select(out=lt8[:, :, :], in_=lt8[:, :, :], compare_op=ALU.is_gt, fill=0.0,
                               base=0, pattern=[[1, N_EXP], [-1, N_EXP]], channel_multiplier=0).then_inc(consts, 1)
            for l in range(DEPTH):
                pool.wait_ge(loaded[l], 64)
                v = cols(l, "w_sT").rearrange("p (h t) -> p h t", t=P)
                pool.affine_select(out=v, in_=v, compare_op=ALU.is_ge, fill=0.0, base=0,
                                   pattern=[[0, NHEAD], [1, P]], channel_multiplier=-1).then_inc(L[l]["w_sT"], 1)
            for l in range(DEPTH):
                S = L[l]
                pool.wait_ge(S["glu"], 2 * CC)
                pool.dma_start(c_prompt[l], cpad[:, :, SEQ:SEQ + TAPS_C - 1]).then_inc(stored, 16)
                pool.dma_start(c_sample[l], xc[:, :, :, :]).then_inc(stored, 16)
                pool.wait_ge(S["ln_b"], CB)
                pool.dma_start(v_sample[l], lnb[:, :, SEQ:T]).then_inc(stored, 16)
                pool.wait_ge(S["y_a"], 1)
                pool.dma_start(a_prompt[l], apad[:, :, SEQ:SEQ + TAPS_A - 1]).then_inc(stored, 16)
                pool.dma_start(a_sample[l], xa[:, :, :, :]).then_inc(stored, 16)
                pool.wait_ge(stored, 80 * (l + 1))
                pool.nop().then_inc(S["tails"], 1)
            for c in range(0, KD, 4):
                pool.wait_ge(F["y_fin"], c + 4)
                pool.dma_start(y_out[:, c:c + 4, :], yn[:, c:c + 4, :]).then_inc(stored, 16)
            pool.wait_ge(stored, 16 * (5 * DEPTH + 2))

        def route(pe):
            pe.wait_ge(F["normed"], KD)
            for j in range(TT):
                for half in range(2):
                    b = (2 * j + half) % BANKS
                    if 2 * j + half >= BANKS:
                        pe.wait_ge(F["ntok"], 2 * j + half - BANKS + 1)
                    for c in range(4):
                        k = half * 4 + c
                        mm = pe.transpose(bank[b][0:TOKS[j], c * P:(c + 1) * P], gh[:, k, j * P:j * P + TOKS[j]],
                                          ident[:, :])
                    mm.then_inc(F["turned"], 1)
            wr = cols(1, "w_router").rearrange("p (k e) -> p k e", e=N_EXP)
            for j in range(TT):
                for k in range(KD):
                    mm = pe.matmul(bank[5][0:TOKS[j], j * N_EXP:(j + 1) * N_EXP], gh[:, k, j * P:j * P + TOKS[j]],
                                   wr[:, k, :], start=(k == 0), stop=(k == KD - 1))
            mm.then_inc(F["logits"], 1)
            pe.wait_ge(F["member"], 1)
            for j in range(TT + 1):
                n = TOKS[j] if j < TT else P
                for i in range(min(j, TT - 1) + 1):
                    w = before if i == j else ones[1]
                    mm = pe.matmul(bank[6][0:n, j * N_EXP:(j + 1) * N_EXP], w[0:TOKS[i], 0:n],
                                   member[0:TOKS[i], i, 0:N_EXP], start=(i == 0), stop=(i == min(j, TT - 1)))
            mm.then_inc(F["ranks"], 1)

        def experts(pe, S, units, slot_landed, slot_used, turn, prior):
            def gather():
                for k in range(KD):
                    for j in range(TT):
                        mm = pe.matmul(bank[2 + k // 4][:, (k % 4) * CAP:(k % 4 + 1) * CAP],
                                       ntok[0:TOKS[j], j, k * P:(k + 1) * P], onehot[0:TOKS[j], j, :],
                                       start=(j == 0), stop=(j == TT - 1))
                    if k % 4 == 3:
                        mm.then_inc(S["gathered"], 1)

            def turn_back(u):
                pe.wait_ge(S["yT"], 2 * u + 2)
                for k in range(KD):
                    mm = pe.transpose(bank[2 + k // 4][0:CAP, (k % 4) * P:(k % 4 + 1) * P], yT[:, k, :], ident[:, :])
                    if k % 4 == 3:
                        mm.then_inc(S["y_turned"], 1)

            def add_back(u, ks, last=None):
                for k in ks:
                    if k == 0:
                        pe.wait_ge(S["gt"], u + 1)
                        pe.wait_ge(S["ytok"], 2 * u + 2)
                    pe.wait_ge(S["sc_free"], KD * u + (k + 1))
                    pe.matmul(bank[6 + k % 2][:, 0:T], ytok[:, k * P:(k + 1) * P], GT[0:CAP, :],
                              start=True, stop=True).then_inc(S["sc_ready"], 1)

            pe.wait_ge(S["onehot"], 1)
            gather()
            with pe.Fori(0, units) as u:
                for j in range(UNIT_SLOTS):
                    pos = (PRE_MOE + j) % RING
                    if j < GU_SLOTS:
                        if j == 0:
                            pe.wait_ge(S["xg"], 2 * u + 2)
                        pe.wait_ge(S["gu_free"], GU_SLOTS * u + (j + 1))
                    elif j == GU_SLOTS:
                        pe.wait_ge(S["gu_free"], GU_SLOTS * u + (GU_SLOTS + 2))
                    pe.wait_ge(slot_landed[pos], u * (16 * (UNIT_SLOTS // RING)) + 16 * turn(j))
                    for w in range(WBLOCKS):
                        if j < GU_SLOTS:
                            i, k = divmod(w, KD)
                            mm = pe.matmul(bank[j % 2][:, i * CAP:(i + 1) * CAP], ring[:, pos, w, :], xg[:, k, :],
                                           start=(k == 0), stop=(k == KD - 1))
                        else:
                            d, k = divmod((j - GU_SLOTS) * WBLOCKS + w, KE)
                            mm = pe.matmul(bank[4 + d // 4][:, (d % 4) * CAP:(d % 4 + 1) * CAP], ring[:, pos, w, :],
                                           hexp[:, k, :], start=(k == 0), stop=(k == KE - 1))
                            if k == KE - 1 and d % 4 == 3:
                                mm.then_inc(S["down"], 1)
                        if w == 0:
                            mm.then_inc(slot_used, 1)
                    if j < GU_SLOTS:
                        mm.then_inc(S["gu_ready"], 1)
                    if j == 1:
                        turn_back(u)
                    elif j == 2:
                        add_back(u, range(0, 4))
                    elif j == 3:
                        add_back(u, range(4, 8))
                    elif j == 6:
                        pe.wait_ge(S["sc_free"], KD * u + (KD + 1))
                        for i in range(TT):
                            mm = pe.transpose(bank[6][0:CAP, i * P:i * P + TOKS[i]], gated[0:TOKS[i], i, :],
                                              ident[0:TOKS[i], 0:TOKS[i]])
                        mm.then_inc(S["gt_turned"], 1)
                    elif j == GU_SLOTS - 1:
                        pe.wait_ge(S["onehot"], u + 2)
                        gather()
            turn_back(units)
            add_back(units, range(KD))

        @block.tensor
        def _(pe):
            used = [0]

            def dense_blocks(n_blocks_done, n):
                for b in range(n_blocks_done, n_blocks_done + n):
                    s, w = divmod(b, WBLOCKS)
                    if w == 0:
                        pe.wait_ge(landed[s % RING], 16 * (s // RING + 1))
                    yield ring[:, s % RING, w, :], w == 0 and 0 < s < SLOTS - TAIL_SLOTS

            def project(first_chunk, n_chunks, rhs, k_waits=None):
                for i in range(n_chunks):
                    c = first_chunk + i
                    if c >= BANKS:
                        pe.wait_ge(acc_evac, c - BANKS + 1)
                    for k, (w, tell) in enumerate(dense_blocks(used[0], len(rhs))):
                        if i == 0 and k_waits:
                            pe.wait_ge(*k_waits[k])
                        mm = pe.matmul(bank[c % BANKS][:, 0:T], w, rhs[k], start=(k == 0), stop=(k == len(rhs) - 1))
                        if tell:
                            mm.then_inc(slots_used, 1)
                    mm.then_inc(acc_ready, 1)
                    used[0] += len(rhs)

            def average(out, d, srcs, signal, waits=None):
                for k, s in enumerate(srcs):
                    if waits:
                        pe.wait_ge(waits[0], waits[1] + k)
                    mm = pe.matmul(out[:, 0:T], ones[d][:, :], s, start=(k == 0), stop=(k == len(srcs) - 1))
                mm.then_inc(signal, 1)

            ghs = [gh[:, k, :] for k in range(KD)]
            ghs_mix = [gh_mix[:, k, :] for k in range(KD)]
            pe.wait_ge(consts, len(ones) + 10)
            for l in range(DEPTH):
                S, B = L[l], BASE[l]
                average(bank[4], D_MODEL, [sq[:, k, :] for k in range(KD)], S["ms_mix"], (S["sq_mix"], 1))
                project(B["zc"], N_ZC, ghs_mix, [(S["gh_mix"], k + 1) for k in range(KD)])
                project(B["zab"], 2 * CB, ghs_mix)
                average(bank[5], D_B, [zb[:, c, :] for c in range(CB)], S["mean_b"], (S["gelu"], 1))
                project(B["zab"] + 2 * CB, 2, ghs_mix)
                pe.wait_ge(S["sq_b"], 1)
                average(bank[5], D_B, [sq[:, c, :] for c in range(CB)], S["var_b"])
                project(B["zab"] + 2 * CB + 2, 3 * CA - 2, ghs_mix)
                pe.wait_ge(S["ln_b"], CB)
                for t in range(CHUNKS):
                    for c in range(CB):
                        mm = pe.transpose(bank[5][:, (t * CB + c) * P:(t * CB + c + 1) * P],
                                          lnb[:, c, t * P:(t + 1) * P], ident[:, :])
                mm.then_inc(S["vt"], 1)
                average_c = [cv[:, c, :] for c in range(CC)]
                pe.wait_ge(S["taps"], 1)
                average(bank[4], D_C, average_c, S["mean_c"])
                pe.wait_ge(loaded[l], 64)
                project(B["pp"], 4, [pe_in[:, l, k, :] for k in range(KP)])
                pe.wait_ge(S["vtok"], 1)
                pe.wait_ge(S["w_sT"], 1)
                wsT = cols(l, "w_sT").rearrange("p (h t) -> p h t", t=P)
                for t in range(CHUNKS):
                    for c in range(CB):
                        for j in range(2):
                            mm = pe.matmul(bank[6 + t][:, (c * 2 + j) * P:(c * 2 + j + 1) * P],
                                           vtok[:, t, c * P:(c + 1) * P], wsT[:, 2 * c + j, :], start=True, stop=True)
                mm.then_inc(S["mixed"], 1)
                pe.wait_ge(S["sq_c"], 1)
                average(bank[5], D_C, [sq[:, CB + c, :] for c in range(CC)], S["var_c"])
                project(B["pp"] + 4, KD - 4, [pe_in[:, l, k, :] for k in range(KP)])
                at = 0
                for g, (d, n) in enumerate(((D_A, CA), (D_B, CB), (D_C, CC))):
                    pe.wait_ge(S["ys_sq"], g + 1)
                    average(bank[4 + g], d, [sq[:, at + c, :] for c in range(n)], S["y_ms"])
                    at += n
                project(B["wo"], KD, [yn[:, k, :] for k in range(KD)], [(S["yn"], k + 1) for k in range(KD)])
                average(bank[4], D_MODEL, [sq[:, k, :] for k in range(KD)], S["ms_ffn"], (S["sq_ffn"], 1))
                if l == 0:
                    project(B["ff"], 2 * KF, ghs, [(S["gh_ffn"], k + 1) for k in range(KD)])
                    project(B["down"], KD, [hid[:, k, :] for k in range(KF)], [(S["hid"], k + 1) for k in range(KF)])
                else:
                    route(pe)
                    experts(pe, M[0], N_EXP, landed, slots_used, lambda j: (PRE_MOE + j) // RING + 1, 1)
                    pe.wait_ge(flag_ready, 1)
                    some = pe.value_load(flag[0:1, 0:1], min_val=0, max_val=1)
                    with pe.If(some > 0):
                        experts(pe, M[1], UNITS - N_EXP, over_landed, over_used, lambda j: j // RING + 1, 0)
                    used[0] += N_EXP * UNIT_SLOTS * WBLOCKS
                average(bank[4], D_MODEL, [sq[:, k, :] for k in range(KD)], S["ms_ple"], (S["sq_ple"], 1))
                project(B["ple"], KD, ghs, [(S["gh_ple"], k + 1) for k in range(KD)])
            average(bank[4], D_MODEL, [sq[:, k, :] for k in range(KD)], F["ms_fin"], (L[1]["y_fin_sq"], 1))

        def gu_halves(j):
            return bank[j % 2][:, 0:4 * CAP].rearrange("p (f g t) -> p g f t", g=2, t=CAP)

        sg = sig[:, :, 0:2 * CAP].rearrange("p b (f t) -> p b f t", t=CAP)

        def expert_gates(act, S, units):
            with act.Fori(0, units) as u:
                for j in range(GU_SLOTS):
                    act.wait_ge(S["gu_ready"], GU_SLOTS * u + (j + 1))
                    act.wait_ge(S["gu_free"], GU_SLOTS * u + (j + 1))
                    nc.scalar.activation(sg[:, j % 2], gu_halves(j)[:, 0], ACT.Silu).then_inc(S["silu"], 1)

        @block.scalar
        def _(act):
            def root_of(src, dst, ready, signal):
                act.wait_ge(*ready)
                nc.scalar.activation(dst[:, :], src[:, 0:T], ACT.Sqrt, bias=eps[:, :]).then_inc(signal, 1)

            act.wait_ge(consts, len(ones) + 10)
            act.wait_ge(x_loaded, 16)
            for k in range(KD):
                nc.scalar.activation(sq[:, k, :], h[:, k, :], ACT.Square).then_inc(L[0]["sq_mix"], 1)
            for l in range(DEPTH):
                S, B = L[l], BASE[l]
                root_of(bank[4], root, (S["ms_mix"], 1), S["root_mix"])
                for c in range(CC):
                    act.wait_ge(acc_evac, B["zc"] + 2 * c + 2)
                    nc.scalar.activation(sig[:, c % 2, :], pp[:, 2 * c + 1, :], ACT.Sigmoid).then_inc(S["sigmoid_zc"], 1)
                    if c == 0:
                        continue
                    if c == 1:
                        act.wait_ge(S["glu"], 2)
                for c in range(CB):
                    act.wait_ge(acc_evac, B["zab"] + c + 1)
                    nc.scalar.activation(zb[:, c, :], ycat[:, c, :], ACT.Gelu_apprx_tanh).then_inc(S["gelu"], 1)
                for c in range(CB, 2 * CB):
                    act.wait_ge(acc_evac, B["zab"] + c + 1)
                    nc.scalar.activation(zb[:, c, :], ycat[:, c, :], ACT.Gelu_apprx_tanh).then_inc(S["gelu"], 1)
                act.wait_ge(S["xc_b"], 1)
                nc.scalar.activation(sq[:, 0:CB, :], lnb[:, :, :], ACT.Square).then_inc(S["sq_b"], 1)
                root_of(bank[5], root, (S["var_b"], 1), S["root_b"])
                act.wait_ge(S["rs_b"], 1)
                for c in range(CB):
                    nc.scalar.activation(lnb[:, c, :], lnb[:, c, :], ACT.Identity, bias=col(l, "b_ln_b", c),
                                         scale=col(l, "g_ln_b", c)).then_inc(S["ln_b"], 1)
                act.wait_ge(S["xc_c"], 1)
                nc.scalar.activation(sq[:, CB:CB + CC, :], cv[:, :, :], ACT.Square).then_inc(S["sq_c"], 1)
                root_of(bank[5], root, (S["var_c"], 1), S["root_c"])
                act.wait_ge(S["rs_c"], 1)
                for c in range(CC):
                    nc.scalar.activation(ycat[:, CA + CB + c, :], cv[:, c, :], ACT.Silu, bias=col(l, "b_ln_c", c),
                                         scale=col(l, "g_ln_c", c)).then_inc(S["y_c"], 1)
                at = 0
                for g, (n, ready) in enumerate(((CA, "y_a"), (CB, "y_b"), (CC, "y_c"))):
                    act.wait_ge(S[ready], CC if g == 2 else 1)
                    nc.scalar.activation(sq[:, at:at + n, :], ycat[:, at:at + n, :], ACT.Square).then_inc(S["ys_sq"], 1)
                    at += n
                for g in range(3):
                    if g:
                        act.wait_ge(S["yn"], (0, CA, CA + CB)[g])
                    root_of(bank[4 + g], root, (S["y_ms"], g + 1), S["y_root"])
                for k in range(KD):
                    act.wait_ge(acc_evac, B["wo"] + k + 1)
                    nc.scalar.activation(sq[:, k, :], h[:, k, :], ACT.Square).then_inc(S["sq_ffn"], 1)
                root_of(bank[4], root, (S["ms_ffn"], 1), S["root_ffn"])
                if l == 0:
                    for f in range(KF):
                        act.wait_ge(acc_evac, B["ff"] + 2 * f + 1)
                        if f >= 2:
                            act.wait_ge(S["hid"], f - 1)
                        nc.scalar.activation(sig[:, f % 2, :], up[:, f % 2, :], ACT.Silu).then_inc(S["silu"], 1)
                    for k in range(KD):
                        act.wait_ge(acc_evac, B["down"] + k + 1)
                        nc.scalar.activation(sq[:, k, :], h[:, k, :], ACT.Square).then_inc(S["sq_ple"], 1)
                else:
                    act.wait_ge(F["exp_in"], 1)
                    nc.scalar.activation(top[:, 3, :], top[:, 2, :], ACT.Exp).then_inc(F["exp_out"], 1)
                    expert_gates(act, M[0], N_EXP)
                    act.wait_ge(flag_ready, 1)
                    some = act.value_load(flag[0:1, 0:1], min_val=0, max_val=1)
                    with act.If(some > 0):
                        expert_gates(act, M[1], UNITS - N_EXP)
                    for k in range(KD):
                        act.wait_ge(S["gh_ple"], k + 1)
                        nc.scalar.activation(sq[:, k, :], h[:, k, :], ACT.Square).then_inc(S["sq_ple"], 1)
                root_of(bank[4], root, (S["ms_ple"], 1), S["root_ple"])
                done = L[l + 1]["sq_mix"] if l + 1 < DEPTH else S["y_fin_sq"]
                made = L[l + 1]["gh_mix"] if l + 1 < DEPTH else S["y_fin_h"]
                for k in range(KD):
                    act.wait_ge(acc_evac, B["ple"] + k + 1)
                    nc.scalar.activation(sig[:, k % 2, :], up[:, k % 2, :], ACT.Sigmoid).then_inc(S["sig_ple"], 1)
                    if k:
                        act.wait_ge(made, k)
                        nc.scalar.activation(sq[:, k - 1, :], h[:, k - 1, :], ACT.Square).then_inc(done, 1)
                act.wait_ge(made, KD)
                nc.scalar.activation(sq[:, KD - 1, :], h[:, KD - 1, :], ACT.Square).then_inc(done, 1)
            root_of(bank[4], root, (F["ms_fin"], 1), F["root_fin"])

        def route_tokens(dve, link, S):
            v = nc.vector
            dve.wait_ge(S["gh_ffn"], KD)
            for k in range(KD):
                v.tensor_tensor(gh[:, k, :], gh[:, k, :], rstd[:, :], ALU.mult).then_inc(F["normed"], 1)
            link(v.memset(logit, 0.0))
            for j in range(TT):
                for half in range(2):
                    i = 2 * j + half
                    dve.wait_ge(F["turned"], i + 1)
                    v.tensor_copy(ntok[0:TOKS[j], j, half * 512:(half + 1) * 512],
                                  bank[i % BANKS][0:TOKS[j], :]).then_inc(F["ntok"], 1)
            dve.wait_ge(F["logits"], 1)
            for j in range(TT):
                i = v.tensor_copy(logit[0:TOKS[j], j, :], bank[5][0:TOKS[j], j * N_EXP:(j + 1) * N_EXP])
            link(i)
            shape = [P, TT, N_EXP, N_EXP]
            others = logit.unsqueeze(2).to_broadcast(shape)
            mine = logit.unsqueeze(3).to_broadcast(shape)
            for j in range(TT):
                v.tensor_tensor(beats[:, j], others[:, j], mine[:, j], ALU.is_gt)
                link(v.tensor_tensor(ties[:, j], others[:, j], mine[:, j], ALU.is_equal))
                link(v.tensor_tensor(ties[:, j], ties[:, j], lt8[:, :, :], ALU.mult))
            link(v.tensor_tensor(beats, beats, ties, ALU.add))
            link(v.tensor_reduce(rank, beats, AX_X, ALU.add))
            v.tensor_scalar(first, rank, 0.0, None, ALU.is_equal)
            link(v.tensor_scalar(second, rank, 1.0, None, ALU.is_equal))
            link(v.tensor_tensor(tmp8, logit, first, ALU.mult))
            link(v.tensor_reduce(top[:, 0, :], tmp8, AX_X, ALU.add))
            link(v.tensor_tensor(tmp8, logit, second, ALU.mult))
            link(v.tensor_reduce(top[:, 1, :], tmp8, AX_X, ALU.add))
            v.tensor_tensor(top[:, 2, :], top[:, 1, :], top[:, 0, :], ALU.subtract).then_inc(F["exp_in"], 1)
            for r in range(ROUNDS + 1):
                n = min(N_EXP, UNITS + 1 - r * N_EXP)
                i = v.tensor_tensor(member[:, :, r * N_EXP:r * N_EXP + n], first[:, :, 0:n], second[:, :, 0:n], ALU.add)
            i.then_inc(F["member"], 1)
            dve.wait_ge(F["exp_out"], 1)
            link(v.tensor_scalar(top[:, 4, :], top[:, 3, :], 1.0, None, ALU.add))
            link(v.reciprocal(top[:, 0, :], top[:, 4, :]))
            link(v.tensor_tensor(top[:, 1, :], top[:, 3, :], top[:, 0, :], ALU.mult))
            full = [P, TT, N_EXP]
            link(v.tensor_tensor(first, first, top[:, 0, :].unsqueeze(2).to_broadcast(full), ALU.mult))
            link(v.tensor_tensor(second, second, top[:, 1, :].unsqueeze(2).to_broadcast(full), ALU.mult))
            for r in range(ROUNDS + 1):
                n = min(N_EXP, UNITS + 1 - r * N_EXP)
                i = v.tensor_tensor(weight[:, :, r * N_EXP:r * N_EXP + n], first[:, :, 0:n], second[:, :, 0:n], ALU.add)
            link(i)
            dve.wait_ge(F["ranks"], 1)
            link(v.memset(place, 0.0))
            for r in range(ROUNDS + 1):
                n = min(N_EXP, UNITS + 1 - r * N_EXP)
                for j in range(TT):
                    v.tensor_scalar(place[0:TOKS[j], j, r * N_EXP:r * N_EXP + n],
                                    bank[6][0:TOKS[j], j * N_EXP:j * N_EXP + n], float(r * CAP), None, ALU.subtract)
            link(v.tensor_reduce(most[0:1, :], bank[6][0:1, TT * N_EXP:(TT + 1) * N_EXP], AX_X, ALU.max))
            v.tensor_scalar(flag[0:1, 0:1], most[0:1, :], float(CAP), None, ALU.is_gt).then_inc(flag_ready, 1)
            dve.wait_ge(flag_ready, 1)

        def expert_rows(dve, S, units, first_unit):
            v = nc.vector

            def one_hot(u, what, out):
                for j in range(TT):
                    n = TOKS[j]
                    i = v.tensor_scalar(out[0:n, j, :], iota[0:n, :], place[0:n, j, bass.ds(u, 1)],
                                        what[0:n, j, bass.ds(u, 1)], ALU.is_equal, ALU.mult)
                return i

            def sums(u, ks):
                for k in ks:
                    dve.wait_ge(S["sc_ready"], KD * u + (k + 1))
                    v.tensor_tensor(h[:, k, :], h[:, k, :], bank[6 + k % 2][:, 0:T], ALU.add).then_inc(S["sc_free"], 1)

            def rows_out(u):
                for half in range(2):
                    dve.wait_ge(S["y_turned"], 2 * u + (half + 1))
                    v.tensor_copy(ytok[:, half * 512:(half + 1) * 512], bank[2 + half][0:CAP, :]).then_inc(S["ytok"], 1)

            def rows_in(u):
                for half in range(2):
                    dve.wait_ge(S["gathered"], 2 * u + (half + 1))
                    v.tensor_copy(xg[:, half * 4:half * 4 + 4, :].rearrange("p c t -> p (c t)"),
                                  bank[2 + half][:, 0:4 * CAP]).then_inc(S["xg"], 1)

            for half in range(2):
                v.memset(yT[:, half * 4:half * 4 + 4, :], 0.0).then_inc(S["yT"], 1)
            v.memset(GT[0:CAP, :], 0.0).then_inc(S["gt"], 1)
            one_hot(first_unit, member, onehot).then_inc(S["onehot"], 1)
            dve.wait_ge(S["gt"], 1)
            for i in range(2):
                dve.nop().then_inc(S["gu_free"], 1)
                dve.nop().then_inc(S["sc_free"], 1)
            if first_unit:
                for i in range(RING):
                    dve.nop().then_inc(over_used, 1)
            rows_in(0)
            with dve.Fori(0, units) as u:
                one_hot(u + (first_unit + 1), member, onehot).then_inc(S["onehot"], 1)
                one_hot(u + first_unit, weight, gated).then_inc(S["gated"], 1)
                for j in range(GU_SLOTS):
                    dve.wait_ge(S["silu"], GU_SLOTS * u + (j + 1))
                    v.tensor_tensor(hexp[:, 2 * j:2 * j + 2, :], sg[:, j % 2], gu_halves(j)[:, 1], ALU.mult).then_inc(
                        S["gu_free"], 1)
                    if j == 1:
                        rows_out(u)
                    elif j == 2:
                        sums(u, range(0, 4))
                    elif j == 3:
                        sums(u, range(4, 8))
                    elif j == 6:
                        dve.wait_ge(S["gt_turned"], u + 1)
                        v.tensor_copy(GT[0:CAP, :], bank[6][0:CAP, 0:T]).then_inc(S["gt"], 1)
                rows_in(u + 1)
                for half in range(2):
                    dve.wait_ge(S["down"], 2 * u + (half + 1))
                    v.tensor_copy(yT[:, half * 4:half * 4 + 4, :].rearrange("p c t -> p (c t)"),
                                  bank[4 + half][:, 0:4 * CAP]).then_inc(S["yT"], 1)
            rows_out(units)
            sums(units, range(KD))

        @block.vector
        def _(dve):
            steps = [0]

            def link(ins):
                steps[0] += 1
                ins.then_inc(dve_step, 1)
                dve.wait_ge(dve_step, steps[0])

            def tick(ins):
                steps[0] += 1
                ins.then_inc(dve_step, 1)
                return steps[0]

            def gain(l, name, k, signal, dst=gh):
                nc.vector.tensor_scalar(dst[:, k, :], h[:, k, :], col(l, name, k), None, ALU.mult).then_inc(signal, 1)

            def reciprocal_root(ready, dst=rstd):
                dve.wait_ge(*ready)
                link(nc.vector.reciprocal(dst[:, :], root[:, :]))

            def evacuate(chunk, dst, scale=rstd):
                dve.wait_ge(acc_ready, chunk + 1)
                nc.vector.tensor_tensor(dst, bank[chunk % BANKS][:, 0:T], scale[:, :], ALU.mult).then_inc(acc_evac, 1)

            def add_to_h(chunk, k):
                dve.wait_ge(acc_ready, chunk + 1)
                nc.vector.tensor_tensor(h[:, k, :], h[:, k, :], bank[chunk % BANKS][:, 0:T], ALU.add).then_inc(acc_evac, 1)
                dve.wait_ge(acc_evac, chunk + 1)

            dve.wait_ge(consts, len(ones) + 10)
            dve.wait_ge(x_loaded, 16)
            dve.wait_ge(loaded[0], 64)
            for k in range(KD):
                gain(0, "g_mix", k, L[0]["gh_mix"], gh_mix)
            for l in range(DEPTH):
                S, B = L[l], BASE[l]
                dve.wait_ge(loaded[l], 64)
                if l:
                    dve.wait_ge(L[l - 1]["tails"], 1)
                nc.vector.tensor_copy(xa[:, :, :, 0:TAPS_A - 1], sta[:, l])
                link(nc.vector.tensor_copy(xc[:, :, :, 0:TAPS_C - 1], stc[:, l]))
                reciprocal_root((S["root_mix"], 1))

                wc = cols(l, "w_conv_c").rearrange("p (c k) -> p c k", k=TAPS_C)
                for c in range(CC):
                    evacuate(B["zc"] + 2 * c, pp[:, 2 * c, :])
                    evacuate(B["zc"] + 2 * c + 1, pp[:, 2 * c + 1, :])
                    dve.wait_ge(S["sigmoid_zc"], c + 1)
                    dve.wait_ge(acc_evac, B["zc"] + 2 * c + 1)
                    nc.vector.tensor_tensor(cpad[:, c, TAPS_C - 1:], pp[:, 2 * c, 0:SEQ], sig[:, c % 2, 0:SEQ],
                                            ALU.mult).then_inc(S["glu"], 1)
                    nc.vector.tensor_tensor(xc[:, c, :, TAPS_C - 1], pp[:, 2 * c, SEQ:T], sig[:, c % 2, SEQ:T],
                                            ALU.mult).then_inc(S["glu"], 1)
                dve.wait_ge(S["glu"], 2 * CC)

                def conv_c():
                    for k in range(TAPS_C):
                        for c in range(CC):
                            src, dst = cpad[:, c, k:k + SEQ], cv[:, c, 0:SEQ]
                            if k == 0:
                                last[c] = tick(nc.vector.tensor_scalar(dst, src, wc[:, c, 0:1], col(l, "b_conv_c", c),
                                                                       ALU.mult, ALU.add))
                            else:
                                dve.wait_ge(dve_step, last[c])
                                last[c] = tick(nc.vector.scalar_tensor_tensor(dst, src, wc[:, c, k:k + 1], dst,
                                                                              ALU.mult, ALU.add))
                            yield
                    for c in range(CC):
                        pv = prod[:, :].rearrange("p (b k) -> p b k", k=TAPS_C)
                        link(nc.vector.tensor_tensor(pv, xc[:, c], wc[:, c, :].unsqueeze(1).to_broadcast(
                            [P, NB, TAPS_C]), ALU.mult))
                        link(nc.vector.tensor_reduce(cv[:, c, SEQ:T], pv, AX_X, ALU.add))
                        link(nc.vector.tensor_scalar(cv[:, c, SEQ:T], cv[:, c, SEQ:T], col(l, "b_conv_c", c), None,
                                                     ALU.add))
                        yield
                    yield

                last = [0] * CC
                taps = conv_c()

                def some_taps(n):
                    for _ in range(n):
                        next(taps, None)

                for c in range(2 * CB):
                    evacuate(B["zab"] + c, ycat[:, c, :])
                    some_taps(8)
                dve.wait_ge(S["mean_b"], 1)
                dve.wait_ge(S["gelu"], CB)
                nc.vector.tensor_tensor(lnb[:, :, :], zb[:, 0:CB, :], bank[5][:, 0:T].unsqueeze(1).to_broadcast(
                    [P, CB, T]), ALU.subtract).then_inc(S["xc_b"], 1)

                wa = cols(l, "w_conv_a").rearrange("p (c k) -> p c k", k=TAPS_A)
                at = B["zab"] + 2 * CB
                dve.wait_ge(S["gelu"], 2 * CB)
                for c in range(CA):
                    evacuate(at + 2 * c, pp[:, 6, :])
                    some_taps(6)
                    evacuate(at + 2 * c + 1, pp[:, 7, :])
                    dve.wait_ge(acc_evac, at + 2 * c + 2)
                    nc.vector.tensor_tensor(apad[:, c, TAPS_A - 1:], pp[:, 6, 0:SEQ], pp[:, 7, 0:SEQ], ALU.mult)
                    link(nc.vector.tensor_tensor(xa[:, c, :, TAPS_A - 1], pp[:, 6, SEQ:T], pp[:, 7, SEQ:T], ALU.mult))
                    some_taps(5)
                    if c == 0:
                        reciprocal_root((S["root_b"], 1), rstd2)
                        dve.wait_ge(S["xc_b"], 1)
                        nc.vector.tensor_tensor(lnb[:, :, :], lnb[:, :, :], rstd2[:, :].unsqueeze(1).to_broadcast(
                            [P, CB, T]), ALU.mult).then_inc(S["rs_b"], 1)
                for c in range(CA):
                    evacuate(at + 2 * CA + c, ycat[:, c, :])
                    for k in range(TAPS_A):
                        src, dst = apad[:, c, k:k + SEQ], up[:, 0, 0:SEQ]
                        link(nc.vector.tensor_scalar(dst, src, wa[:, c, 0:1], None, ALU.mult) if k == 0 else
                             nc.vector.scalar_tensor_tensor(dst, src, wa[:, c, k:k + 1], dst, ALU.mult, ALU.add))
                    pv = prod[:, 0:NB * TAPS_A].rearrange("p (b k) -> p b k", k=TAPS_A)
                    link(nc.vector.tensor_tensor(pv, xa[:, c], wa[:, c, :].unsqueeze(1).to_broadcast([P, NB, TAPS_A]),
                                                 ALU.mult))
                    link(nc.vector.tensor_reduce(up[:, 0, SEQ:T], pv, AX_X, ALU.add))
                    dve.wait_ge(acc_evac, at + 2 * CA + c + 1)
                    i = nc.vector.tensor_tensor(ycat[:, c, :], ycat[:, c, :], up[:, 0, :], ALU.mult)
                    if c == CA - 1:
                        i.then_inc(S["y_a"], 1)
                    else:
                        link(i)
                    some_taps(5)
                some_taps(TAPS_C * CC + CC + 1)
                nc.vector.tensor_copy(prod[:, 0:1], cv[:, 0, 0:1]).then_inc(S["taps"], 1)

                dve.wait_ge(S["mean_c"], 1)
                nc.vector.tensor_tensor(cv[:, :, :], cv[:, :, :], bank[4][:, 0:T].unsqueeze(1).to_broadcast([P, CC, T]),
                                        ALU.subtract).then_inc(S["xc_c"], 1)
                dve.wait_ge(S["vt"], 1)
                nc.vector.tensor_copy(vtok[:, :, :], bank[5][:, :].rearrange("p (j d) -> p j d", j=CHUNKS)).then_inc(
                    S["vtok"], 1)
                for k in range(4):
                    dve.wait_ge(acc_ready, B["pp"] + k + 1)
                    nc.vector.tensor_copy(pp[:, k, :], bank[(B["pp"] + k) % BANKS][:, 0:T]).then_inc(acc_evac, 1)
                reciprocal_root((S["root_c"], 1))
                dve.wait_ge(S["xc_c"], 1)
                nc.vector.tensor_tensor(cv[:, :, :], cv[:, :, :], rstd[:, :].unsqueeze(1).to_broadcast([P, CC, T]),
                                        ALU.mult).then_inc(S["rs_c"], 1)
                dve.wait_ge(S["mixed"], 1)
                dve.wait_ge(S["ln_b"], CB)
                bs = cols(l, "b_s").rearrange("p (c t) -> p c t", t=P)
                for t in range(CHUNKS):
                    for j in range(2):
                        rows = slice(HEAD * j, HEAD * (j + 1))
                        src = bank[6 + t][rows, :].rearrange("p (c j t) -> p j c t", j=2, t=P)[:, j]
                        nc.vector.tensor_tensor(ycat[rows, CA:CA + CB, t * P:(t + 1) * P], src, bs[rows], ALU.add)
                for c in range(CB):
                    i = nc.vector.tensor_scalar(ycat[:, CA + c, SEQ:T], lnb[:, c, SEQ:T], col(l, "w00", c),
                                                bs[:, c, 0:1], ALU.mult, ALU.add)
                link(i)
                dve.wait_ge(S["gelu"], 2 * CB)
                nc.vector.tensor_tensor(ycat[:, CA:CA + CB, :], ycat[:, CA:CA + CB, :], zb[:, CB:2 * CB, :],
                                        ALU.mult).then_inc(S["y_b"], 1)
                for k in range(4, KD):
                    dve.wait_ge(acc_ready, B["pp"] + k + 1)
                    nc.vector.tensor_copy(pp[:, k, :], bank[(B["pp"] + k) % BANKS][:, 0:T]).then_inc(acc_evac, 1)

                dve.wait_ge(S["y_b"], 1)
                dve.wait_ge(S["y_c"], CC)
                at = 0
                for g, n in enumerate((CA, CB, CC)):
                    reciprocal_root((S["y_root"], g + 1))
                    for c in range(at, at + n):
                        nc.vector.scalar_tensor_tensor(yn[:, c, :], ycat[:, c, :], col(l, "g_out", c), rstd[:, :],
                                                       ALU.mult, ALU.mult).then_inc(S["yn"], 1)
                    at += n
                for k in range(KD):
                    add_to_h(B["wo"] + k, k)
                    gain(l, "g_ffn", k, S["gh_ffn"])
                reciprocal_root((S["root_ffn"], 1))

                if l == 0:
                    for f in range(KF):
                        if f >= 2:
                            dve.wait_ge(S["silu"], f - 1)
                        evacuate(B["ff"] + 2 * f, up[:, f % 2, :])
                        evacuate(B["ff"] + 2 * f + 1, hid[:, f, :])
                        dve.wait_ge(acc_evac, B["ff"] + 2 * f + 2)
                        dve.wait_ge(S["silu"], f + 1)
                        nc.vector.tensor_tensor(hid[:, f, :], hid[:, f, :], sig[:, f % 2, :], ALU.mult).then_inc(
                            S["hid"], 1)
                    for k in range(KD):
                        add_to_h(B["down"] + k, k)
                        gain(l, "g_ple", k, S["gh_ple"])
                else:
                    route_tokens(dve, link, S)
                    expert_rows(dve, M[0], N_EXP, 0)
                    dve.wait_ge(flag_ready, 1)
                    some = dve.value_load(flag[0:1, 0:1], min_val=0, max_val=1)
                    with dve.If(some > 0):
                        expert_rows(dve, M[1], UNITS - N_EXP, N_EXP)
                    dve.wait_ge(M[0]["sc_free"], KD * (N_EXP + 1) + 2)
                    for k in range(KD):
                        gain(l, "g_ple", k, S["gh_ple"])

                reciprocal_root((S["root_ple"], 1))
                for k in range(KD):
                    if k >= 2:
                        dve.wait_ge(S["sig_ple"], k - 1)
                    evacuate(B["ple"] + k, up[:, k % 2, :])
                    dve.wait_ge(S["sig_ple"], k + 1)
                    link(nc.vector.tensor_tensor(pp[:, k, :], pp[:, k, :], sig[:, k % 2, :], ALU.mult))
                    if l + 1 < DEPTH:
                        link(nc.vector.tensor_tensor(h[:, k, :], h[:, k, :], pp[:, k, :], ALU.add))
                        gain(l + 1, "g_mix", k, L[l + 1]["gh_mix"], gh_mix)
                    else:
                        nc.vector.tensor_tensor(h[:, k, :], h[:, k, :], pp[:, k, :], ALU.add).then_inc(S["y_fin_h"], 1)
            reciprocal_root((F["root_fin"], 1))
            dve.wait_ge(L[DEPTH - 1]["y_fin_h"], KD)
            for k in range(KD):
                nc.vector.scalar_tensor_tensor(yn[:, k, :], h[:, k, :], col(0, "g_final", k), rstd[:, :], ALU.mult,
                                               ALU.mult).then_inc(F["y_fin"], 1)

def _blocks(w, order=None):
    import numpy as np
    k, n = w.shape
    b = w.reshape(k // P, P, n // P, P).transpose(2, 0, 1, 3)
    if order is not None:
        b = b[np.asarray(order)]
    return b.reshape(-1, P, P)


def _features(a):
    import numpy as np
    lead = a.shape[:-1]
    b = a.reshape(*lead, a.shape[-1] // P, P)
    return np.moveaxis(np.moveaxis(b, -1, 0), -1, 1)


def kernel(**inputs):
    import numpy as np
    import concourse.bacc as _bacc
    from concourse.bass_utils import run_bass_kernel_spmd as _run

    a = {k: np.asarray(v) for k, v in inputs.items()}
    ca = list(range(CA))
    o_gc, o_xa, o_b, o_c = CA, 2 * CA, 3 * CA, 3 * CA + 2 * CB
    in_order = [o_c + CC * j + c for c in range(CC) for j in range(2)]
    in_order += [o_b + CB + c for c in range(CB)] + [o_b + c for c in range(CB)]
    in_order += [o for c in ca for o in (o_gc + c, o_xa + c)] + ca

    def gate_up(g, u):
        b = np.stack([_blocks(g).reshape(-1, KD, P, P), _blocks(u).reshape(-1, KD, P, P)], axis=1)
        return b.reshape(-1, P, P)

    parts = []
    for l in range(DEPTH):
        parts += [_blocks(a["w_in"][l], in_order), _blocks(a["w_ple_proj"][l]), _blocks(a["w_o"][l])]
        if l == 0:
            parts += [gate_up(a["w_ff_gate"][0], a["w_ff_up"][0]), _blocks(a["w_ff_down"][0])]
        else:
            for e in range(N_EXP):
                parts += [gate_up(a["w_ex_gate"][0, e], a["w_ex_up"][0, e]), _blocks(a["w_ex_down"][0, e])]
        parts.append(_blocks(a["w_ple_gate"][l]))
    blocks = np.concatenate(parts)
    assert len(blocks) == SLOTS * WBLOCKS
    wstream = np.ascontiguousarray(blocks.reshape(SLOTS, WBLOCKS, P, P).transpose(0, 2, 1, 3)).reshape(
        SLOTS, P, WBLOCKS * P)

    def tokens(prompt, sample):
        return _features(np.concatenate([prompt.reshape(SEQ, -1), sample.reshape(NB, -1)]))

    x = np.ascontiguousarray(tokens(a["x_prompt"], a["x_sample"]))
    p = np.stack([tokens(a["p_prompt"][l], a["p_sample"][l]) for l in range(DEPTH)])
    par = np.zeros((DEPTH, P, NPAR), x.dtype)
    state = []
    heads = np.arange(D_B) // HEAD
    for l in range(DEPTH):
        put = {n: a[n][l] for n in ("g_mix", "g_ln_b", "b_ln_b", "b_conv_c", "g_ln_c", "b_ln_c", "g_out", "g_ffn",
                                    "g_ple", "w_conv_a", "w_conv_c")}
        put["g_final"] = a["g_final"]
        put["b_s"] = a["b_s"][l].T[:, heads]
        put["w00"] = a["w_s"][l][:, 0, 0][heads]
        for n, v in put.items():
            o, size = PAR[n]
            par[l, :, o:o + size] = _features(v).reshape(P, size)
        o, size = PAR["w_sT"]
        par[l, :, o:o + size] = a["w_s"][l].transpose(2, 0, 1).reshape(P, size)
        o, size = PAR["w_router"]
        par[l, :, o:o + size] = a["w_router"][0].reshape(KD, P, N_EXP).transpose(1, 0, 2).reshape(P, size)
        state.append(np.concatenate([_features(a["state_conv_a"][l]).reshape(P, -1),
                                     _features(a["state_conv_c"][l]).reshape(P, -1)], axis=1))
    arrays = {"wstream": wstream, "x_in": x, "p_in": np.ascontiguousarray(p), "par_in": par,
              "state_in": np.ascontiguousarray(np.stack(state))}
    outs = {"y_out": (P, KD, T), "a_prompt": (DEPTH, P, CA, TAPS_A - 1), "a_sample": (DEPTH, P, CA, NB, TAPS_A),
            "c_prompt": (DEPTH, P, CC, TAPS_C - 1), "c_sample": (DEPTH, P, CC, NB, TAPS_C),
            "v_sample": (DEPTH, P, CB, NB)}
    nc = _bacc.Bacc("TRN2", target_bir_lowering=False, num_devices=1)
    aps = [nc.dram_tensor(n, v.shape, F32, kind="ExternalInput").ap() for n, v in arrays.items()]
    aps += [nc.dram_tensor(n, s, F32, kind="ExternalOutput").ap() for n, s in outs.items()]
    build(nc, *aps)
    r = _run(nc, [arrays], core_ids=[0]).results[0]

    def rows(v, lead):
        v = np.moveaxis(np.moveaxis(v, 1, -1), 0, -1)
        return np.ascontiguousarray(v.reshape(*lead, -1))

    y = rows(np.asarray(r["y_out"]), (T,))
    ap, as_, cp, cs, vs = (np.asarray(r[n]) for n in ("a_prompt", "a_sample", "c_prompt", "c_sample", "v_sample"))
    return (y[0:SEQ].reshape(1, SEQ, D_MODEL), y[SEQ:].reshape(NB, 1, D_MODEL),
            np.stack([rows(v, (1, TAPS_A - 1)) for v in ap]), np.stack([rows(v[:, :, :, 1:], (NB, TAPS_A - 1)) for v in as_]),
            np.stack([rows(v, (1, TAPS_C - 1)) for v in cp]), np.stack([rows(v[:, :, :, 1:], (NB, TAPS_C - 1)) for v in cs]),
            np.stack([rows(v, (NB, 1)) for v in vs]))
```

```python
from contextlib import ExitStack

import concourse.bass as bass
from concourse import mybir

F32 = mybir.dt.float32
F32R = mybir.dt.float32r
I32 = mybir.dt.int32
ALU = mybir.AluOpType
ACT = mybir.ActivationFunctionType
AX_X = mybir.AxisListType.X

P = 128
D_MODEL, SEQ, DEPTH, NB = 1024, 256, 2, 8
HEAD = 64
D_A, D_B = 3 * D_MODEL // 8, D_MODEL // 4
D_C = D_MODEL - D_A - D_B
TAPS_A, TAPS_C = 3, 31
D_PLE, D_FF, N_EXP, D_EXP = 256, 11 * D_MODEL // 4, 8, 2 * D_MODEL
EPS = 1e-6
T = SEQ + NB
KD = D_MODEL // P
CA, CB, CC = D_A // P, D_B // P, D_C // P
NHEAD = D_B // HEAD
CHUNKS = SEQ // P
KF, KE, KP = D_FF // P, D_EXP // P, D_PLE // P
TT = CHUNKS + 1
TOKS = [P] * CHUNKS + [NB]

CAP = 128
ROUNDS = -(-T // CAP)
UNITS = ROUNDS * N_EXP

WBLOCKS = 32
RING = 3
PRE_MOE = (2 * (KD * (3 * CA + 2 * CB + 2 * CC) + KP * KD + KD * KD) + 3 * KF * KD + KD * KD) // WBLOCKS
UNIT_SLOTS = 3 * KE * KD // WBLOCKS
TAIL_SLOTS = KD * KD // WBLOCKS
SLOTS = PRE_MOE + N_EXP * UNIT_SLOTS + TAIL_SLOTS
QBLOCKS = 8
QUARTERS = WBLOCKS // QBLOCKS
SPLITS = 4
AHEAD = SPLITS - 1
UNIT_Q = UNIT_SLOTS * QUARTERS
NG = D_EXP // 512
GROUP_Q = 2 * KD * 4 // QBLOCKS
DOWN_Q0 = NG * GROUP_Q
KH = KF // 2
TURN_Q = 1
GATHER_Q = DOWN_Q0 + 2
SUMS_Q = DOWN_Q0 + 7
XG_Q = (GATHER_Q + 5, GATHER_Q + 9)
assert UNIT_SLOTS % RING == 0 and PRE_MOE % RING == 0 and UNIT_Q % SPLITS == 0 and KF % 2 == 0 and SUMS_Q + KD < UNIT_Q

PAR = {}
_at = 0
for _name, _n in (("g_mix", KD), ("g_ln_b", CB), ("b_ln_b", CB), ("b_conv_c", CC), ("g_ln_c", CC),
                  ("b_ln_c", CC), ("g_out", KD), ("g_ffn", KD), ("g_ple", KD), ("g_final", KD),
                  ("w_conv_a", CA * TAPS_A), ("w_conv_c", CC * TAPS_C), ("b_s", CB * P), ("w00", CB),
                  ("w_sT", NHEAD * P), ("w_router", KD * N_EXP)):
    PAR[_name] = (_at, _n)
    _at += _n
NPAR = _at
NST_A, NST_C = CA * NB * (TAPS_A - 1), CC * NB * (TAPS_C - 1)

N_ZC, N_ZAB = 2 * CC, 3 * CA + 2 * CB
BASE = []
_at = 0
for _l in range(DEPTH):
    _b = {}
    for _name, _n in (("zc", N_ZC), ("zab", N_ZAB), ("pp", KD), ("wo", KD),
                      ("ff", KF if _l == 0 else 0), ("down", KD if _l == 0 else 0),
                      ("ff2", KF if _l == 0 else 0), ("down2", KD if _l == 0 else 0), ("ple", KD)):
        _b[_name] = _at
        _at += _n
    BASE.append(_b)
BANKS = 4
_k = {"zc": KD, "zab": KD, "pp": KP, "wo": KD, "ff": KD, "down": KH, "ff2": KD, "down2": KH, "ple": KD}
NEED = []
_t = 0
for _b in BASE:
    _ends = sorted((v, n) for n, v in _b.items())
    for _i, (_v, _n) in enumerate(_ends):
        _stop = _ends[_i + 1][0] if _i + 1 < len(_ends) else _v + KD
        for _c in range(_v, _stop):
            _t += _k[_n]
            NEED.append(-(-_t // QBLOCKS))
DENSE_Q = PRE_MOE * QUARTERS


def dense_quarters(chunk):
    return min(NEED[chunk] + AHEAD, DENSE_Q)


def tail_quarters(k):
    return min(k + 1 + AHEAD, TAIL_SLOTS * QUARTERS)



def build(nc, wstream, x_in, p_in, par_in, state_in, y_out, a_prompt, a_sample, c_prompt, c_sample, v_sample):
    with ExitStack() as ctx:
        def sb(name, shape, dt=F32):
            return ctx.enter_context(nc.sbuf_tensor(name, shape, dt))

        def sem(name):
            return ctx.enter_context(nc.semaphore(name))

        ring = sb("ring", [P, RING, WBLOCKS * P])
        whi = sb("whi", [P, SPLITS, QBLOCKS * P], F32R)
        wlo = sb("wlo", [P, SPLITS, QBLOCKS * P], F32R)
        gh_hi, gh_lo = (sb(f"gh_{x}", [P, KD, T], F32R) for x in ("hi", "lo"))
        hid_hi, hid_lo = (sb(f"hid_{x}", [P, KH, T], F32R) for x in ("hi", "lo"))
        p_hi, p_lo = (sb(f"p_{x}", [P, KP, T], F32R) for x in ("hi", "lo"))
        xg_hi, xg_lo = (g[:, :, :].rearrange("p c t -> p (c t)")[:, 0:KD * CAP].rearrange("p (c t) -> p c t", t=CAP)
                        for g in (gh_hi, gh_lo))
        hexp_hi, hexp_lo = (g[:, :, :].rearrange("p c t -> p (c t)")[:, 0:KE * CAP].rearrange(
            "p (c t) -> p c t", t=CAP) for g in (hid_hi, hid_lo))
        h = sb("h", [P, KD, T])
        sq = sb("sq", [P, KD, T])
        pp = sb("pp", [P, KD, T])
        work = sb("work", [P, (KD + 2 * CB) * T])
        par = sb("par", [P, DEPTH, NPAR])
        pe_in = sb("pe_in", [P, KP, T])
        sta = sb("sta", [P, CA, NB, TAPS_A - 1])
        stc = sb("stc", [P, CC, NB, TAPS_C - 1])
        xa = sb("xa", [P, CA, NB, TAPS_A])
        xc = sb("xc", [P, CC, NB, TAPS_C])
        apad = sb("apad", [P, CA, TAPS_A - 1 + SEQ])
        cpad = sb("cpad", [P, CC, TAPS_C - 1 + SEQ])
        prod = sb("prod", [P, NB * TAPS_C])
        root = sb("root", [P, T])
        rstd = sb("rstd", [P, T])
        rstd2 = sb("rstd2", [P, T])
        vtok = sb("vtok", [P, CHUNKS, D_B])
        sig = sb("sig", [P, 2, T])
        up = sb("up", [P, 2, T])
        ones = {d: sb(f"ones_{d}", [P, P]) for d in (D_MODEL, D_A, D_B, 1)}
        before = sb("before", [P, P])
        ident = sb("ident", [P, P])
        eps = sb("eps", [P, 1])
        iota = sb("iota", [P, CAP])
        lt8 = sb("lt8", [P, N_EXP, N_EXP])
        cv = sb("cv", [P, CC, T])
        lnb = sb("lnb", [P, CB, T])
        small = sb("small", [P, 1024])

        ycat = work[:, 0:KD * T].rearrange("p (c t) -> p c t", t=T)
        zb = work[:, KD * T:(KD + 2 * CB) * T].rearrange("p (c t) -> p c t", t=T)
        ntok = work[:, 0:TT * D_MODEL].rearrange("p (j d) -> p j d", d=D_MODEL)
        sq_row = sq[:, :, :].rearrange("p c t -> p (c t)")
        onehot = sq_row[:, D_MODEL:D_MODEL + TT * CAP].rearrange("p (j t) -> p j t", t=CAP)
        y_hi, y_lo = (g[:, :, :].rearrange("p c t -> p (c t)")[:, KD * CAP:KD * CAP + D_MODEL]
                      for g in (gh_hi, gh_lo))
        back, next_back = (hid_hi[:, :, :].rearrange("p c t -> p (c t)")[:, KE * CAP + i * T:KE * CAP + (i + 1) * T]
                           for i in range(2))
        sg = sig[:, :, :].rearrange("p b t -> p (b t)")[:, 0:512]
        htok = [up[:, :, :].rearrange("p b t -> p (b t)")[:, 0:512], vtok[:, :, :].rearrange("p b t -> p (b t)")]
        _s = [0]

        def cut(*shape):
            n = 1
            for k in shape:
                n *= k
            v = small[:, _s[0]:_s[0] + n]
            _s[0] += n
            return v if len(shape) == 1 else v.rearrange(
                "p (a b) -> p a b", b=shape[1]) if len(shape) == 2 else v.rearrange(
                "p (a b c) -> p a b c", b=shape[1], c=shape[2])

        logit = cut(TT, N_EXP)
        beats = cut(TT, N_EXP, N_EXP)
        ties = cut(TT, N_EXP, N_EXP)
        rank = cut(TT, N_EXP)
        first = cut(TT, N_EXP)
        second = cut(TT, N_EXP)
        tmp8 = cut(TT, N_EXP)
        gate = cut(TT, N_EXP)
        top = cut(5, TT)
        place = cut(TT, UNITS + 1)
        member = cut(TT, UNITS + 1)
        weight = cut(TT, UNITS + 1)
        most = cut(1)
        weight_col = cut(TT)
        slot_gate = cut(1)
        flag = sb("flag", [1, 1], I32)
        assert _s[0] <= 1024

        bank = [ctx.enter_context(nc.psum_tensor(f"bank{i}", [P, 512], F32)) for i in range(8)]

        def col(l, name, i=0):
            o = PAR[name][0] + i
            return par[:, l, o:o + 1]

        def cols(l, name):
            o, n = PAR[name]
            return par[:, l, o:o + n]

        consts = sem("consts_ready")
        loaded = [sem(f"layer_inputs_loaded_{l}") for l in range(DEPTH)]
        par_loaded = [sem(f"parameters_loaded_{l}") for l in range(DEPTH)]
        x_loaded = sem("x_loaded")
        landed = [sem(f"slot_landed_{i}") for i in range(RING)]
        over_landed = [sem(f"overflow_slot_landed_{i}") for i in range(RING)]
        dense = {n: sem(f"{n}_dense") for n in ("hi", "lo", "used")}
        tail = {n: sem(f"{n}_tail") for n in ("hi", "lo", "used")}
        acc_ready = sem("acc_ready")
        acc_evac = sem("acc_evacuated")
        dve_step = sem("dve_step")
        stored = sem("stored")
        flag_ready = sem("flag_ready")

        L = [{n: sem(f"{n}_{l}") for n in (
            "gh_mix", "sq_mix", "ms", "root", "sigmoid_zc", "glu", "gelu", "taps",
            "mean", "centred", "squared", "variance", "root_v", "scaled", "ln_b", "vt", "vtok", "mixed",
            "y_c", "y_a", "y_b", "ys_sq", "y_ms", "y_root", "y_normed", "yn_hi", "yn", "sq_ffn",
            "gh_ple", "sq_ple", "sig_ple", "tails", "w_sT", "p_lo")} for l in range(DEPTH)]
        L[0].update({n: sem(n) for n in ("gh_ffn", "silu", "hid_f32", "hid_hi", "hid", "hid2")})
        L[1].update({n: sem(n) for n in ("y_fin_sq", "y_fin_h")})
        F = {n: sem(n) for n in ("ms_fin", "root_fin", "y_fin", "normed", "turned", "ntok", "logits",
                                 "exp_in", "exp_out", "member", "ranks")}
        M = [{n: sem(f"{n}_{k}") for n in (
            "hi", "lo", "used", "onehot", "gathered", "xg_hi", "xg_lo", "gate", "up", "silu", "htok",
            "turned", "hexp_hi", "hexp_lo", "back_turned", "next_back", "back", "down", "y_hi", "y_lo", "sc_ready", "sc_free")} for k in ("moe", "over")]

        block = ctx.enter_context(nc.Block())

        @block.sync
        def _(sp):
            sp.dma_start(h[:, :, :], x_in).then_inc(x_loaded, 16)

            def layer_inputs(l):
                sp.dma_start(sta[:, :, :, :], state_in[l, :, 0:NST_A].rearrange(
                    "p (c b k) -> p c b k", c=CA, b=NB)).then_inc(loaded[l], 16)
                sp.dma_start(stc[:, :, :, :], state_in[l, :, NST_A:NST_A + NST_C].rearrange(
                    "p (c b k) -> p c b k", c=CC, b=NB)).then_inc(loaded[l], 16)
                sp.dma_start(pe_in[:, :, :], p_in[l]).then_inc(loaded[l], 16)

            def load(slot, pos, landed=landed):
                sp.dma_start(ring[:, pos], wstream[bass.ds(slot, 1)].rearrange("s p n -> p (s n)")
                             if not isinstance(slot, int) else wstream[slot]).then_inc(
                                 landed[pos] if isinstance(landed, list) else landed, 16)

            sp.dma_start(par[:, 0, :], par_in[0]).then_inc(par_loaded[0], 16)
            load(0, 0)
            layer_inputs(0)
            for s in range(1, RING):
                load(s, s)
            def dense_slots(first, end):
                with sp.Fori(first, end) as n:
                    for pos in range(RING):
                        sp.wait_ge(dense["lo"], n * (RING * QUARTERS) + QUARTERS * (pos + 1 - RING))
                        load(n * RING + pos, pos)

            middle = PRE_MOE // RING // 2
            dense_slots(1, middle)
            sp.wait_ge(L[0]["p_lo"], KP)
            sp.wait_ge(L[0]["glu"], 2 * CC)
            sp.dma_start(par[:, 1, :], par_in[1]).then_inc(par_loaded[1], 16)
            layer_inputs(1)
            dense_slots(middle, PRE_MOE // RING)

            def unit_slots(landed, lo, e, base, js):
                for j in js:
                    sp.wait_ge(lo, base * QUARTERS + QUARTERS * (j + 1 - RING))
                    load(e * UNIT_SLOTS + (PRE_MOE + j), j % RING, landed)

            def tail_slots(lo, slots_before, first_landed):
                for j in range(TAIL_SLOTS):
                    sp.wait_ge(lo, QUARTERS * (slots_before + j + 1 - RING))
                    load(SLOTS - TAIL_SLOTS + j, j, landed if j else first_landed)

            for j in range(RING):
                sp.wait_ge(dense["lo"], QUARTERS * (PRE_MOE + j + 1 - RING))
                load(PRE_MOE + j, j)
            with sp.Fori(0, N_EXP - 1) as u:
                unit_slots(landed, M[0]["lo"], u, u * UNIT_SLOTS, range(RING, UNIT_SLOTS + RING))
            unit_slots(landed, M[0]["lo"], N_EXP - 1, (N_EXP - 1) * UNIT_SLOTS, range(RING, UNIT_SLOTS))
            sp.wait_ge(flag_ready, 1)
            some = sp.value_load(flag[0:1, 0:1], min_val=0, max_val=1)
            with sp.If(some > 0):
                over = M[1]["lo"]
                for r in range(ROUNDS - 1):
                    for j in range(RING):
                        if r:
                            sp.wait_ge(over, QUARTERS * (r * N_EXP * UNIT_SLOTS + j + 1 - RING))
                        else:
                            sp.wait_ge(M[0]["lo"], QUARTERS * (N_EXP * UNIT_SLOTS + j + 1 - RING))
                        load(PRE_MOE + j, j, over_landed if r or j else landed)
                    with sp.Fori(0, N_EXP - 1) as u:
                        unit_slots(over_landed, over, u, u * UNIT_SLOTS + r * N_EXP * UNIT_SLOTS,
                                   range(RING, UNIT_SLOTS + RING))
                    unit_slots(over_landed, over, N_EXP - 1, ((r + 1) * N_EXP - 1) * UNIT_SLOTS,
                               range(RING, UNIT_SLOTS))
                tail_slots(over, (ROUNDS - 1) * N_EXP * UNIT_SLOTS, over_landed[0])
            with sp.If(some < 1):
                tail_slots(M[0]["lo"], N_EXP * UNIT_SLOTS, landed[0])

        @block.gpsimd
        def _(pool):
            for d, t in ones.items():
                pool.memset(t[:, :], 1.0 / d).then_inc(consts, 1)
            pool.memset(eps[:, :], EPS).then_inc(consts, 1)
            pool.memset(ident[:, :], 0.0).then_inc(consts, 1)
            pool.memset(before[:, :], 1.0).then_inc(consts, 1)
            pool.memset(lt8[:, :, :], 1.0).then_inc(consts, 1)
            pool.memset(apad[:, :, 0:TAPS_A - 1], 0.0).then_inc(consts, 1)
            pool.memset(cpad[:, :, 0:TAPS_C - 1], 0.0).then_inc(consts, 1)
            pool.iota(iota[:, :], [[1, CAP]], base=0, channel_multiplier=0,
                      allow_small_or_imprecise_dtypes=True).then_inc(consts, 1)
            n = len(ones) + 7
            pool.wait_ge(consts, n)
            pool.affine_select(out=ident[:, :], in_=ident[:, :], compare_op=ALU.not_equal, fill=1.0,
                               base=0, pattern=[[-1, P]], channel_multiplier=1).then_inc(consts, 1)
            pool.affine_select(out=before[:, :], in_=before[:, :], compare_op=ALU.is_gt, fill=0.0,
                               base=0, pattern=[[1, P]], channel_multiplier=-1).then_inc(consts, 1)
            pool.affine_select(out=lt8[:, :, :], in_=lt8[:, :, :], compare_op=ALU.is_gt, fill=0.0,
                               base=0, pattern=[[1, N_EXP], [-1, N_EXP]], channel_multiplier=0).then_inc(consts, 1)
            for l in range(DEPTH):
                S = L[l]
                pool.wait_ge(par_loaded[l], 16)
                v = cols(l, "w_sT").rearrange("p (h t) -> p h t", t=P)
                pool.affine_select(out=v, in_=v, compare_op=ALU.is_ge, fill=0.0, base=0,
                                   pattern=[[0, NHEAD], [1, P]], channel_multiplier=-1).then_inc(S["w_sT"], 1)
                pool.wait_ge(S["glu"], 2 * CC)
                pool.dma_start(c_prompt[l], cpad[:, :, SEQ:SEQ + TAPS_C - 1]).then_inc(stored, 16)
                pool.dma_start(c_sample[l], xc[:, :, :, :]).then_inc(stored, 16)
                pool.wait_ge(S["ln_b"], CB)
                pool.dma_start(v_sample[l], lnb[:, :, SEQ:T]).then_inc(stored, 16)
                pool.wait_ge(S["y_a"], 1)
                pool.dma_start(a_prompt[l], apad[:, :, SEQ:SEQ + TAPS_A - 1]).then_inc(stored, 16)
                pool.dma_start(a_sample[l], xa[:, :, :, :]).then_inc(stored, 16)
                pool.wait_ge(stored, 80 * (l + 1))
                pool.nop().then_inc(S["tails"], 1)
            for c in range(0, KD, 4):
                pool.wait_ge(F["y_fin"], c + 4)
                pool.dma_start(y_out[:, c:c + 4, :], ycat[:, c:c + 4, :]).then_inc(stored, 16)
            pool.wait_ge(stored, 16 * (5 * DEPTH + 2))

        def route(pe):
            pe.wait_ge(F["normed"], KD)
            for j in range(TT):
                for half in range(2):
                    b = (2 * j + half) % BANKS
                    if 2 * j + half >= BANKS:
                        pe.wait_ge(F["ntok"], 2 * j + half - BANKS + 1)
                    for c in range(4):
                        k = half * 4 + c
                        mm = pe.transpose(bank[b][0:TOKS[j], c * P:(c + 1) * P], sq[:, k, j * P:j * P + TOKS[j]],
                                          ident[:, :])
                    mm.then_inc(F["turned"], 1)
            wr = cols(1, "w_router").rearrange("p (k e) -> p k e", e=N_EXP)
            for j in range(TT):
                for k in range(KD):
                    mm = pe.matmul(bank[5][0:TOKS[j], j * N_EXP:(j + 1) * N_EXP], sq[:, k, j * P:j * P + TOKS[j]],
                                   wr[:, k, :], start=(k == 0), stop=(k == KD - 1))
            mm.then_inc(F["logits"], 1)
            pe.wait_ge(F["member"], 1)
            for j in range(TT + 1):
                n = TOKS[j] if j < TT else P
                for i in range(min(j, TT - 1) + 1):
                    w = before if i == j else ones[1]
                    mm = pe.matmul(bank[6][0:n, j * N_EXP:(j + 1) * N_EXP], w[0:TOKS[i], 0:n],
                                   member[0:TOKS[i], i, 0:N_EXP], start=(i == 0), stop=(i == min(j, TT - 1)))
            mm.then_inc(F["ranks"], 1)

        def experts(pe, S, units):
            def gather(ks=range(KD)):
                for k in ks:
                    for j in range(TT):
                        mm = pe.matmul(bank[k // 4][:, (k % 4) * CAP:(k % 4 + 1) * CAP],
                                       ntok[0:TOKS[j], j, k * P:(k + 1) * P], onehot[0:TOKS[j], j, :],
                                       start=(j == 0), stop=(j == TT - 1))
                    if k % 4 == 3:
                        mm.then_inc(S["gathered"], 1)

            def add_back(u, k):
                if k == 0:
                    pe.wait_ge(S["back"], u + 1)
                    pe.wait_ge(S["y_lo"], 2 * u + 2)
                pe.wait_ge(S["sc_free"], KD * u + (k + 1))
                out = bank[2 + k % 2][:, 0:T]
                pe.matmul(out, y_hi[:, k * P:(k + 1) * P], back, start=True, stop=False)
                pe.matmul(out, y_lo[:, k * P:(k + 1) * P], back, start=False, stop=True).then_inc(
                    S["sc_ready"], 1)

            def turn_back(u):
                for i in range(TT):
                    pe.transpose(bank[4][:, i * P:i * P + TOKS[i]], onehot[0:TOKS[i], i, :],
                                 ident[0:TOKS[i], 0:TOKS[i]])
                for i in range(TT):
                    mm = pe.matmul(bank[4][:, T:T + 1], onehot[0:TOKS[i], i, :], weight_col[0:TOKS[i], i:i + 1],
                                   start=(i == 0), stop=(i == TT - 1))
                mm.then_inc(S["back_turned"], 1)

            def turn(n, u):
                pe.wait_ge(S["htok"], NG * u + (n + 1))
                for i in range(4):
                    mm = pe.transpose(bank[4 + n % 2][:, i * P:(i + 1) * P], htok[n % 2][:, i * P:(i + 1) * P],
                                      ident[:, :])
                mm.then_inc(S["turned"], 1)

            pe.wait_ge(S["onehot"], 1)
            gather()
            with pe.Fori(0, units) as u:
                for q in range(UNIT_Q):
                    pos = q % SPLITS
                    n, r = divmod(q, GROUP_Q)
                    if q < 4 and q % 2 == 0:
                        pe.wait_ge(S["xg_lo"], 2 * u + (q // 2 + 1))
                    elif q == GROUP_Q:
                        pe.wait_ge(S["sc_free"], KD * u + 2)
                        pe.wait_ge(S["next_back"], u + 1)
                    elif q < DOWN_Q0 and r == 0:
                        pe.wait_ge(S["htok"], NG * u + (n - 1))
                    elif q >= DOWN_Q0 and (q - DOWN_Q0) % 4 == 0:
                        pe.wait_ge(S["hexp_lo"], NG * u + ((q - DOWN_Q0) // 4 + 1))
                    pe.wait_ge(S["lo"], UNIT_Q * u + (q + 1))
                    for i in range(2):
                        cols_ = slice(i * 512, (i + 1) * 512)
                        if q < DOWN_Q0:
                            k, last = 2 * (r % 4) + i, KD - 1
                            out, xh, xl = bank[2 * (n % 2) + r // 4], xg_hi[:, k, :], xg_lo[:, k, :]
                        else:
                            k, last = q - DOWN_Q0, KE - 1
                            out, xh, xl = bank[6 + i], hexp_hi[:, k, :], hexp_lo[:, k, :]
                        mm = pe.matmul(out[:, :], xh, whi[:, pos, cols_], start=(k == 0), stop=False)
                        if i == 0:
                            mm.then_inc(S["used"], 1)
                        pe.matmul(out[:, :], xh, wlo[:, pos, cols_], start=False, stop=False)
                        mm = pe.matmul(out[:, :], xl, whi[:, pos, cols_], start=False, stop=(k == last))
                        if k == last:
                            mm.then_inc(S["down"] if q >= DOWN_Q0 else S["up"] if r // 4 else S["gate"], 1)
                    if q == TURN_Q:
                        turn_back(u)
                    elif q >= GROUP_Q and r == 1 and n <= NG:
                        turn(n - 1, u)
                    if GATHER_Q <= q < GATHER_Q + KD:
                        if q == GATHER_Q:
                            pe.wait_ge(S["onehot"], u + 2)
                        gather([q - GATHER_Q])
                    if SUMS_Q <= q < SUMS_Q + KD:
                        add_back(u, q - SUMS_Q)
            for k in range(KD):
                add_back(units, k)

        @block.tensor
        def _(pe):
            at = [0]

            def block_of(S, q, w):
                return (whi[:, q % SPLITS, w * P:(w + 1) * P], wlo[:, q % SPLITS, w * P:(w + 1) * P])

            def project(first_chunk, n_chunks, hi, lo, waits=None, S=dense):
                for i in range(n_chunks):
                    c = first_chunk + i
                    if c >= BANKS:
                        pe.wait_ge(acc_evac, c - BANKS + 1)
                    out = bank[c % BANKS][:, 0:T]
                    for k in range(len(hi)):
                        q, w = divmod(at[0], QBLOCKS)
                        if w == 0:
                            pe.wait_ge(S["lo"], q + 1)
                        if i == 0 and waits:
                            pe.wait_ge(waits, k + 1)
                        wh, wl = block_of(S, q, w)
                        mm = pe.matmul(out, wh, hi[k], start=(k == 0), stop=False)
                        if w == 0:
                            mm.then_inc(S["used"], 1)
                        pe.matmul(out, wh, lo[k], start=False, stop=False)
                        mm = pe.matmul(out, wl, hi[k], start=False, stop=(k == len(hi) - 1))
                        at[0] += 1
                    mm.then_inc(acc_ready, 1)

            def average(out, d, srcs, signal, waits=None):
                for k, s in enumerate(srcs):
                    if waits:
                        pe.wait_ge(waits[0], waits[1] + k)
                    mm = pe.matmul(out[:, 0:T], ones[d][:, :], s, start=(k == 0), stop=(k == len(srcs) - 1))
                mm.then_inc(signal, 1)

            def both(a, b, n):
                return [a[:, k, :] for k in range(n)], [b[:, k, :] for k in range(n)]

            ghs = both(gh_hi, gh_lo, KD)
            mix = both(hid_hi, hid_lo, KD)
            pe.wait_ge(consts, len(ones) + 10)
            for l in range(DEPTH):
                S, B = L[l], BASE[l]
                average(bank[4], D_MODEL, [sq[:, k, :] for k in range(KD)], S["ms"], (S["sq_mix"], 1))
                project(B["zc"], N_ZC, *mix, S["gh_mix"])
                project(B["zab"], 2 * CB, *mix)
                average(bank[5], D_B, [zb[:, c, :] for c in range(CB)], S["mean"], (S["gelu"], 1))
                project(B["zab"] + 2 * CB, 2, *mix)
                pe.wait_ge(S["squared"], 1)
                average(bank[5], D_B, [sq[:, c, :] for c in range(CB)], S["variance"])
                project(B["zab"] + 2 * CB + 2, 3 * CA - 2, *mix)
                pe.wait_ge(S["ln_b"], CB)
                for t in range(CHUNKS):
                    for c in range(CB):
                        mm = pe.transpose(bank[5][:, (t * CB + c) * P:(t * CB + c + 1) * P],
                                          lnb[:, c, t * P:(t + 1) * P], ident[:, :])
                mm.then_inc(S["vt"], 1)
                average_c = [cv[:, c, :] for c in range(CC)]
                pe.wait_ge(S["taps"], 1)
                average(bank[4], D_C, average_c, S["mean"])
                project(B["pp"], 4, *both(p_hi, p_lo, KP), S["p_lo"])
                pe.wait_ge(S["vtok"], 1)
                pe.wait_ge(S["w_sT"], 1)
                wsT = cols(l, "w_sT").rearrange("p (h t) -> p h t", t=P)
                for t in range(CHUNKS):
                    for c in range(CB):
                        for j in range(2):
                            mm = pe.matmul(bank[6 + t][:, (c * 2 + j) * P:(c * 2 + j + 1) * P],
                                           vtok[:, t, c * P:(c + 1) * P], wsT[:, 2 * c + j, :], start=True, stop=True)
                mm.then_inc(S["mixed"], 1)
                pe.wait_ge(S["squared"], 2)
                average(bank[5], D_C, [sq[:, CB + c, :] for c in range(CC)], S["variance"])
                project(B["pp"] + 4, KD - 4, *both(p_hi, p_lo, KP))
                first = 0
                for g, (d, n) in enumerate(((D_A, CA), (D_B, CB), (D_C, CC))):
                    pe.wait_ge(S["ys_sq"], g + 1)
                    average(bank[4 + g], d, [sq[:, first + c, :] for c in range(n)], S["y_ms"])
                    first += n
                project(B["wo"], KD, *mix, S["yn"])
                average(bank[4], D_MODEL, [sq[:, k, :] for k in range(KD)], S["ms"], (S["sq_ffn"], 1))
                if l == 0:
                    hids = both(hid_hi, hid_lo, KH)
                    project(B["ff"], KF, *ghs, S["gh_ffn"])
                    project(B["down"], KD, *hids, S["hid"])
                    project(B["ff2"], KF, *ghs)
                    project(B["down2"], KD, *hids, S["hid2"])
                else:
                    route(pe)
                    experts(pe, M[0], N_EXP)
                    pe.wait_ge(flag_ready, 1)
                    some = pe.value_load(flag[0:1, 0:1], min_val=0, max_val=1)
                    with pe.If(some > 0):
                        experts(pe, M[1], UNITS - N_EXP)
                    at[0] = 0
                average(bank[4], D_MODEL, [sq[:, k, :] for k in range(KD)], S["ms"], (S["sq_ple"], 1))
                project(B["ple"], KD, *ghs, S["gh_ple"], tail if l else dense)
            average(bank[4], D_MODEL, [sq[:, k, :] for k in range(KD)], F["ms_fin"], (L[1]["y_fin_sq"], 1))

        def quarter_at(q):
            return ring[:, q // QUARTERS % RING, q % QUARTERS * (QBLOCKS * P):(q % QUARTERS + 1) * (QBLOCKS * P)]

        def expert_functions(act, S, units, slot_landed, landed_before):
            def high(u, q):
                s = q // QUARTERS
                if q % QUARTERS == 0:
                    act.wait_ge(slot_landed[s % RING],
                                u * (16 * UNIT_SLOTS // RING) + 16 * (s // RING + 1 + landed_before[s % RING]))
                act.wait_ge(S["used"], UNIT_Q * u + (q + 2))
                nc.scalar.activation(whi[:, q % SPLITS, :], quarter_at(q), ACT.Copy).then_inc(S["hi"], 1)

            def gathered_high(half):
                return nc.scalar.activation(xg_hi[:, half * 4:half * 4 + 4, :].rearrange("p c t -> p (c t)"),
                                            bank[half][:, :], ACT.Copy)

            for half in range(2):
                act.wait_ge(S["gathered"], half + 1)
                gathered_high(half).then_inc(S["xg_hi"], 1)
            def result_high(u, half):
                act.wait_ge(S["down"], 2 * u + (half + 1))
                nc.scalar.activation(y_hi[:, half * 512:(half + 1) * 512], bank[6 + half][:, :],
                                     ACT.Copy, scale=slot_gate).then_inc(S["y_hi"], 1)

            with act.Fori(0, units) as u:
                nc.scalar.activation(top[:, 4, 0:1], eps[:, :], ACT.Silu)
                for q in range(UNIT_Q):
                    n, r = divmod(q, GROUP_Q)
                    if r == 2 and 1 <= n <= NG:
                        act.wait_ge(S["turned"], NG * u + n)
                        nc.scalar.activation(hexp_hi[:, 4 * n - 4:4 * n, :].rearrange("p c t -> p (c t)"),
                                             bank[4 + (n - 1) % 2][:, :], ACT.Copy).then_inc(S["hexp_hi"], 1)
                    high(u, q + AHEAD)
                    if q < 2:
                        result_high(u, q)
                    if r == 4 and n < NG:
                        act.wait_ge(S["gate"], NG * u + (n + 1))
                        if n:
                            act.wait_ge(S["htok"], NG * u + n)
                        nc.scalar.activation(sg, bank[2 * (n % 2)][:, :], ACT.Silu).then_inc(S["silu"], 1)
                    for half in range(2):
                        if q == XG_Q[half]:
                            act.wait_ge(S["gathered"], 2 * u + (half + 3))
                            gathered_high(half).then_inc(S["xg_hi"], 1)
                act.wait_ge(S["sc_ready"], KD * u + KD)
                act.wait_ge(S["next_back"], u + 1)
                nc.scalar.activation(back, next_back, ACT.Copy).then_inc(S["back"], 1)
            for half in range(2):
                result_high(units, half)

        @block.scalar
        def _(act):
            def root_of(src, dst, ready, signal):
                act.wait_ge(*ready)
                nc.scalar.activation(dst[:, :], src[:, 0:T], ACT.Sqrt, bias=eps[:, :]).then_inc(signal, 1)

            done_hi = [0]

            def high_upto(n, S=dense):
                before = 0 if S is dense else (PRE_MOE + N_EXP * UNIT_SLOTS) * QUARTERS
                for q in range(done_hi[0], n):
                    s = (before + q) // QUARTERS
                    if (before + q) % QUARTERS == 0:
                        act.wait_ge(landed[s % RING], 16 * (s // RING + 1))
                    if q >= SPLITS:
                        act.wait_ge(S["used"], q - SPLITS + 2)
                    nc.scalar.activation(whi[:, q % SPLITS, :], quarter_at(before + q), ACT.Copy).then_inc(S["hi"], 1)
                done_hi[0] = max(done_hi[0], n)

            act.wait_ge(consts, len(ones) + 10)
            high_upto(AHEAD)
            act.wait_ge(x_loaded, 16)
            for k in range(KD):
                nc.scalar.activation(sq[:, k, :], h[:, k, :], ACT.Square).then_inc(L[0]["sq_mix"], 1)
            for l in range(DEPTH):
                S, B = L[l], BASE[l]
                root_of(bank[4], root, (S["ms"], 1), S["root"])
                for c in range(CC):
                    high_upto(dense_quarters(B["zc"] + 2 * c + 1))
                    act.wait_ge(acc_evac, B["zc"] + 2 * c + 2)
                    nc.scalar.activation(sig[:, c % 2, :], pp[:, 2 * c + 1, :], ACT.Sigmoid).then_inc(S["sigmoid_zc"], 1)
                    if c == 0:
                        continue
                    if c == 1:
                        act.wait_ge(S["glu"], 2)
                for c in range(CB):
                    high_upto(dense_quarters(B["zab"] + c))
                    act.wait_ge(acc_evac, B["zab"] + c + 1)
                    nc.scalar.activation(zb[:, c, :], ycat[:, c, :], ACT.Gelu_apprx_tanh).then_inc(S["gelu"], 1)
                for c in range(CB, 2 * CB):
                    high_upto(dense_quarters(B["zab"] + c))
                    act.wait_ge(acc_evac, B["zab"] + c + 1)
                    nc.scalar.activation(zb[:, c, :], ycat[:, c, :], ACT.Gelu_apprx_tanh).then_inc(S["gelu"], 1)
                high_upto(dense_quarters(B["zab"] + 2 * CB + 1))
                act.wait_ge(S["centred"], 1)
                nc.scalar.activation(sq[:, 0:CB, :], lnb[:, :, :], ACT.Square).then_inc(S["squared"], 1)
                root_of(bank[5], root, (S["variance"], 1), S["root_v"])
                act.wait_ge(S["scaled"], 1)
                for c in range(CB):
                    nc.scalar.activation(lnb[:, c, :], lnb[:, c, :], ACT.Identity, bias=col(l, "b_ln_b", c),
                                         scale=col(l, "g_ln_b", c)).then_inc(S["ln_b"], 1)
                for c in range(2 * CB + 2, N_ZAB):
                    high_upto(dense_quarters(B["zab"] + c))
                high_upto(dense_quarters(B["pp"]))
                act.wait_ge(S["centred"], 2)
                nc.scalar.activation(sq[:, CB:CB + CC, :], cv[:, :, :], ACT.Square).then_inc(S["squared"], 1)
                root_of(bank[5], root, (S["variance"], 2), S["root_v"])
                high_upto(dense_quarters(B["pp"] + KD - 1))
                act.wait_ge(S["scaled"], 2)
                for c in range(CC):
                    nc.scalar.activation(ycat[:, CA + CB + c, :], cv[:, c, :], ACT.Silu, bias=col(l, "b_ln_c", c),
                                         scale=col(l, "g_ln_c", c)).then_inc(S["y_c"], 1)
                at = 0
                for g, (n, ready) in enumerate(((CA, "y_a"), (CB, "y_b"), (CC, "y_c"))):
                    act.wait_ge(S[ready], CC if g == 2 else 1)
                    nc.scalar.activation(sq[:, at:at + n, :], ycat[:, at:at + n, :], ACT.Square).then_inc(S["ys_sq"], 1)
                    at += n
                at = 0
                for g, n in enumerate((CA, CB, CC)):
                    root_of(bank[4 + g], root, (S["y_ms"], g + 1), S["y_root"])
                    for c in range(at, at + n):
                        act.wait_ge(S["y_normed"], c + 1)
                        nc.scalar.activation(hid_hi[:, c, :], ycat[:, c, :], ACT.Copy).then_inc(S["yn_hi"], 1)
                    at += n
                for k in range(KD):
                    high_upto(dense_quarters(B["wo"] + k))
                    act.wait_ge(acc_evac, B["wo"] + k + 1)
                    nc.scalar.activation(sq[:, k, :], h[:, k, :], ACT.Square).then_inc(S["sq_ffn"], 1)
                root_of(bank[4], root, (S["ms"], 2), S["root"])
                if l == 0:
                    for half, (ff, down, hid) in enumerate((("ff", "down", "hid"), ("ff2", "down2", "hid2"))):
                        for f in range(KH):
                            high_upto(dense_quarters(B[ff] + 2 * f))
                            act.wait_ge(acc_evac, B[ff] + 2 * f + 1)
                            n = half * KH + f
                            if n >= 2:
                                act.wait_ge(S["hid_f32"], n - 1)
                            nc.scalar.activation(sig[:, n % 2, :], up[:, n % 2, :], ACT.Silu).then_inc(S["silu"], 1)
                            high_upto(dense_quarters(B[ff] + 2 * f + 1))
                            act.wait_ge(S["hid_f32"], n + 1)
                            if half and f == 0:
                                act.wait_ge(acc_evac, B["down"] + KD)
                            nc.scalar.activation(hid_hi[:, f, :], zb[:, 2 + n % 2, :], ACT.Copy).then_inc(S["hid_hi"], 1)
                        for k in range(KD):
                            high_upto(dense_quarters(B[down] + k))
                            if half:
                                act.wait_ge(acc_evac, B[down] + k + 1)
                                nc.scalar.activation(sq[:, k, :], h[:, k, :], ACT.Square).then_inc(S["sq_ple"], 1)
                else:
                    for q in range(AHEAD):
                        if q == 0:
                            act.wait_ge(landed[0], 16 * (PRE_MOE // RING + 1))
                        act.wait_ge(acc_evac, B["wo"] + KD)
                        nc.scalar.activation(whi[:, q, :], quarter_at(q), ACT.Copy).then_inc(M[0]["hi"], 1)
                    act.wait_ge(F["exp_in"], 1)
                    nc.scalar.activation(top[:, 3, :], top[:, 2, :], ACT.Exp).then_inc(F["exp_out"], 1)
                    expert_functions(act, M[0], N_EXP, landed, [PRE_MOE // RING] * RING)
                    act.wait_ge(M[0]["hi"], N_EXP * UNIT_Q + AHEAD)
                    act.wait_ge(flag_ready, 1)
                    some = act.value_load(flag[0:1, 0:1], min_val=0, max_val=1)
                    with act.If(some > 0):
                        for _ in range(AHEAD):
                            act.nop().then_inc(M[1]["hi"], 1)
                        expert_functions(act, M[1], UNITS - N_EXP, over_landed, [-1] + [0] * (RING - 1))
                        act.wait_ge(M[1]["hi"], (UNITS - N_EXP) * UNIT_Q + AHEAD)
                    for _ in range(AHEAD):
                        act.nop().then_inc(tail["hi"], 1)
                    done_hi[0] = AHEAD
                    for k in range(KD):
                        act.wait_ge(S["gh_ple"], k + 1)
                        nc.scalar.activation(sq[:, k, :], h[:, k, :], ACT.Square).then_inc(S["sq_ple"], 1)
                root_of(bank[4], root, (S["ms"], 3), S["root"])
                done = L[l + 1]["sq_mix"] if l + 1 < DEPTH else S["y_fin_sq"]
                made = L[l + 1]["gh_mix"] if l + 1 < DEPTH else S["y_fin_h"]
                for k in range(KD):
                    if l:
                        high_upto(tail_quarters(k), tail)
                    else:
                        high_upto(dense_quarters(B["ple"] + k))
                    act.wait_ge(acc_evac, B["ple"] + k + 1)
                    nc.scalar.activation(sig[:, k % 2, :], up[:, k % 2, :], ACT.Sigmoid).then_inc(S["sig_ple"], 1)
                    if k:
                        act.wait_ge(made, k)
                        nc.scalar.activation(sq[:, k - 1, :], h[:, k - 1, :], ACT.Square).then_inc(done, 1)
                act.wait_ge(made, KD)
                nc.scalar.activation(sq[:, KD - 1, :], h[:, KD - 1, :], ACT.Square).then_inc(done, 1)
            root_of(bank[4], root, (F["ms_fin"], 1), F["root_fin"])

        def route_tokens(dve, link, S):
            v = nc.vector
            for k in range(KD):
                v.scalar_tensor_tensor(sq[:, k, :], h[:, k, :], col(1, "g_ffn", k), rstd[:, :], ALU.mult,
                                       ALU.mult).then_inc(F["normed"], 1)
            link(v.memset(logit, 0.0))
            for j in range(TT):
                for half in range(2):
                    i = 2 * j + half
                    dve.wait_ge(F["turned"], i + 1)
                    v.tensor_copy(ntok[0:TOKS[j], j, half * 512:(half + 1) * 512],
                                  bank[i % BANKS][0:TOKS[j], :]).then_inc(F["ntok"], 1)
            for q in range(AHEAD):
                dve.wait_ge(M[0]["hi"], q + 1)
                v.tensor_tensor(wlo[:, q, :], quarter_at(q), whi[:, q, :].bitcast(F32),
                                ALU.subtract).then_inc(M[0]["lo"], 1)
            dve.wait_ge(F["logits"], 1)
            for j in range(TT):
                i = v.tensor_copy(logit[0:TOKS[j], j, :], bank[5][0:TOKS[j], j * N_EXP:(j + 1) * N_EXP])
            link(i)
            shape = [P, TT, N_EXP, N_EXP]
            others = logit.unsqueeze(2).to_broadcast(shape)
            mine = logit.unsqueeze(3).to_broadcast(shape)
            for j in range(TT):
                v.tensor_tensor(beats[:, j], others[:, j], mine[:, j], ALU.is_gt)
                link(v.tensor_tensor(ties[:, j], others[:, j], mine[:, j], ALU.is_equal))
                link(v.tensor_tensor(ties[:, j], ties[:, j], lt8[:, :, :], ALU.mult))
            link(v.tensor_tensor(beats, beats, ties, ALU.add))
            link(v.tensor_reduce(rank, beats, AX_X, ALU.add))
            v.tensor_scalar(first, rank, 0.0, None, ALU.is_equal)
            link(v.tensor_scalar(second, rank, 1.0, None, ALU.is_equal))
            link(v.tensor_tensor(tmp8, logit, first, ALU.mult))
            link(v.tensor_reduce(top[:, 0, :], tmp8, AX_X, ALU.add))
            link(v.tensor_tensor(tmp8, logit, second, ALU.mult))
            link(v.tensor_reduce(top[:, 1, :], tmp8, AX_X, ALU.add))
            v.tensor_tensor(top[:, 2, :], top[:, 1, :], top[:, 0, :], ALU.subtract).then_inc(F["exp_in"], 1)
            for r in range(ROUNDS + 1):
                n = min(N_EXP, UNITS + 1 - r * N_EXP)
                i = v.tensor_tensor(member[:, :, r * N_EXP:r * N_EXP + n], first[:, :, 0:n], second[:, :, 0:n], ALU.add)
            i.then_inc(F["member"], 1)
            dve.wait_ge(F["exp_out"], 1)
            link(v.tensor_scalar(top[:, 4, :], top[:, 3, :], 1.0, None, ALU.add))
            link(v.reciprocal(top[:, 0, :], top[:, 4, :]))
            link(v.tensor_tensor(top[:, 1, :], top[:, 3, :], top[:, 0, :], ALU.mult))
            full = [P, TT, N_EXP]
            link(v.tensor_tensor(first, first, top[:, 0, :].unsqueeze(2).to_broadcast(full), ALU.mult))
            link(v.tensor_tensor(second, second, top[:, 1, :].unsqueeze(2).to_broadcast(full), ALU.mult))
            for r in range(ROUNDS + 1):
                n = min(N_EXP, UNITS + 1 - r * N_EXP)
                i = v.tensor_tensor(weight[:, :, r * N_EXP:r * N_EXP + n], first[:, :, 0:n], second[:, :, 0:n], ALU.add)
            link(i)
            dve.wait_ge(F["ranks"], 1)
            link(v.memset(place, 0.0))
            for r in range(ROUNDS + 1):
                n = min(N_EXP, UNITS + 1 - r * N_EXP)
                for j in range(TT):
                    v.tensor_scalar(place[0:TOKS[j], j, r * N_EXP:r * N_EXP + n],
                                    bank[6][0:TOKS[j], j * N_EXP:j * N_EXP + n], float(r * CAP), None, ALU.subtract)
            link(v.tensor_reduce(most[0:1, :], bank[6][0:1, TT * N_EXP:(TT + 1) * N_EXP], AX_X, ALU.max))
            v.tensor_scalar(flag[0:1, 0:1], most[0:1, :], float(CAP), None, ALU.is_gt).then_inc(flag_ready, 1)
            dve.wait_ge(flag_ready, 1)

        def expert_rows(dve, S, units, first_unit):
            v = nc.vector

            def one_hot(u):
                for j in range(TT):
                    n = TOKS[j]
                    v.tensor_scalar(onehot[0:n, j, :], iota[0:n, :], place[0:n, j, bass.ds(u, 1)],
                                    member[0:n, j, bass.ds(u, 1)], ALU.is_equal, ALU.mult)
                v.tensor_copy(weight_col, weight[:, :, bass.ds(u, 1)].rearrange("p j o -> p (j o)")).then_inc(
                    S["onehot"], 1)

            def add_sum(u, k):
                dve.wait_ge(S["sc_ready"], KD * u + (k + 1))
                v.tensor_tensor(h[:, k, :], h[:, k, :], bank[2 + k % 2][:, 0:T], ALU.add).then_inc(S["sc_free"], 1)

            def low(u, q):
                dve.wait_ge(S["hi"], UNIT_Q * u + (q + 1))
                v.tensor_tensor(wlo[:, q % SPLITS, :], quarter_at(q), whi[:, q % SPLITS, :].bitcast(F32),
                                ALU.subtract).then_inc(S["lo"], 1)

            for i in range(SPLITS):
                dve.nop().then_inc(S["used"], 1)
            for i in range(2):
                dve.nop().then_inc(S["sc_free"], 1)
            v.memset(slot_gate, 0.0).then_inc(S["down"], 1)
            v.memset(back.bitcast(F32), 0.0).then_inc(S["back"], 1)
            dve.nop().then_inc(S["down"], 1)
            one_hot(first_unit)

            def gathered_low(half):
                c = slice(half * 4, half * 4 + 4)
                v.tensor_tensor(xg_lo[:, c, :].rearrange("p c t -> p (c t)"), bank[half][:, :],
                                xg_hi[:, c, :].rearrange("p c t -> p (c t)").bitcast(F32),
                                ALU.subtract).then_inc(S["xg_lo"], 1)

            for half in range(2):
                dve.wait_ge(S["xg_hi"], half + 1)
                gathered_low(half)
            def result_low(u, half):
                dve.wait_ge(S["y_hi"], 2 * u + (half + 1))
                c = slice(half * 512, (half + 1) * 512)
                v.scalar_tensor_tensor(y_lo[:, c], bank[6 + half][:, :], slot_gate, y_hi[:, c].bitcast(F32),
                                       ALU.mult, ALU.subtract).then_inc(S["y_lo"], 1)

            with dve.Fori(0, units) as u:
                for q in range(UNIT_Q):
                    n, r = divmod(q, GROUP_Q)
                    if r == 0 and 1 <= n <= NG:
                        dve.wait_ge(S["up"], NG * u + n)
                        dve.wait_ge(S["silu"], NG * u + n)
                        v.tensor_tensor(htok[(n - 1) % 2], sg, bank[2 * ((n - 1) % 2) + 1][:, :],
                                        ALU.mult).then_inc(S["htok"], 1)
                    elif r == 2 and 1 <= n <= NG:
                        c = slice(4 * n - 4, 4 * n)
                        dve.wait_ge(S["hexp_hi"], NG * u + n)
                        v.tensor_tensor(hexp_lo[:, c, :].rearrange("p c t -> p (c t)"), bank[4 + (n - 1) % 2][:, :],
                                        hexp_hi[:, c, :].rearrange("p c t -> p (c t)").bitcast(F32),
                                        ALU.subtract).then_inc(S["hexp_lo"], 1)
                    low(u, q + AHEAD)
                    if SUMS_Q <= q < SUMS_Q + KD:
                        add_sum(u, q - SUMS_Q)
                    for half in range(2):
                        if q == XG_Q[half]:
                            dve.wait_ge(S["xg_hi"], 2 * u + (half + 3))
                            gathered_low(half)
                    if q < 2:
                        result_low(u, q)
                    elif q == TURN_Q + 2:
                        dve.wait_ge(S["back_turned"], u + 1)
                        dve.wait_ge(S["back"], u + 1)
                        dve.wait_ge(S["y_lo"], 2 * u + 2)
                        v.tensor_copy(slot_gate, bank[4][:, T:T + 1])
                        v.tensor_copy(next_back, bank[4][:, 0:T]).then_inc(S["next_back"], 1)
                    elif q == DOWN_Q0 + 1:
                        one_hot(u + (first_unit + 1))
            for half in range(2):
                result_low(units, half)
            for k in range(KD):
                add_sum(units, k)
            dve.wait_ge(S["sc_free"], KD * (units + 1) + 2)

        @block.vector
        def _(dve):
            steps = [0]

            def link(ins):
                steps[0] += 1
                ins.then_inc(dve_step, 1)
                dve.wait_ge(dve_step, steps[0])

            def tick(ins):
                steps[0] += 1
                ins.then_inc(dve_step, 1)
                return steps[0]

            done_lo = [0]

            def low_upto(n, S=dense):
                before = 0 if S is dense else (PRE_MOE + N_EXP * UNIT_SLOTS) * QUARTERS
                for q in range(done_lo[0], n):
                    dve.wait_ge(S["hi"], q + 1)
                    nc.vector.tensor_tensor(wlo[:, q % SPLITS, :], quarter_at(before + q),
                                            whi[:, q % SPLITS, :].bitcast(F32), ALU.subtract).then_inc(S["lo"], 1)
                done_lo[0] = max(done_lo[0], n)

            def gain(l, name, k, signal, hi=gh_hi, lo=gh_lo):
                link(nc.vector.tensor_scalar(hi[:, k, :], h[:, k, :], col(l, name, k), None, ALU.mult))
                nc.vector.scalar_tensor_tensor(lo[:, k, :], h[:, k, :], col(l, name, k), hi[:, k, :].bitcast(F32),
                                               ALU.mult, ALU.subtract).then_inc(signal, 1)

            def reciprocal_root(ready, dst=rstd):
                dve.wait_ge(*ready)
                link(nc.vector.reciprocal(dst[:, :], root[:, :]))

            def evacuate(chunk, dst, scale=rstd):
                if chunk < BASE[1]["ple"]:
                    low_upto(NEED[chunk])
                dve.wait_ge(acc_ready, chunk + 1)
                nc.vector.tensor_tensor(dst, bank[chunk % BANKS][:, 0:T], scale[:, :], ALU.mult).then_inc(acc_evac, 1)

            def add_to_h(chunk, k):
                low_upto(NEED[chunk])
                dve.wait_ge(acc_ready, chunk + 1)
                nc.vector.tensor_tensor(h[:, k, :], h[:, k, :], bank[chunk % BANKS][:, 0:T], ALU.add).then_inc(acc_evac, 1)
                dve.wait_ge(acc_evac, chunk + 1)

            dve.wait_ge(consts, len(ones) + 10)
            low_upto(AHEAD)
            dve.wait_ge(x_loaded, 16)
            dve.wait_ge(par_loaded[0], 16)
            for k in range(KD):
                gain(0, "g_mix", k, L[0]["gh_mix"], hid_hi, hid_lo)
            for l in range(DEPTH):
                S, B = L[l], BASE[l]
                dve.wait_ge(par_loaded[l], 16)
                dve.wait_ge(loaded[l], 48)
                if l:
                    dve.wait_ge(L[l - 1]["tails"], 1)
                nc.vector.tensor_copy(xa[:, :, :, 0:TAPS_A - 1], sta[:, :, :, :])
                link(nc.vector.tensor_copy(xc[:, :, :, 0:TAPS_C - 1], stc[:, :, :, :]))
                link(nc.vector.tensor_copy(p_hi[:, :, :], pe_in[:, :, :]))
                for k in range(KP):
                    nc.vector.tensor_tensor(p_lo[:, k, :], pe_in[:, k, :], p_hi[:, k, :].bitcast(F32),
                                            ALU.subtract).then_inc(S["p_lo"], 1)
                reciprocal_root((S["root"], 1))

                wc = cols(l, "w_conv_c").rearrange("p (c k) -> p c k", k=TAPS_C)
                for c in range(CC):
                    evacuate(B["zc"] + 2 * c, pp[:, 2 * c, :])
                    evacuate(B["zc"] + 2 * c + 1, pp[:, 2 * c + 1, :])
                    dve.wait_ge(S["sigmoid_zc"], c + 1)
                    dve.wait_ge(acc_evac, B["zc"] + 2 * c + 1)
                    nc.vector.tensor_tensor(cpad[:, c, TAPS_C - 1:], pp[:, 2 * c, 0:SEQ], sig[:, c % 2, 0:SEQ],
                                            ALU.mult).then_inc(S["glu"], 1)
                    nc.vector.tensor_tensor(xc[:, c, :, TAPS_C - 1], pp[:, 2 * c, SEQ:T], sig[:, c % 2, SEQ:T],
                                            ALU.mult).then_inc(S["glu"], 1)
                    low_upto(dense_quarters(B["zc"] + 2 * c + 1))
                dve.wait_ge(S["glu"], 2 * CC)

                def conv_c():
                    for k in range(TAPS_C):
                        for c in range(CC):
                            src, dst = cpad[:, c, k:k + SEQ], cv[:, c, 0:SEQ]
                            if k == 0:
                                last[c] = tick(nc.vector.tensor_scalar(dst, src, wc[:, c, 0:1], col(l, "b_conv_c", c),
                                                                       ALU.mult, ALU.add))
                            else:
                                dve.wait_ge(dve_step, last[c])
                                last[c] = tick(nc.vector.scalar_tensor_tensor(dst, src, wc[:, c, k:k + 1], dst,
                                                                              ALU.mult, ALU.add))
                            yield
                    for c in range(CC):
                        pv = prod[:, :].rearrange("p (b k) -> p b k", k=TAPS_C)
                        link(nc.vector.tensor_tensor(pv, xc[:, c], wc[:, c, :].unsqueeze(1).to_broadcast(
                            [P, NB, TAPS_C]), ALU.mult))
                        link(nc.vector.tensor_reduce(cv[:, c, SEQ:T], pv, AX_X, ALU.add))
                        link(nc.vector.tensor_scalar(cv[:, c, SEQ:T], cv[:, c, SEQ:T], col(l, "b_conv_c", c), None,
                                                     ALU.add))
                        yield
                    yield

                last = [0] * CC
                taps = conv_c()

                def some_taps(n):
                    for _ in range(n):
                        next(taps, None)

                for c in range(2 * CB):
                    evacuate(B["zab"] + c, ycat[:, c, :])
                    some_taps(4)
                    low_upto(dense_quarters(B["zab"] + c))
                    some_taps(4)
                dve.wait_ge(S["mean"], 1)
                dve.wait_ge(S["gelu"], CB)
                nc.vector.tensor_tensor(lnb[:, :, :], zb[:, 0:CB, :], bank[5][:, 0:T].unsqueeze(1).to_broadcast(
                    [P, CB, T]), ALU.subtract).then_inc(S["centred"], 1)

                wa = cols(l, "w_conv_a").rearrange("p (c k) -> p c k", k=TAPS_A)
                at = B["zab"] + 2 * CB
                dve.wait_ge(S["gelu"], 2 * CB)
                for c in range(CA):
                    evacuate(at + 2 * c, pp[:, 6, :])
                    some_taps(3)
                    low_upto(dense_quarters(at + 2 * c))
                    some_taps(3)
                    evacuate(at + 2 * c + 1, pp[:, 7, :])
                    dve.wait_ge(acc_evac, at + 2 * c + 2)
                    nc.vector.tensor_tensor(apad[:, c, TAPS_A - 1:], pp[:, 6, 0:SEQ], pp[:, 7, 0:SEQ], ALU.mult)
                    link(nc.vector.tensor_tensor(xa[:, c, :, TAPS_A - 1], pp[:, 6, SEQ:T], pp[:, 7, SEQ:T], ALU.mult))
                    some_taps(5)
                    if c:
                        low_upto(dense_quarters(at + 2 * c + 1))
                    if c == 0:
                        reciprocal_root((S["root_v"], 1), rstd2)
                        dve.wait_ge(S["centred"], 1)
                        nc.vector.tensor_tensor(lnb[:, :, :], lnb[:, :, :], rstd2[:, :].unsqueeze(1).to_broadcast(
                            [P, CB, T]), ALU.mult).then_inc(S["scaled"], 1)
                        low_upto(dense_quarters(at + 1))
                for c in range(CA):
                    evacuate(at + 2 * CA + c, ycat[:, c, :])
                    for k in range(TAPS_A):
                        src, dst = apad[:, c, k:k + SEQ], up[:, 0, 0:SEQ]
                        link(nc.vector.tensor_scalar(dst, src, wa[:, c, 0:1], None, ALU.mult) if k == 0 else
                             nc.vector.scalar_tensor_tensor(dst, src, wa[:, c, k:k + 1], dst, ALU.mult, ALU.add))
                    pv = prod[:, 0:NB * TAPS_A].rearrange("p (b k) -> p b k", k=TAPS_A)
                    link(nc.vector.tensor_tensor(pv, xa[:, c], wa[:, c, :].unsqueeze(1).to_broadcast([P, NB, TAPS_A]),
                                                 ALU.mult))
                    link(nc.vector.tensor_reduce(up[:, 0, SEQ:T], pv, AX_X, ALU.add))
                    dve.wait_ge(acc_evac, at + 2 * CA + c + 1)
                    i = nc.vector.tensor_tensor(ycat[:, c, :], ycat[:, c, :], up[:, 0, :], ALU.mult)
                    if c == CA - 1:
                        i.then_inc(S["y_a"], 1)
                    else:
                        link(i)
                    low_upto(dense_quarters(at + 2 * CA + c))
                    some_taps(5)
                some_taps(TAPS_C * CC + CC + 1)
                nc.vector.tensor_copy(prod[:, 0:1], cv[:, 0, 0:1]).then_inc(S["taps"], 1)

                dve.wait_ge(S["mean"], 2)
                nc.vector.tensor_tensor(cv[:, :, :], cv[:, :, :], bank[4][:, 0:T].unsqueeze(1).to_broadcast([P, CC, T]),
                                        ALU.subtract).then_inc(S["centred"], 1)
                dve.wait_ge(S["vt"], 1)
                nc.vector.tensor_copy(vtok[:, :, :], bank[5][:, :].rearrange("p (j d) -> p j d", j=CHUNKS)).then_inc(
                    S["vtok"], 1)
                for k in range(4):
                    low_upto(NEED[B["pp"] + k])
                    dve.wait_ge(acc_ready, B["pp"] + k + 1)
                    nc.vector.tensor_copy(pp[:, k, :], bank[(B["pp"] + k) % BANKS][:, 0:T]).then_inc(acc_evac, 1)
                reciprocal_root((S["root_v"], 2))
                dve.wait_ge(S["centred"], 2)
                nc.vector.tensor_tensor(cv[:, :, :], cv[:, :, :], rstd[:, :].unsqueeze(1).to_broadcast([P, CC, T]),
                                        ALU.mult).then_inc(S["scaled"], 1)
                dve.wait_ge(S["mixed"], 1)
                dve.wait_ge(S["ln_b"], CB)
                bs = cols(l, "b_s").rearrange("p (c t) -> p c t", t=P)
                for t in range(CHUNKS):
                    for j in range(2):
                        rows = slice(HEAD * j, HEAD * (j + 1))
                        src = bank[6 + t][rows, :].rearrange("p (c j t) -> p j c t", j=2, t=P)[:, j]
                        nc.vector.tensor_tensor(ycat[rows, CA:CA + CB, t * P:(t + 1) * P], src, bs[rows], ALU.add)
                for c in range(CB):
                    i = nc.vector.tensor_scalar(ycat[:, CA + c, SEQ:T], lnb[:, c, SEQ:T], col(l, "w00", c),
                                                bs[:, c, 0:1], ALU.mult, ALU.add)
                link(i)
                dve.wait_ge(S["gelu"], 2 * CB)
                nc.vector.tensor_tensor(ycat[:, CA:CA + CB, :], ycat[:, CA:CA + CB, :], zb[:, CB:2 * CB, :],
                                        ALU.mult).then_inc(S["y_b"], 1)
                low_upto(dense_quarters(B["pp"] + KD - 1))
                for k in range(4, KD):
                    dve.wait_ge(acc_ready, B["pp"] + k + 1)
                    nc.vector.tensor_copy(pp[:, k, :], bank[(B["pp"] + k) % BANKS][:, 0:T]).then_inc(acc_evac, 1)

                dve.wait_ge(S["y_b"], 1)
                dve.wait_ge(S["y_c"], CC)
                at = 0
                for g, n in enumerate((CA, CB, CC)):
                    reciprocal_root((S["y_root"], g + 1))
                    for c in range(at, at + n):
                        nc.vector.scalar_tensor_tensor(ycat[:, c, :], ycat[:, c, :], col(l, "g_out", c), rstd[:, :],
                                                       ALU.mult, ALU.mult).then_inc(S["y_normed"], 1)
                    for c in range(at, at + n):
                        dve.wait_ge(S["yn_hi"], c + 1)
                        nc.vector.tensor_tensor(hid_lo[:, c, :], ycat[:, c, :], hid_hi[:, c, :].bitcast(F32),
                                                ALU.subtract).then_inc(S["yn"], 1)
                    at += n
                for k in range(KD):
                    add_to_h(B["wo"] + k, k)
                    if l == 0:
                        gain(l, "g_ffn", k, S["gh_ffn"])
                    low_upto(dense_quarters(B["wo"] + k))
                reciprocal_root((S["root"], 2))

                if l == 0:
                    def hidden_low(n):
                        dve.wait_ge(S["hid_hi"], n + 1)
                        f = n % KH
                        nc.vector.tensor_tensor(hid_lo[:, f, :], zb[:, 2 + n % 2, :], hid_hi[:, f, :].bitcast(F32),
                                                ALU.subtract).then_inc(S["hid2" if n >= KH else "hid"], 1)

                    for half, (ff, down) in enumerate((("ff", "down"), ("ff2", "down2"))):
                        for f in range(KH):
                            n = half * KH + f
                            if n >= 2:
                                dve.wait_ge(S["silu"], n - 1)
                            evacuate(B[ff] + 2 * f, up[:, n % 2, :])
                            if f:
                                hidden_low(n - 1)
                            low_upto(dense_quarters(B[ff] + 2 * f))
                            evacuate(B[ff] + 2 * f + 1, zb[:, n % 2, :])
                            dve.wait_ge(acc_evac, B[ff] + 2 * f + 2)
                            dve.wait_ge(S["silu"], n + 1)
                            nc.vector.tensor_tensor(zb[:, 2 + n % 2, :], zb[:, n % 2, :], sig[:, n % 2, :],
                                                    ALU.mult).then_inc(S["hid_f32"], 1)
                            if f < KH - 1:
                                low_upto(dense_quarters(B[ff] + 2 * f + 1))
                        hidden_low(half * KH + KH - 1)
                        low_upto(dense_quarters(B[ff] + KF - 1))
                        for k in range(KD):
                            add_to_h(B[down] + k, k)
                            if half:
                                gain(l, "g_ple", k, S["gh_ple"])
                            low_upto(dense_quarters(B[down] + k))
                else:
                    route_tokens(dve, link, S)
                    expert_rows(dve, M[0], N_EXP, 0)
                    dve.wait_ge(M[0]["lo"], N_EXP * UNIT_Q + AHEAD)
                    dve.wait_ge(flag_ready, 1)
                    some = dve.value_load(flag[0:1, 0:1], min_val=0, max_val=1)
                    with dve.If(some > 0):
                        for _ in range(AHEAD):
                            dve.nop().then_inc(M[1]["lo"], 1)
                        expert_rows(dve, M[1], UNITS - N_EXP, N_EXP)
                        dve.wait_ge(M[1]["lo"], (UNITS - N_EXP) * UNIT_Q + AHEAD)
                    for _ in range(AHEAD):
                        dve.nop().then_inc(tail["lo"], 1)
                    done_lo[0] = AHEAD
                    for k in range(KD):
                        gain(l, "g_ple", k, S["gh_ple"])

                reciprocal_root((S["root"], 3))
                for k in range(KD):
                    if k >= 2:
                        dve.wait_ge(S["sig_ple"], k - 1)
                    if l:
                        low_upto(k + 1, tail)
                    evacuate(B["ple"] + k, up[:, k % 2, :])
                    dve.wait_ge(S["sig_ple"], k + 1)
                    link(nc.vector.tensor_tensor(pp[:, k, :], pp[:, k, :], sig[:, k % 2, :], ALU.mult))
                    if l + 1 < DEPTH:
                        link(nc.vector.tensor_tensor(h[:, k, :], h[:, k, :], pp[:, k, :], ALU.add))
                        gain(l + 1, "g_mix", k, L[l + 1]["gh_mix"], hid_hi, hid_lo)
                        low_upto(dense_quarters(B["ple"] + k))
                    else:
                        nc.vector.tensor_tensor(h[:, k, :], h[:, k, :], pp[:, k, :], ALU.add).then_inc(S["y_fin_h"], 1)
                        low_upto(tail_quarters(k), tail)
            reciprocal_root((F["root_fin"], 1))
            dve.wait_ge(L[DEPTH - 1]["y_fin_h"], KD)
            for k in range(KD):
                nc.vector.scalar_tensor_tensor(ycat[:, k, :], h[:, k, :], col(0, "g_final", k), rstd[:, :], ALU.mult,
                                               ALU.mult).then_inc(F["y_fin"], 1)

def _blocks(w, order=None):
    import numpy as np
    k, n = w.shape
    b = w.reshape(k // P, P, n // P, P).transpose(2, 0, 1, 3)
    if order is not None:
        b = b[np.asarray(order)]
    return b.reshape(-1, P, P)


def _features(a):
    import numpy as np
    lead = a.shape[:-1]
    b = a.reshape(*lead, a.shape[-1] // P, P)
    return np.moveaxis(np.moveaxis(b, -1, 0), -1, 1)


def kernel(**inputs):
    import numpy as np
    import concourse.bacc as _bacc
    from concourse.bass_utils import run_bass_kernel_spmd as _run

    a = {k: np.asarray(v) for k, v in inputs.items()}
    ca = list(range(CA))
    o_gc, o_xa, o_b, o_c = CA, 2 * CA, 3 * CA, 3 * CA + 2 * CB
    in_order = [o_c + CC * j + c for c in range(CC) for j in range(2)]
    in_order += [o_b + CB + c for c in range(CB)] + [o_b + c for c in range(CB)]
    in_order += [o for c in ca for o in (o_gc + c, o_xa + c)] + ca

    def moving(w, n_group):
        k, n = w.shape
        return w.reshape(k // P, P, n // n_group, n_group // P, P).transpose(2, 0, 3, 1, 4).reshape(
            n // n_group, -1, P, P)

    def gate_up(g, u):
        b = np.stack([_blocks(g).reshape(-1, KD, P, P), _blocks(u).reshape(-1, KD, P, P)], axis=1)
        return b.reshape(-1, P, P)

    parts = []
    for l in range(DEPTH):
        parts += [_blocks(a["w_in"][l], in_order), _blocks(a["w_ple_proj"][l]), _blocks(a["w_o"][l])]
        if l == 0:
            n = D_FF // 2
            for c in (slice(0, n), slice(n, D_FF)):
                parts += [gate_up(a["w_ff_gate"][0][:, c], a["w_ff_up"][0][:, c]), _blocks(a["w_ff_down"][0][c])]
        else:
            for e in range(N_EXP):
                parts += [np.stack([moving(a["w_ex_gate"][0, e], 512), moving(a["w_ex_up"][0, e], 512)],
                                   axis=1).reshape(-1, P, P), moving(a["w_ex_down"][0, e], D_MODEL)[0]]
        parts.append(_blocks(a["w_ple_gate"][l]))
    blocks = np.concatenate(parts)
    assert len(blocks) == SLOTS * WBLOCKS
    wstream = np.ascontiguousarray(blocks.reshape(SLOTS, WBLOCKS, P, P).transpose(0, 2, 1, 3)).reshape(
        SLOTS, P, WBLOCKS * P)

    def tokens(prompt, sample):
        return _features(np.concatenate([prompt.reshape(SEQ, -1), sample.reshape(NB, -1)]))

    x = np.ascontiguousarray(tokens(a["x_prompt"], a["x_sample"]))
    p = np.stack([tokens(a["p_prompt"][l], a["p_sample"][l]) for l in range(DEPTH)])
    par = np.zeros((DEPTH, P, NPAR), x.dtype)
    state = []
    heads = np.arange(D_B) // HEAD
    for l in range(DEPTH):
        put = {n: a[n][l] for n in ("g_mix", "g_ln_b", "b_ln_b", "b_conv_c", "g_ln_c", "b_ln_c", "g_out", "g_ffn",
                                    "g_ple", "w_conv_a", "w_conv_c")}
        put["g_final"] = a["g_final"]
        put["b_s"] = a["b_s"][l].T[:, heads]
        put["w00"] = a["w_s"][l][:, 0, 0][heads]
        for n, v in put.items():
            o, size = PAR[n]
            par[l, :, o:o + size] = _features(v).reshape(P, size)
        o, size = PAR["w_sT"]
        par[l, :, o:o + size] = a["w_s"][l].transpose(2, 0, 1).reshape(P, size)
        o, size = PAR["w_router"]
        par[l, :, o:o + size] = a["w_router"][0].reshape(KD, P, N_EXP).transpose(1, 0, 2).reshape(P, size)
        state.append(np.concatenate([_features(a["state_conv_a"][l]).reshape(P, -1),
                                     _features(a["state_conv_c"][l]).reshape(P, -1)], axis=1))
    arrays = {"wstream": wstream, "x_in": x, "p_in": np.ascontiguousarray(p), "par_in": par,
              "state_in": np.ascontiguousarray(np.stack(state))}
    outs = {"y_out": (P, KD, T), "a_prompt": (DEPTH, P, CA, TAPS_A - 1), "a_sample": (DEPTH, P, CA, NB, TAPS_A),
            "c_prompt": (DEPTH, P, CC, TAPS_C - 1), "c_sample": (DEPTH, P, CC, NB, TAPS_C),
            "v_sample": (DEPTH, P, CB, NB)}
    nc = _bacc.Bacc("TRN2", target_bir_lowering=False, num_devices=1)
    aps = [nc.dram_tensor(n, v.shape, F32, kind="ExternalInput").ap() for n, v in arrays.items()]
    aps += [nc.dram_tensor(n, s, F32, kind="ExternalOutput").ap() for n, s in outs.items()]
    build(nc, *aps)
    r = _run(nc, [arrays], core_ids=[0]).results[0]

    def rows(v, lead):
        v = np.moveaxis(np.moveaxis(v, 1, -1), 0, -1)
        return np.ascontiguousarray(v.reshape(*lead, -1))

    y = rows(np.asarray(r["y_out"]), (T,))
    ap, as_, cp, cs, vs = (np.asarray(r[n]) for n in ("a_prompt", "a_sample", "c_prompt", "c_sample", "v_sample"))
    return (y[0:SEQ].reshape(1, SEQ, D_MODEL), y[SEQ:].reshape(NB, 1, D_MODEL),
            np.stack([rows(v, (1, TAPS_A - 1)) for v in ap]), np.stack([rows(v[:, :, :, 1:], (NB, TAPS_A - 1)) for v in as_]),
            np.stack([rows(v, (1, TAPS_C - 1)) for v in cp]), np.stack([rows(v[:, :, :, 1:], (NB, TAPS_C - 1)) for v in cs]),
            np.stack([rows(v, (NB, 1)) for v in vs]))
```

```python
from contextlib import ExitStack

import concourse.bass as bass
from concourse import mybir

F32 = mybir.dt.float32
F32R = mybir.dt.float32r
I32 = mybir.dt.int32
ALU = mybir.AluOpType
ACT = mybir.ActivationFunctionType
AX_X = mybir.AxisListType.X

P = 128
D_MODEL, SEQ, DEPTH, NB = 1024, 256, 2, 8
HEAD = 64
D_A, D_B = 3 * D_MODEL // 8, D_MODEL // 4
D_C = D_MODEL - D_A - D_B
TAPS_A, TAPS_C = 3, 31
D_PLE, D_FF, N_EXP, D_EXP = 256, 11 * D_MODEL // 4, 8, 2 * D_MODEL
EPS = 1e-6
T = SEQ + NB
KD = D_MODEL // P
CA, CB, CC = D_A // P, D_B // P, D_C // P
NHEAD = D_B // HEAD
CHUNKS = SEQ // P
KF, KE, KP = D_FF // P, D_EXP // P, D_PLE // P
TT = CHUNKS + 1
TOKS = [P] * CHUNKS + [NB]

CAP = 128
ROUNDS = -(-T // CAP)
UNITS = ROUNDS * N_EXP

WBLOCKS = 32
RING = 3
PRE_MOE = (2 * (KD * (3 * CA + 2 * CB + 2 * CC) + KP * KD + KD * KD) + 3 * KF * KD + KD * KD) // WBLOCKS
UNIT_SLOTS = 3 * KE * KD // WBLOCKS
TAIL_SLOTS = KD * KD // WBLOCKS
SLOTS = PRE_MOE + N_EXP * UNIT_SLOTS + TAIL_SLOTS
QBLOCKS = 8
QUARTERS = WBLOCKS // QBLOCKS
SPLITS = 4
AHEAD = SPLITS - 1
UNIT_Q = UNIT_SLOTS * QUARTERS
NG = D_EXP // 512
GROUP_Q = 2 * KD * 4 // QBLOCKS
DOWN_Q0 = NG * GROUP_Q
KH = KF // 2
TURN_Q = 1
ONEHOT_Q = 5
GATHER_Q = (14, 20, 22, 28, DOWN_Q0 + 2, DOWN_Q0 + 3, DOWN_Q0 + 4, DOWN_Q0 + 5)
SUMS_Q = DOWN_Q0 + 7
XG_Q = (DOWN_Q0 + 3, GATHER_Q[-1] + 3)
XG_BANK = (5, 1)
assert UNIT_SLOTS % RING == 0 and PRE_MOE % RING == 0 and UNIT_Q % SPLITS == 0 and KF % 2 == 0 and SUMS_Q + KD < UNIT_Q

PAR = {}
_at = 0
for _name, _n in (("g_mix", KD), ("g_ln_b", CB), ("b_ln_b", CB), ("b_conv_c", CC), ("g_ln_c", CC),
                  ("b_ln_c", CC), ("g_out", KD), ("g_ffn", KD), ("g_ple", KD), ("g_final", KD),
                  ("w_conv_a", CA * TAPS_A), ("w_conv_c", CC * TAPS_C), ("b_s", CB * P), ("w00", CB),
                  ("w_sT", NHEAD * P), ("w_router", KD * N_EXP)):
    PAR[_name] = (_at, _n)
    _at += _n
NPAR = _at
NST_A, NST_C = CA * NB * (TAPS_A - 1), CC * NB * (TAPS_C - 1)

N_ZC, N_ZAB = 2 * CC, 3 * CA + 2 * CB
BASE = []
_at = 0
for _l in range(DEPTH):
    _b = {}
    for _name, _n in (("zc", N_ZC), ("zab", N_ZAB), ("pp", KD), ("wo", KD),
                      ("ff", KF if _l == 0 else 0), ("down", KD if _l == 0 else 0),
                      ("ff2", KF if _l == 0 else 0), ("down2", KD if _l == 0 else 0), ("ple", KD)):
        _b[_name] = _at
        _at += _n
    BASE.append(_b)
BANKS = 4
DIAGS = 12
TAPS_PE = -(-TAPS_C // (N_ZAB - 1))
_k = {"zc": KD, "zab": KD, "pp": KP, "wo": KD, "ff": KD, "down": KH, "ff2": KD, "down2": KH, "ple": KD}
NEED = []
_t = 0
for _b in BASE:
    _ends = sorted((v, n) for n, v in _b.items())
    for _i, (_v, _n) in enumerate(_ends):
        _stop = _ends[_i + 1][0] if _i + 1 < len(_ends) else _v + KD
        for _c in range(_v, _stop):
            _t += _k[_n]
            NEED.append(-(-_t // QBLOCKS))
DENSE_Q = PRE_MOE * QUARTERS


def dense_quarters(chunk):
    return min(NEED[chunk] + AHEAD, DENSE_Q)


def tail_quarters(k):
    return min(k + 1 + AHEAD, TAIL_SLOTS * QUARTERS)



def build(nc, wstream, x_in, p_in, par_in, state_in, y_out, a_prompt, a_sample, c_prompt, c_sample, v_sample):
    with ExitStack() as ctx:
        def sb(name, shape, dt=F32):
            return ctx.enter_context(nc.sbuf_tensor(name, shape, dt))

        def sem(name):
            return ctx.enter_context(nc.semaphore(name))

        ring = sb("ring", [P, RING, WBLOCKS * P])
        whi = sb("whi", [P, SPLITS, QBLOCKS * P], F32R)
        wlo = sb("wlo", [P, SPLITS, QBLOCKS * P], F32R)
        gh_hi, gh_lo = (sb(f"gh_{x}", [P, KD, T], F32R) for x in ("hi", "lo"))
        hid_hi, hid_lo = (sb(f"hid_{x}", [P, KH, T], F32R) for x in ("hi", "lo"))
        p_hi, p_lo = (sb(f"p_{x}", [P, KP, T], F32R) for x in ("hi", "lo"))
        xg_hi, xg_lo = (g[:, :, :].rearrange("p c t -> p (c t)")[:, 0:KD * CAP].rearrange("p (c t) -> p c t", t=CAP)
                        for g in (gh_hi, gh_lo))
        hexp_hi, hexp_lo = (g[:, :, :].rearrange("p c t -> p (c t)")[:, 0:KE * CAP].rearrange(
            "p (c t) -> p c t", t=CAP) for g in (hid_hi, hid_lo))
        h = sb("h", [P, KD, T])
        sq = sb("sq", [P, KD, T])
        pp = sb("pp", [P, KD, T])
        work = sb("work", [P, (KD + 2 * CB) * T])
        par = sb("par", [P, DEPTH, NPAR])
        pe_in = sb("pe_in", [P, KP, T])
        sta = sb("sta", [P, CA, NB, TAPS_A - 1])
        stc = sb("stc", [P, CC, NB, TAPS_C - 1])
        xa = sb("xa", [P, CA, NB, TAPS_A])
        xc = sb("xc", [P, CC, NB, TAPS_C])
        apad = sb("apad", [P, CA, TAPS_A - 1 + SEQ])
        cpad = sb("cpad", [P, CC, TAPS_C - 1 + SEQ])
        prod = sb("prod", [P, NB * TAPS_A])
        root = sb("root", [P, T])
        rstd = sb("rstd", [P, T])
        rstd2 = sb("rstd2", [P, T])
        vtok = sb("vtok", [P, CHUNKS, D_B])
        sig = sb("sig", [P, 2, T])
        up = sb("up", [P, 2, T])
        ones = {d: sb(f"ones_{d}", [P, P]) for d in (D_MODEL, D_A, D_B, 1)}
        before = sb("before", [P, P])
        ident = sb("ident", [P, P])
        eps = sb("eps", [P, 1])
        iota = sb("iota", [P, CAP])
        lt8 = sb("lt8", [P, N_EXP, N_EXP])
        cv = sb("cv", [P, CC, T])
        lnb = sb("lnb", [P, CB, T])
        small = sb("small", [P, 1024])

        ycat = work[:, 0:KD * T].rearrange("p (c t) -> p c t", t=T)
        zb = work[:, KD * T:(KD + 2 * CB) * T].rearrange("p (c t) -> p c t", t=T)
        ntok = work[:, 0:TT * D_MODEL].rearrange("p (j d) -> p j d", d=D_MODEL)
        sq_row = sq[:, :, :].rearrange("p c t -> p (c t)")
        onehot = sq_row[:, D_MODEL:D_MODEL + TT * CAP].rearrange("p (j t) -> p j t", t=CAP)
        y_hi, y_lo = (g[:, :, :].rearrange("p c t -> p (c t)")[:, KD * CAP:KD * CAP + D_MODEL]
                      for g in (gh_hi, gh_lo))
        back, next_back = (hid_hi[:, :, :].rearrange("p c t -> p (c t)")[:, KE * CAP + i * T:KE * CAP + (i + 1) * T]
                           for i in range(2))
        diag = sq_row[:, 2 * T:2 * T + DIAGS * P].rearrange("p (i q) -> p i q", q=P)
        assert 2 * T + DIAGS * P <= KD * T
        sg = sig[:, :, :].rearrange("p b t -> p (b t)")[:, 0:512]
        htok = [up[:, :, :].rearrange("p b t -> p (b t)")[:, 0:512], vtok[:, :, :].rearrange("p b t -> p (b t)")]
        _s = [0]

        def cut(*shape):
            n = 1
            for k in shape:
                n *= k
            v = small[:, _s[0]:_s[0] + n]
            _s[0] += n
            return v if len(shape) == 1 else v.rearrange(
                "p (a b) -> p a b", b=shape[1]) if len(shape) == 2 else v.rearrange(
                "p (a b c) -> p a b c", b=shape[1], c=shape[2])

        logit = cut(TT, N_EXP)
        beats = cut(TT, N_EXP, N_EXP)
        ties = cut(TT, N_EXP, N_EXP)
        rank = cut(TT, N_EXP)
        first = cut(TT, N_EXP)
        second = cut(TT, N_EXP)
        tmp8 = cut(TT, N_EXP)
        gate = cut(TT, N_EXP)
        top = cut(5, TT)
        place = cut(TT, UNITS + 1)
        member = cut(TT, UNITS + 1)
        weight = cut(TT, UNITS + 1)
        most = cut(1)
        weight_col = cut(TT)
        slot_gate = cut(1)
        flag = sb("flag", [1, 1], I32)
        assert _s[0] <= 1024

        bank = [ctx.enter_context(nc.psum_tensor(f"bank{i}", [P, 512], F32)) for i in range(8)]

        def col(l, name, i=0):
            o = PAR[name][0] + i
            return par[:, l, o:o + 1]

        def cols(l, name):
            o, n = PAR[name]
            return par[:, l, o:o + n]

        consts = sem("consts_ready")
        loaded = [sem(f"layer_inputs_loaded_{l}") for l in range(DEPTH)]
        par_loaded = [sem(f"parameters_loaded_{l}") for l in range(DEPTH)]
        x_loaded = sem("x_loaded")
        landed = [sem(f"slot_landed_{i}") for i in range(RING)]
        over_landed = [sem(f"overflow_slot_landed_{i}") for i in range(RING)]
        dense = {n: sem(f"{n}_dense") for n in ("hi", "lo", "used")}
        tail = {n: sem(f"{n}_tail") for n in ("hi", "lo", "used")}
        acc_ready = sem("acc_ready")
        acc_evac = sem("acc_evacuated")
        dve_step = sem("dve_step")
        stored = sem("stored")
        flag_ready = sem("flag_ready")

        diag_ready = sem("diag_ready")
        diag_used = sem("diag_used")
        conv_0 = sem("first_chunk_convolved")

        L = [{n: sem(f"{n}_{l}") for n in (
            "gh_mix", "sq_mix", "ms", "root", "sigmoid_zc", "glu", "gelu", "taps",
            "mean", "centred", "squared", "variance", "root_v", "scaled", "ln_b", "vt", "vtok", "mixed",
            "y_c", "y_a", "y_b", "ys_sq", "y_ms", "y_root", "y_normed", "yn_hi", "yn", "sq_ffn",
            "gh_ple", "sq_ple", "sig_ple", "tails", "w_sT", "p_lo")} for l in range(DEPTH)]
        L[0].update({n: sem(n) for n in ("gh_ffn", "silu", "hid_f32", "hid_hi", "hid", "hid2")})
        L[1].update({n: sem(n) for n in ("y_fin_sq", "y_fin_h")})
        F = {n: sem(n) for n in ("ms_fin", "root_fin", "y_fin", "normed", "turned", "ntok", "logits",
                                 "exp_in", "exp_out", "member", "ranks")}
        M = [{n: sem(f"{n}_{k}") for n in (
            "hi", "lo", "used", "onehot", "gathered", "xg_hi", "xg_lo", "gate", "up", "silu", "htok",
            "turned", "hexp_hi", "hexp_lo", "back_turned", "next_back", "back", "down",
            "y_hi", "y_lo", "sc_ready", "sc_free")} for k in ("moe", "over")]

        block = ctx.enter_context(nc.Block())

        @block.sync
        def _(sp):
            sp.dma_start(h[:, :, :], x_in).then_inc(x_loaded, 16)

            def layer_inputs(l):
                sp.dma_start(sta[:, :, :, :], state_in[l, :, 0:NST_A].rearrange(
                    "p (c b k) -> p c b k", c=CA, b=NB)).then_inc(loaded[l], 16)
                sp.dma_start(stc[:, :, :, :], state_in[l, :, NST_A:NST_A + NST_C].rearrange(
                    "p (c b k) -> p c b k", c=CC, b=NB)).then_inc(loaded[l], 16)
                sp.dma_start(pe_in[:, :, :], p_in[l]).then_inc(loaded[l], 16)

            def load(slot, pos, landed=landed):
                sp.dma_start(ring[:, pos], wstream[bass.ds(slot, 1)].rearrange("s p n -> p (s n)")
                             if not isinstance(slot, int) else wstream[slot]).then_inc(
                                 landed[pos] if isinstance(landed, list) else landed, 16)

            sp.dma_start(par[:, 0, :], par_in[0]).then_inc(par_loaded[0], 16)
            load(0, 0)
            layer_inputs(0)
            for s in range(1, RING):
                load(s, s)
            def dense_slots(first, end):
                with sp.Fori(first, end) as n:
                    for pos in range(RING):
                        sp.wait_ge(dense["lo"], n * (RING * QUARTERS) + QUARTERS * (pos + 1 - RING))
                        load(n * RING + pos, pos)

            middle = PRE_MOE // RING // 2
            dense_slots(1, middle)
            sp.wait_ge(L[0]["p_lo"], KP)
            sp.wait_ge(L[0]["glu"], 2 * CC)
            sp.dma_start(par[:, 1, :], par_in[1]).then_inc(par_loaded[1], 16)
            layer_inputs(1)
            dense_slots(middle, PRE_MOE // RING)

            def unit_slots(landed, lo, e, base, js):
                for j in js:
                    sp.wait_ge(lo, base * QUARTERS + QUARTERS * (j + 1 - RING))
                    load(e * UNIT_SLOTS + (PRE_MOE + j), j % RING, landed)

            def tail_slots(lo, slots_before, first_landed):
                for j in range(TAIL_SLOTS):
                    sp.wait_ge(lo, QUARTERS * (slots_before + j + 1 - RING))
                    load(SLOTS - TAIL_SLOTS + j, j, landed if j else first_landed)

            for j in range(RING):
                sp.wait_ge(dense["lo"], QUARTERS * (PRE_MOE + j + 1 - RING))
                load(PRE_MOE + j, j)
            with sp.Fori(0, N_EXP - 1) as u:
                unit_slots(landed, M[0]["lo"], u, u * UNIT_SLOTS, range(RING, UNIT_SLOTS + RING))
            unit_slots(landed, M[0]["lo"], N_EXP - 1, (N_EXP - 1) * UNIT_SLOTS, range(RING, UNIT_SLOTS))
            sp.wait_ge(flag_ready, 1)
            some = sp.value_load(flag[0:1, 0:1], min_val=0, max_val=1)
            with sp.If(some > 0):
                over = M[1]["lo"]
                for r in range(ROUNDS - 1):
                    for j in range(RING):
                        if r:
                            sp.wait_ge(over, QUARTERS * (r * N_EXP * UNIT_SLOTS + j + 1 - RING))
                        else:
                            sp.wait_ge(M[0]["lo"], QUARTERS * (N_EXP * UNIT_SLOTS + j + 1 - RING))
                        load(PRE_MOE + j, j, over_landed if r or j else landed)
                    with sp.Fori(0, N_EXP - 1) as u:
                        unit_slots(over_landed, over, u, u * UNIT_SLOTS + r * N_EXP * UNIT_SLOTS,
                                   range(RING, UNIT_SLOTS + RING))
                    unit_slots(over_landed, over, N_EXP - 1, ((r + 1) * N_EXP - 1) * UNIT_SLOTS,
                               range(RING, UNIT_SLOTS))
                tail_slots(over, (ROUNDS - 1) * N_EXP * UNIT_SLOTS, over_landed[0])
            with sp.If(some < 1):
                tail_slots(M[0]["lo"], N_EXP * UNIT_SLOTS, landed[0])

        @block.gpsimd
        def _(pool):
            for d, t in ones.items():
                pool.memset(t[:, :], 1.0 / d).then_inc(consts, 1)
            pool.memset(eps[:, :], EPS).then_inc(consts, 1)
            pool.memset(ident[:, :], 0.0).then_inc(consts, 1)
            pool.memset(before[:, :], 1.0).then_inc(consts, 1)
            pool.memset(lt8[:, :, :], 1.0).then_inc(consts, 1)
            pool.memset(apad[:, :, 0:TAPS_A - 1], 0.0).then_inc(consts, 1)
            pool.memset(cpad[:, :, 0:TAPS_C - 1], 0.0).then_inc(consts, 1)
            pool.iota(iota[:, :], [[1, CAP]], base=0, channel_multiplier=0,
                      allow_small_or_imprecise_dtypes=True).then_inc(consts, 1)
            n = len(ones) + 7
            pool.wait_ge(consts, n)
            pool.affine_select(out=ident[:, :], in_=ident[:, :], compare_op=ALU.not_equal, fill=1.0,
                               base=0, pattern=[[-1, P]], channel_multiplier=1).then_inc(consts, 1)
            pool.affine_select(out=before[:, :], in_=before[:, :], compare_op=ALU.is_gt, fill=0.0,
                               base=0, pattern=[[1, P]], channel_multiplier=-1).then_inc(consts, 1)
            pool.affine_select(out=lt8[:, :, :], in_=lt8[:, :, :], compare_op=ALU.is_gt, fill=0.0,
                               base=0, pattern=[[1, N_EXP], [-1, N_EXP]], channel_multiplier=0).then_inc(consts, 1)
            for l in range(DEPTH):
                S = L[l]
                pool.wait_ge(par_loaded[l], 16)
                v = cols(l, "w_sT").rearrange("p (h t) -> p h t", t=P)
                pool.affine_select(out=v, in_=v, compare_op=ALU.is_ge, fill=0.0, base=0,
                                   pattern=[[0, NHEAD], [1, P]], channel_multiplier=-1).then_inc(S["w_sT"], 1)
                pool.wait_ge(S["ms"], 1)
                for k in range(TAPS_C):
                    if l or k >= DIAGS:
                        pool.wait_ge(diag_used, l * TAPS_C + max(k - DIAGS + 1, 0))
                    pool.tensor_scalar(diag[:, k % DIAGS, :], ident[:, :], col(l, "w_conv_c", k), None,
                                       ALU.mult).then_inc(diag_ready, 1)
                pool.wait_ge(S["glu"], 2 * CC)
                pool.dma_start(c_prompt[l], cpad[:, :, SEQ:SEQ + TAPS_C - 1]).then_inc(stored, 16)
                pool.dma_start(c_sample[l], xc[:, :, :, :]).then_inc(stored, 16)
                pool.wait_ge(S["ln_b"], CB)
                pool.dma_start(v_sample[l], lnb[:, :, SEQ:T]).then_inc(stored, 16)
                pool.wait_ge(S["y_a"], 1)
                pool.dma_start(a_prompt[l], apad[:, :, SEQ:SEQ + TAPS_A - 1]).then_inc(stored, 16)
                pool.dma_start(a_sample[l], xa[:, :, :, :]).then_inc(stored, 16)
                pool.wait_ge(stored, 80 * (l + 1))
                pool.nop().then_inc(S["tails"], 1)
            for c in range(0, KD, 4):
                pool.wait_ge(F["y_fin"], c + 4)
                pool.dma_start(y_out[:, c:c + 4, :], ycat[:, c:c + 4, :]).then_inc(stored, 16)
            pool.wait_ge(stored, 16 * (5 * DEPTH + 2))

        def route(pe):
            pe.wait_ge(F["normed"], KD)
            wr = cols(1, "w_router").rearrange("p (k e) -> p k e", e=N_EXP)
            for j in range(TT):
                for k in range(KD):
                    mm = pe.matmul(bank[5][0:TOKS[j], j * N_EXP:(j + 1) * N_EXP], sq[:, k, j * P:j * P + TOKS[j]],
                                   wr[:, k, :], start=(k == 0), stop=(k == KD - 1))
            mm.then_inc(F["logits"], 1)
            for j in range(TT):
                for half in range(2):
                    b = (2 * j + half) % BANKS
                    if 2 * j + half >= BANKS:
                        pe.wait_ge(F["ntok"], 2 * j + half - BANKS + 1)
                    for c in range(4):
                        k = half * 4 + c
                        mm = pe.transpose(bank[b][0:TOKS[j], c * P:(c + 1) * P], sq[:, k, j * P:j * P + TOKS[j]],
                                          ident[:, :])
                    mm.then_inc(F["turned"], 1)
            pe.wait_ge(F["member"], 1)
            for j in range(TT + 1):
                n = TOKS[j] if j < TT else P
                for i in range(min(j, TT - 1) + 1):
                    w = before if i == j else ones[1]
                    mm = pe.matmul(bank[6][0:n, j * N_EXP:(j + 1) * N_EXP], w[0:TOKS[i], 0:n],
                                   member[0:TOKS[i], i, 0:N_EXP], start=(i == 0), stop=(i == min(j, TT - 1)))
            mm.then_inc(F["ranks"], 1)

        def experts(pe, S, units):
            def gather(ks=range(KD)):
                for k in ks:
                    for j in range(TT):
                        mm = pe.matmul(bank[XG_BANK[k // 4]][:, (k % 4) * CAP:(k % 4 + 1) * CAP],
                                       ntok[0:TOKS[j], j, k * P:(k + 1) * P], onehot[0:TOKS[j], j, :],
                                       start=(j == 0), stop=(j == TT - 1))
                    if k % 4 == 3:
                        mm.then_inc(S["gathered"], 1)

            def add_back(u, k):
                if k == 0:
                    pe.wait_ge(S["back"], u + 1)
                    pe.wait_ge(S["y_lo"], 2 * u + 2)
                pe.wait_ge(S["sc_free"], KD * u + (k + 1))
                out = bank[2 + k % 2][:, 0:T]
                pe.matmul(out, y_hi[:, k * P:(k + 1) * P], back, start=True, stop=False)
                pe.matmul(out, y_lo[:, k * P:(k + 1) * P], back, start=False, stop=True).then_inc(
                    S["sc_ready"], 1)

            def turn_back(u):
                for i in range(TT):
                    pe.transpose(bank[4][:, i * P:i * P + TOKS[i]], onehot[0:TOKS[i], i, :],
                                 ident[0:TOKS[i], 0:TOKS[i]])
                for i in range(TT):
                    mm = pe.matmul(bank[4][:, T:T + 1], onehot[0:TOKS[i], i, :], weight_col[0:TOKS[i], i:i + 1],
                                   start=(i == 0), stop=(i == TT - 1))
                mm.then_inc(S["back_turned"], 1)

            def turn(n, u):
                if n:
                    pe.wait_ge(S["hexp_lo"], NG * u + n)
                pe.wait_ge(S["htok"], NG * u + (n + 1))
                for i in range(4):
                    mm = pe.transpose(bank[4][:, i * P:(i + 1) * P], htok[n % 2][:, i * P:(i + 1) * P],
                                      ident[:, :])
                mm.then_inc(S["turned"], 1)

            pe.wait_ge(F["ntok"], 2 * TT)
            pe.wait_ge(S["onehot"], 1)
            gather()
            with pe.Fori(0, units) as u:
                for q in range(UNIT_Q):
                    pos = q % SPLITS
                    n, r = divmod(q, GROUP_Q)
                    if q < 4 and q % 2 == 0:
                        pe.wait_ge(S["xg_lo"], 2 * u + (q // 2 + 1))
                    elif q == GROUP_Q:
                        pe.wait_ge(S["sc_free"], KD * u + 2)
                        pe.wait_ge(S["next_back"], u + 1)
                    elif q < DOWN_Q0 and r == 0:
                        pe.wait_ge(S["htok"], NG * u + (n - 1))
                    elif q >= DOWN_Q0 and (q - DOWN_Q0) % 4 == 0:
                        pe.wait_ge(S["hexp_lo"], NG * u + ((q - DOWN_Q0) // 4 + 1))
                    pe.wait_ge(S["lo"], UNIT_Q * u + (q + 1))
                    for i in range(2):
                        cols_ = slice(i * 512, (i + 1) * 512)
                        if q < DOWN_Q0:
                            k, last = 2 * (r % 4) + i, KD - 1
                            out, xh, xl = bank[2 * (n % 2) + r // 4], xg_hi[:, k, :], xg_lo[:, k, :]
                        else:
                            k, last = q - DOWN_Q0, KE - 1
                            out, xh, xl = bank[6 + i], hexp_hi[:, k, :], hexp_lo[:, k, :]
                        mm = pe.matmul(out[:, :], xh, whi[:, pos, cols_], start=(k == 0), stop=False)
                        if i == 0:
                            mm.then_inc(S["used"], 1)
                        pe.matmul(out[:, :], xh, wlo[:, pos, cols_], start=False, stop=False)
                        mm = pe.matmul(out[:, :], xl, whi[:, pos, cols_], start=False, stop=(k == last))
                        if k == last:
                            mm.then_inc(S["down"] if q >= DOWN_Q0 else S["up"] if r // 4 else S["gate"], 1)
                    if q == TURN_Q:
                        turn_back(u)
                    elif q >= GROUP_Q and r == 1 and n <= NG:
                        turn(n - 1, u)
                    if q in GATHER_Q:
                        if q == GATHER_Q[0]:
                            pe.wait_ge(S["onehot"], u + 2)
                        gather([GATHER_Q.index(q)])
                    if SUMS_Q <= q < SUMS_Q + KD:
                        add_back(u, q - SUMS_Q)
            for k in range(KD):
                add_back(units, k)

        @block.tensor
        def _(pe):
            at = [0]

            def block_of(S, q, w):
                return (whi[:, q % SPLITS, w * P:(w + 1) * P], wlo[:, q % SPLITS, w * P:(w + 1) * P])

            def project(first_chunk, n_chunks, hi, lo, waits=None, S=dense, between=None):
                for i in range(n_chunks):
                    c = first_chunk + i
                    if c >= BANKS:
                        pe.wait_ge(acc_evac, c - BANKS + 1)
                    out = bank[c % BANKS][:, 0:T]
                    for k in range(len(hi)):
                        q, w = divmod(at[0], QBLOCKS)
                        if w == 0:
                            pe.wait_ge(S["lo"], q + 1)
                        if i == 0 and waits:
                            pe.wait_ge(waits, k + 1)
                        wh, wl = block_of(S, q, w)
                        mm = pe.matmul(out, wh, hi[k], start=(k == 0), stop=False)
                        if w == 0:
                            mm.then_inc(S["used"], 1)
                        pe.matmul(out, wh, lo[k], start=False, stop=False)
                        mm = pe.matmul(out, wl, hi[k], start=False, stop=(k == len(hi) - 1))
                        at[0] += 1
                    mm.then_inc(acc_ready, 1)
                    if between:
                        between()

            def average(out, d, srcs, signal, waits=None):
                for k, s in enumerate(srcs):
                    if waits:
                        pe.wait_ge(waits[0], waits[1] + k)
                    mm = pe.matmul(out[:, 0:T], ones[d][:, :], s, start=(k == 0), stop=(k == len(srcs) - 1))
                mm.then_inc(signal, 1)

            def both(a, b, n):
                return [a[:, k, :] for k in range(n)], [b[:, k, :] for k in range(n)]

            ghs = both(gh_hi, gh_lo, KD)
            mix = both(hid_hi, hid_lo, KD)
            pe.wait_ge(consts, len(ones) + 10)
            for l in range(DEPTH):
                S, B = L[l], BASE[l]
                average(bank[4], D_MODEL, [sq[:, k, :] for k in range(KD)], S["ms"], (S["sq_mix"], 1))
                project(B["zc"], N_ZC, *mix, S["gh_mix"])
                tap = iter(range(TAPS_C))

                def some_taps():
                    for _ in range(TAPS_PE):
                        k = next(tap, None)
                        if k is None:
                            return
                        if k == 0:
                            pe.wait_ge(S["glu"], 1)
                        pe.wait_ge(diag_ready, l * TAPS_C + k + 1)
                        pe.matmul(bank[6][:, 0:SEQ], diag[:, k % DIAGS, :], cpad[:, 0, k:k + SEQ], start=(k == 0),
                                  stop=(k == TAPS_C - 1)).then_inc(diag_used, 1)

                project(B["zab"], 2 * CB, *mix, between=some_taps)
                average(bank[5], D_B, [zb[:, c, :] for c in range(CB)], S["mean"], (S["gelu"], 1))
                project(B["zab"] + 2 * CB, 2, *mix, between=some_taps)
                pe.wait_ge(S["squared"], 1)
                average(bank[5], D_B, [sq[:, c, :] for c in range(CB)], S["variance"])
                project(B["zab"] + 2 * CB + 2, 3 * CA - 2, *mix, between=some_taps)
                pe.wait_ge(S["ln_b"], CB)
                for t in range(CHUNKS):
                    for c in range(CB):
                        mm = pe.transpose(bank[5][:, (t * CB + c) * P:(t * CB + c + 1) * P],
                                          lnb[:, c, t * P:(t + 1) * P], ident[:, :])
                mm.then_inc(S["vt"], 1)
                average_c = [cv[:, c, :] for c in range(CC)]
                pe.wait_ge(S["taps"], 1)
                pe.wait_ge(conv_0, l + 1)
                average(bank[4], D_C, average_c, S["mean"])
                project(B["pp"], BANKS, *both(p_hi, p_lo, KP), S["p_lo"])
                pe.wait_ge(S["vtok"], 1)
                pe.wait_ge(S["w_sT"], 1)
                wsT = cols(l, "w_sT").rearrange("p (h t) -> p h t", t=P)
                for t in range(CHUNKS):
                    for c in range(CB):
                        for j in range(2):
                            mm = pe.matmul(bank[6 + t][:, (c * 2 + j) * P:(c * 2 + j + 1) * P],
                                           vtok[:, t, c * P:(c + 1) * P], wsT[:, 2 * c + j, :], start=True, stop=True)
                mm.then_inc(S["mixed"], 1)
                pe.wait_ge(S["squared"], 2)
                average(bank[5], D_C, [sq[:, CA + CB + c, :] for c in range(CC)], S["variance"])

                def group_norm(g, d, rows):
                    pe.wait_ge(S["ys_sq"], g + 1)
                    average(bank[4 + g], d, [sq[:, c, :] for c in rows], S["y_ms"])

                group_norm(0, D_A, range(CA))
                pe.wait_ge(S["root_v"], 2)
                group_norm(1, D_B, range(CA, CA + CB))
                project(B["pp"] + BANKS, KD - BANKS, *both(p_hi, p_lo, KP))
                group_norm(2, D_C, range(CA + CB, KD))
                project(B["wo"], KD, *mix, S["yn"])
                average(bank[4], D_MODEL, [sq[:, k, :] for k in range(KD)], S["ms"], (S["sq_ffn"], 1))
                if l == 0:
                    hids = both(hid_hi, hid_lo, KH)
                    project(B["ff"], KF, *ghs, S["gh_ffn"])
                    project(B["down"], KD, *hids, S["hid"])
                    project(B["ff2"], KF, *ghs)
                    project(B["down2"], KD, *hids, S["hid2"])
                else:
                    route(pe)
                    experts(pe, M[0], N_EXP)
                    pe.wait_ge(flag_ready, 1)
                    some = pe.value_load(flag[0:1, 0:1], min_val=0, max_val=1)
                    with pe.If(some > 0):
                        experts(pe, M[1], UNITS - N_EXP)
                    at[0] = 0
                average(bank[4], D_MODEL, [sq[:, k, :] for k in range(KD)], S["ms"], (S["sq_ple"], 1))
                project(B["ple"], KD, *ghs, S["gh_ple"], tail if l else dense)
            average(bank[4], D_MODEL, [sq[:, k, :] for k in range(KD)], F["ms_fin"], (L[1]["y_fin_sq"], 1))

        def quarter_at(q):
            return ring[:, q // QUARTERS % RING, q % QUARTERS * (QBLOCKS * P):(q % QUARTERS + 1) * (QBLOCKS * P)]

        def expert_functions(act, S, units, slot_landed, landed_before):
            def high(u, q):
                s = q // QUARTERS
                if q % QUARTERS == 0:
                    act.wait_ge(slot_landed[s % RING],
                                u * (16 * UNIT_SLOTS // RING) + 16 * (s // RING + 1 + landed_before[s % RING]))
                act.wait_ge(S["used"], UNIT_Q * u + (q + 2))
                nc.scalar.activation(whi[:, q % SPLITS, :], quarter_at(q), ACT.Copy).then_inc(S["hi"], 1)

            def gathered_high(half):
                return nc.scalar.activation(xg_hi[:, half * 4:half * 4 + 4, :].rearrange("p c t -> p (c t)"),
                                            bank[XG_BANK[half]][:, :], ACT.Copy)

            for half in range(2):
                act.wait_ge(S["gathered"], half + 1)
                gathered_high(half).then_inc(S["xg_hi"], 1)
            def result_high(u, half):
                act.wait_ge(S["down"], 2 * u + (half + 1))
                nc.scalar.activation(y_hi[:, half * 512:(half + 1) * 512], bank[6 + half][:, :],
                                     ACT.Copy, scale=slot_gate).then_inc(S["y_hi"], 1)

            with act.Fori(0, units) as u:
                nc.scalar.activation(top[:, 4, 0:1], eps[:, :], ACT.Silu)
                for q in range(UNIT_Q):
                    n, r = divmod(q, GROUP_Q)
                    if r == 2 and 1 <= n <= NG:
                        act.wait_ge(S["turned"], NG * u + n)
                        nc.scalar.activation(hexp_hi[:, 4 * n - 4:4 * n, :].rearrange("p c t -> p (c t)"),
                                             bank[4][:, :], ACT.Copy).then_inc(S["hexp_hi"], 1)
                    high(u, q + AHEAD)
                    if q < 2:
                        result_high(u, q)
                    if r == 4 and n < NG:
                        act.wait_ge(S["gate"], NG * u + (n + 1))
                        if n:
                            act.wait_ge(S["htok"], NG * u + n)
                        nc.scalar.activation(sg, bank[2 * (n % 2)][:, :], ACT.Silu).then_inc(S["silu"], 1)
                    for half in range(2):
                        if q == XG_Q[half]:
                            act.wait_ge(S["up"], NG * u + NG)
                            act.wait_ge(S["gathered"], 2 * u + (half + 3))
                            gathered_high(half).then_inc(S["xg_hi"], 1)
                act.wait_ge(S["sc_ready"], KD * u + KD)
                act.wait_ge(S["next_back"], u + 1)
                nc.scalar.activation(back, next_back, ACT.Copy).then_inc(S["back"], 1)
            for half in range(2):
                result_high(units, half)

        @block.scalar
        def _(act):
            def root_of(src, dst, ready, signal):
                act.wait_ge(*ready)
                nc.scalar.activation(dst, src[:, 0:T], ACT.Sqrt, bias=eps[:, :]).then_inc(signal, 1)

            done_hi = [0]

            def high_upto(n, S=dense):
                before = 0 if S is dense else (PRE_MOE + N_EXP * UNIT_SLOTS) * QUARTERS
                for q in range(done_hi[0], n):
                    s = (before + q) // QUARTERS
                    if (before + q) % QUARTERS == 0:
                        act.wait_ge(landed[s % RING], 16 * (s // RING + 1))
                    if q >= SPLITS:
                        act.wait_ge(S["used"], q - SPLITS + 2)
                    nc.scalar.activation(whi[:, q % SPLITS, :], quarter_at(before + q), ACT.Copy).then_inc(S["hi"], 1)
                done_hi[0] = max(done_hi[0], n)

            def embedding_rows(l, k):
                chunk = BASE[l]["pp"] + k
                act.wait_ge(acc_ready, chunk + 1)
                act.wait_ge(acc_evac, chunk)
                if k == 0:
                    act.wait_ge(L[l]["taps"], 1)
                nc.scalar.activation(pp[:, k, :], bank[chunk % BANKS][:, 0:T], ACT.Copy).then_inc(acc_evac, 1)

            act.wait_ge(consts, len(ones) + 10)
            act.wait_ge(x_loaded, 16)
            for k in range(KD):
                nc.scalar.activation(sq[:, k, :], h[:, k, :], ACT.Square).then_inc(L[0]["sq_mix"], 1)
            high_upto(AHEAD)
            for l in range(DEPTH):
                S, B = L[l], BASE[l]
                root_of(bank[4], root[:, :], (S["ms"], 1), S["root"])
                for c in range(CC):
                    high_upto(dense_quarters(B["zc"] + 2 * c + 1))
                    act.wait_ge(acc_evac, B["zc"] + 2 * c + 2)
                    nc.scalar.activation(sig[:, c % 2, :], pp[:, 2 * c + 1, :], ACT.Sigmoid).then_inc(S["sigmoid_zc"], 1)
                    if c == 1:
                        act.wait_ge(S["glu"], 2)
                for c in range(CB):
                    high_upto(dense_quarters(B["zab"] + c))
                    act.wait_ge(acc_evac, B["zab"] + c + 1)
                    nc.scalar.activation(zb[:, c, :], ycat[:, c, :], ACT.Gelu_apprx_tanh).then_inc(S["gelu"], 1)
                for c in range(CB, 2 * CB):
                    high_upto(dense_quarters(B["zab"] + c))
                    act.wait_ge(acc_evac, B["zab"] + c + 1)
                    nc.scalar.activation(zb[:, c, :], ycat[:, c, :], ACT.Gelu_apprx_tanh).then_inc(S["gelu"], 1)
                high_upto(dense_quarters(B["zab"] + 2 * CB + 1))
                act.wait_ge(S["centred"], 1)
                nc.scalar.activation(sq[:, 0:CB, :], lnb[:, :, :], ACT.Square).then_inc(S["squared"], 1)
                root_of(bank[5], root[:, :], (S["variance"], 1), S["root_v"])
                act.wait_ge(S["scaled"], 1)
                for c in range(CB):
                    nc.scalar.activation(lnb[:, c, :], lnb[:, c, :], ACT.Identity, bias=col(l, "b_ln_b", c),
                                         scale=col(l, "g_ln_b", c)).then_inc(S["ln_b"], 1)
                for c in range(2 * CB + 2, N_ZAB):
                    high_upto(dense_quarters(B["zab"] + c))
                act.wait_ge(diag_used, (l + 1) * TAPS_C)
                nc.scalar.activation(cv[:, 0, 0:SEQ], bank[6][:, 0:SEQ], ACT.Identity,
                                     bias=col(l, "b_conv_c")).then_inc(conv_0, 1)
                high_upto(dense_quarters(B["pp"] + BANKS - 1))
                for k in range(BANKS):
                    embedding_rows(l, k)
                high_upto(NEED[B["pp"] + KD - 1])
                act.wait_ge(S["centred"], 2)
                nc.scalar.activation(sq[:, CA + CB:KD, :], cv[:, :, :], ACT.Square).then_inc(S["squared"], 1)
                root_of(bank[5], root[:, :], (S["variance"], 2), S["root_v"])
                rows = (range(CA), range(CA, CA + CB), range(CA + CB, KD))

                def square_rows(g, ready):
                    act.wait_ge(*ready)
                    c = slice(rows[g][0], rows[g][-1] + 1)
                    nc.scalar.activation(sq[:, c, :], ycat[:, c, :], ACT.Square).then_inc(S["ys_sq"], 1)

                def high_rows(g):
                    for c in rows[g]:
                        act.wait_ge(S["y_normed"], c + 1)
                        nc.scalar.activation(hid_hi[:, c, :], ycat[:, c, :], ACT.Copy).then_inc(S["yn_hi"], 1)

                square_rows(0, (S["y_a"], 1))
                square_rows(1, (S["y_b"], 1))
                for g in range(2):
                    root_of(bank[4 + g], sig[:, g, :], (S["y_ms"], g + 1), S["y_root"])
                act.wait_ge(S["scaled"], 2)
                for c in range(CC):
                    nc.scalar.activation(ycat[:, CA + CB + c, :], cv[:, c, :], ACT.Silu, bias=col(l, "b_ln_c", c),
                                         scale=col(l, "g_ln_c", c)).then_inc(S["y_c"], 1)
                square_rows(2, (S["y_c"], CC))
                high_rows(0)
                root_of(bank[6], root[:, :], (S["y_ms"], 3), S["y_root"])
                high_rows(1)
                for k in range(BANKS, KD):
                    embedding_rows(l, k)
                high_rows(2)
                high_upto(dense_quarters(B["pp"] + KD - 1))
                for k in range(KD):
                    high_upto(dense_quarters(B["wo"] + k))
                    act.wait_ge(acc_evac, B["wo"] + k + 1)
                    nc.scalar.activation(sq[:, k, :], h[:, k, :], ACT.Square).then_inc(S["sq_ffn"], 1)
                root_of(bank[4], root[:, :], (S["ms"], 2), S["root"])
                if l == 0:
                    for half, (ff, down, hid) in enumerate((("ff", "down", "hid"), ("ff2", "down2", "hid2"))):
                        for f in range(KH):
                            high_upto(dense_quarters(B[ff] + 2 * f))
                            act.wait_ge(acc_evac, B[ff] + 2 * f + 1)
                            n = half * KH + f
                            if n >= 2:
                                act.wait_ge(S["hid_f32"], n - 1)
                            nc.scalar.activation(sig[:, n % 2, :], up[:, n % 2, :], ACT.Silu).then_inc(S["silu"], 1)
                            high_upto(dense_quarters(B[ff] + 2 * f + 1))
                            act.wait_ge(S["hid_f32"], n + 1)
                            if half and f == 0:
                                act.wait_ge(acc_evac, B["down"] + KD)
                            nc.scalar.activation(hid_hi[:, f, :], zb[:, 2 + n % 2, :], ACT.Copy).then_inc(S["hid_hi"], 1)
                        for k in range(KD):
                            high_upto(dense_quarters(B[down] + k))
                            if half:
                                act.wait_ge(acc_evac, B[down] + k + 1)
                                nc.scalar.activation(sq[:, k, :], h[:, k, :], ACT.Square).then_inc(S["sq_ple"], 1)
                else:
                    for q in range(AHEAD):
                        if q == 0:
                            act.wait_ge(landed[0], 16 * (PRE_MOE // RING + 1))
                        act.wait_ge(acc_evac, B["wo"] + KD)
                        nc.scalar.activation(whi[:, q, :], quarter_at(q), ACT.Copy).then_inc(M[0]["hi"], 1)
                    for i in range(2 * TT):
                        j, half = divmod(i, 2)
                        act.wait_ge(F["turned"], i + 1)
                        nc.scalar.activation(ntok[0:TOKS[j], j, half * 512:(half + 1) * 512],
                                             bank[i % BANKS][0:TOKS[j], :], ACT.Copy).then_inc(F["ntok"], 1)
                    act.wait_ge(F["exp_in"], 1)
                    nc.scalar.activation(top[:, 3, :], top[:, 2, :], ACT.Exp).then_inc(F["exp_out"], 1)
                    expert_functions(act, M[0], N_EXP, landed, [PRE_MOE // RING] * RING)
                    act.wait_ge(M[0]["hi"], N_EXP * UNIT_Q + AHEAD)
                    act.wait_ge(flag_ready, 1)
                    some = act.value_load(flag[0:1, 0:1], min_val=0, max_val=1)
                    with act.If(some > 0):
                        for _ in range(AHEAD):
                            act.nop().then_inc(M[1]["hi"], 1)
                        expert_functions(act, M[1], UNITS - N_EXP, over_landed, [-1] + [0] * (RING - 1))
                        act.wait_ge(M[1]["hi"], (UNITS - N_EXP) * UNIT_Q + AHEAD)
                    for _ in range(AHEAD):
                        act.nop().then_inc(tail["hi"], 1)
                    done_hi[0] = AHEAD
                    for k in range(KD):
                        act.wait_ge(S["gh_ple"], k + 1)
                        nc.scalar.activation(sq[:, k, :], h[:, k, :], ACT.Square).then_inc(S["sq_ple"], 1)
                root_of(bank[4], root[:, :], (S["ms"], 3), S["root"])
                done = L[l + 1]["sq_mix"] if l + 1 < DEPTH else S["y_fin_sq"]
                made = L[l + 1]["gh_mix"] if l + 1 < DEPTH else S["y_fin_h"]
                for k in range(KD):
                    if l:
                        high_upto(tail_quarters(k), tail)
                    else:
                        high_upto(dense_quarters(B["ple"] + k))
                    act.wait_ge(acc_evac, B["ple"] + k + 1)
                    nc.scalar.activation(sig[:, k % 2, :], up[:, k % 2, :], ACT.Sigmoid).then_inc(S["sig_ple"], 1)
                    if k:
                        act.wait_ge(made, k)
                        nc.scalar.activation(sq[:, k - 1, :], h[:, k - 1, :], ACT.Square).then_inc(done, 1)
                act.wait_ge(made, KD)
                nc.scalar.activation(sq[:, KD - 1, :], h[:, KD - 1, :], ACT.Square).then_inc(done, 1)
            root_of(bank[4], root[:, :], (F["ms_fin"], 1), F["root_fin"])

        def route_tokens(dve, link, S):
            v = nc.vector
            for k in range(KD):
                v.scalar_tensor_tensor(sq[:, k, :], h[:, k, :], col(1, "g_ffn", k), rstd[:, :], ALU.mult,
                                       ALU.mult).then_inc(F["normed"], 1)
            for q in range(AHEAD):
                dve.wait_ge(M[0]["hi"], q + 1)
                v.tensor_tensor(wlo[:, q, :], quarter_at(q), whi[:, q, :].bitcast(F32),
                                ALU.subtract).then_inc(M[0]["lo"], 1)
            dve.wait_ge(F["logits"], 1)
            link(v.tensor_copy(logit, bank[5][:, 0:TT * N_EXP].rearrange("p (j e) -> p j e", e=N_EXP)))
            shape = [P, TT, N_EXP, N_EXP]
            others = logit.unsqueeze(2).to_broadcast(shape)
            mine = logit.unsqueeze(3).to_broadcast(shape)
            for j in range(TT):
                v.tensor_tensor(beats[:, j], others[:, j], mine[:, j], ALU.is_gt)
                link(v.tensor_tensor(ties[:, j], others[:, j], mine[:, j], ALU.is_equal))
                link(v.tensor_tensor(ties[:, j], ties[:, j], lt8[:, :, :], ALU.mult))
            link(v.tensor_tensor(beats, beats, ties, ALU.add))
            link(v.tensor_reduce(rank, beats, AX_X, ALU.add))
            v.tensor_scalar(first, rank, 0.0, None, ALU.is_equal)
            link(v.tensor_scalar(second, rank, 1.0, None, ALU.is_equal))
            link(v.tensor_tensor(tmp8, logit, first, ALU.mult))
            link(v.tensor_reduce(top[:, 0, :], tmp8, AX_X, ALU.add))
            link(v.tensor_tensor(tmp8, logit, second, ALU.mult))
            link(v.tensor_reduce(top[:, 1, :], tmp8, AX_X, ALU.add))
            v.tensor_tensor(top[:, 2, :], top[:, 1, :], top[:, 0, :], ALU.subtract).then_inc(F["exp_in"], 1)
            for r in range(ROUNDS + 1):
                n = min(N_EXP, UNITS + 1 - r * N_EXP)
                i = v.tensor_tensor(member[:, :, r * N_EXP:r * N_EXP + n], first[:, :, 0:n], second[:, :, 0:n], ALU.add)
            i.then_inc(F["member"], 1)
            dve.wait_ge(F["exp_out"], 1)
            link(v.tensor_scalar(top[:, 4, :], top[:, 3, :], 1.0, None, ALU.add))
            link(v.reciprocal(top[:, 0, :], top[:, 4, :]))
            link(v.tensor_tensor(top[:, 1, :], top[:, 3, :], top[:, 0, :], ALU.mult))
            full = [P, TT, N_EXP]
            link(v.tensor_tensor(first, first, top[:, 0, :].unsqueeze(2).to_broadcast(full), ALU.mult))
            link(v.tensor_tensor(second, second, top[:, 1, :].unsqueeze(2).to_broadcast(full), ALU.mult))
            for r in range(ROUNDS + 1):
                n = min(N_EXP, UNITS + 1 - r * N_EXP)
                i = v.tensor_tensor(weight[:, :, r * N_EXP:r * N_EXP + n], first[:, :, 0:n], second[:, :, 0:n], ALU.add)
            link(i)
            dve.wait_ge(F["ranks"], 1)
            for r in range(ROUNDS + 1):
                n = min(N_EXP, UNITS + 1 - r * N_EXP)
                v.tensor_scalar(place[:, :, r * N_EXP:r * N_EXP + n],
                                bank[6][:, 0:TT * N_EXP].rearrange("p (j e) -> p j e", e=N_EXP)[:, :, 0:n],
                                float(r * CAP), None, ALU.subtract)
            link(v.tensor_reduce(most[0:1, :], bank[6][0:1, TT * N_EXP:(TT + 1) * N_EXP], AX_X, ALU.max))
            v.tensor_scalar(flag[0:1, 0:1], most[0:1, :], float(CAP), None, ALU.is_gt).then_inc(flag_ready, 1)
            dve.wait_ge(flag_ready, 1)

        def expert_rows(dve, S, units, first_unit):
            v = nc.vector

            def one_hot(u):
                for j in range(TT):
                    n = TOKS[j]
                    v.tensor_scalar(onehot[0:n, j, :], iota[0:n, :], place[0:n, j, bass.ds(u, 1)],
                                    member[0:n, j, bass.ds(u, 1)], ALU.is_equal, ALU.mult)
                v.tensor_copy(weight_col, weight[:, :, bass.ds(u, 1)].rearrange("p j o -> p (j o)")).then_inc(
                    S["onehot"], 1)

            def add_sum(u, k):
                dve.wait_ge(S["sc_ready"], KD * u + (k + 1))
                v.tensor_tensor(h[:, k, :], h[:, k, :], bank[2 + k % 2][:, 0:T], ALU.add).then_inc(S["sc_free"], 1)

            def low(u, q):
                dve.wait_ge(S["hi"], UNIT_Q * u + (q + 1))
                v.tensor_tensor(wlo[:, q % SPLITS, :], quarter_at(q), whi[:, q % SPLITS, :].bitcast(F32),
                                ALU.subtract).then_inc(S["lo"], 1)

            for i in range(SPLITS):
                dve.nop().then_inc(S["used"], 1)
            for i in range(2):
                dve.nop().then_inc(S["sc_free"], 1)
            v.memset(slot_gate, 0.0).then_inc(S["down"], 1)
            v.memset(back.bitcast(F32), 0.0).then_inc(S["back"], 1)
            dve.nop().then_inc(S["down"], 1)
            one_hot(first_unit)

            def gathered_low(half):
                c = slice(half * 4, half * 4 + 4)
                v.tensor_tensor(xg_lo[:, c, :].rearrange("p c t -> p (c t)"), bank[XG_BANK[half]][:, :],
                                xg_hi[:, c, :].rearrange("p c t -> p (c t)").bitcast(F32),
                                ALU.subtract).then_inc(S["xg_lo"], 1)

            for half in range(2):
                dve.wait_ge(S["xg_hi"], half + 1)
                gathered_low(half)
            def result_low(u, half):
                dve.wait_ge(S["y_hi"], 2 * u + (half + 1))
                c = slice(half * 512, (half + 1) * 512)
                v.scalar_tensor_tensor(y_lo[:, c], bank[6 + half][:, :], slot_gate, y_hi[:, c].bitcast(F32),
                                       ALU.mult, ALU.subtract).then_inc(S["y_lo"], 1)

            with dve.Fori(0, units) as u:
                for q in range(UNIT_Q):
                    n, r = divmod(q, GROUP_Q)
                    if r == 0 and 1 <= n <= NG:
                        dve.wait_ge(S["up"], NG * u + n)
                        dve.wait_ge(S["silu"], NG * u + n)
                        v.tensor_tensor(htok[(n - 1) % 2], sg, bank[2 * ((n - 1) % 2) + 1][:, :],
                                        ALU.mult).then_inc(S["htok"], 1)
                    elif r == 2 and 1 <= n <= NG:
                        c = slice(4 * n - 4, 4 * n)
                        dve.wait_ge(S["hexp_hi"], NG * u + n)
                        v.tensor_tensor(hexp_lo[:, c, :].rearrange("p c t -> p (c t)"), bank[4][:, :],
                                        hexp_hi[:, c, :].rearrange("p c t -> p (c t)").bitcast(F32),
                                        ALU.subtract).then_inc(S["hexp_lo"], 1)
                    low(u, q + AHEAD)
                    if SUMS_Q <= q < SUMS_Q + KD:
                        add_sum(u, q - SUMS_Q)
                    for half in range(2):
                        if q == XG_Q[half]:
                            dve.wait_ge(S["xg_hi"], 2 * u + (half + 3))
                            gathered_low(half)
                    if q < 2:
                        result_low(u, q)
                    elif q == TURN_Q + 2:
                        dve.wait_ge(S["back_turned"], u + 1)
                        dve.wait_ge(S["back"], u + 1)
                        dve.wait_ge(S["y_lo"], 2 * u + 2)
                        v.tensor_copy(slot_gate, bank[4][:, T:T + 1])
                        v.tensor_copy(next_back, bank[4][:, 0:T]).then_inc(S["next_back"], 1)
                    elif q == ONEHOT_Q:
                        one_hot(u + (first_unit + 1))
            for half in range(2):
                result_low(units, half)
            for k in range(KD):
                add_sum(units, k)
            dve.wait_ge(S["sc_free"], KD * (units + 1) + 2)

        @block.vector
        def _(dve):
            steps = [0]

            def link(ins):
                steps[0] += 1
                ins.then_inc(dve_step, 1)
                dve.wait_ge(dve_step, steps[0])

            def tick(ins):
                steps[0] += 1
                ins.then_inc(dve_step, 1)
                return steps[0]

            done_lo = [0]

            def low_upto(n, S=dense):
                before = 0 if S is dense else (PRE_MOE + N_EXP * UNIT_SLOTS) * QUARTERS
                for q in range(done_lo[0], n):
                    dve.wait_ge(S["hi"], q + 1)
                    nc.vector.tensor_tensor(wlo[:, q % SPLITS, :], quarter_at(before + q),
                                            whi[:, q % SPLITS, :].bitcast(F32), ALU.subtract).then_inc(S["lo"], 1)
                done_lo[0] = max(done_lo[0], n)

            def gain(l, name, k, signal, hi=gh_hi, lo=gh_lo):
                link(nc.vector.tensor_scalar(hi[:, k, :], h[:, k, :], col(l, name, k), None, ALU.mult))
                nc.vector.scalar_tensor_tensor(lo[:, k, :], h[:, k, :], col(l, name, k), hi[:, k, :].bitcast(F32),
                                               ALU.mult, ALU.subtract).then_inc(signal, 1)

            def reciprocal_root(ready, dst=rstd, src=root[:, :]):
                dve.wait_ge(*ready)
                link(nc.vector.reciprocal(dst[:, :], src))

            def evacuate(chunk, dst, scale=rstd):
                if chunk < BASE[1]["ple"]:
                    low_upto(NEED[chunk])
                dve.wait_ge(acc_ready, chunk + 1)
                nc.vector.tensor_tensor(dst, bank[chunk % BANKS][:, 0:T], scale[:, :], ALU.mult).then_inc(acc_evac, 1)

            def add_to_h(chunk, k):
                low_upto(NEED[chunk])
                dve.wait_ge(acc_ready, chunk + 1)
                nc.vector.tensor_tensor(h[:, k, :], h[:, k, :], bank[chunk % BANKS][:, 0:T], ALU.add).then_inc(acc_evac, 1)
                dve.wait_ge(acc_evac, chunk + 1)

            dve.wait_ge(consts, len(ones) + 10)
            dve.wait_ge(x_loaded, 16)
            dve.wait_ge(par_loaded[0], 16)
            for k in range(KD):
                gain(0, "g_mix", k, L[0]["gh_mix"], hid_hi, hid_lo)
            low_upto(AHEAD)
            for l in range(DEPTH):
                S, B = L[l], BASE[l]
                dve.wait_ge(par_loaded[l], 16)
                dve.wait_ge(loaded[l], 48)
                if l:
                    dve.wait_ge(L[l - 1]["tails"], 1)
                nc.vector.tensor_copy(xa[:, :, :, 0:TAPS_A - 1], sta[:, :, :, :])
                link(nc.vector.tensor_copy(xc[:, :, :, 0:TAPS_C - 1], stc[:, :, :, :]))
                link(nc.vector.tensor_copy(p_hi[:, :, :], pe_in[:, :, :]))
                for k in range(KP):
                    nc.vector.tensor_tensor(p_lo[:, k, :], pe_in[:, k, :], p_hi[:, k, :].bitcast(F32),
                                            ALU.subtract).then_inc(S["p_lo"], 1)
                reciprocal_root((S["root"], 1))

                wc = cols(l, "w_conv_c").rearrange("p (c k) -> p c k", k=TAPS_C)
                for c in range(CC):
                    evacuate(B["zc"] + 2 * c, pp[:, 2 * c, :])
                    evacuate(B["zc"] + 2 * c + 1, pp[:, 2 * c + 1, :])
                    dve.wait_ge(S["sigmoid_zc"], c + 1)
                    dve.wait_ge(acc_evac, B["zc"] + 2 * c + 1)
                    nc.vector.tensor_tensor(cpad[:, c, TAPS_C - 1:], pp[:, 2 * c, 0:SEQ], sig[:, c % 2, 0:SEQ],
                                            ALU.mult).then_inc(S["glu"], 1)
                    nc.vector.tensor_tensor(xc[:, c, :, TAPS_C - 1], pp[:, 2 * c, SEQ:T], sig[:, c % 2, SEQ:T],
                                            ALU.mult).then_inc(S["glu"], 1)
                    low_upto(dense_quarters(B["zc"] + 2 * c + 1))
                dve.wait_ge(S["glu"], 2 * CC)

                def conv_c():
                    for k in range(TAPS_C):
                        for c in range(1, CC):
                            src, dst = cpad[:, c, k:k + SEQ], cv[:, c, 0:SEQ]
                            if k == 0:
                                last[c] = tick(nc.vector.tensor_scalar(dst, src, wc[:, c, 0:1], col(l, "b_conv_c", c),
                                                                       ALU.mult, ALU.add))
                            else:
                                dve.wait_ge(dve_step, last[c])
                                last[c] = tick(nc.vector.scalar_tensor_tensor(dst, src, wc[:, c, k:k + 1], dst,
                                                                              ALU.mult, ALU.add))
                            yield
                    pv = pp[:, :, :].rearrange("p c t -> p (c t)")[:, 0:CC * NB * TAPS_C].rearrange(
                        "p (c b k) -> p c b k", c=CC, k=TAPS_C)
                    w = wc.unsqueeze(2).to_broadcast([P, CC, NB, TAPS_C])
                    for c in range(CC):
                        i = nc.vector.tensor_tensor(pv[:, c], xc[:, c], w[:, c], ALU.mult)
                    link(i)
                    yield
                    for c in range(CC):
                        i = nc.vector.tensor_reduce(cv[:, c, SEQ:T], pv[:, c], AX_X, ALU.add)
                    link(i)
                    yield
                    dve.wait_ge(dve_step, max(last))
                    nc.vector.tensor_tensor(cv[:, :, SEQ:T], cv[:, :, SEQ:T], cols(l, "b_conv_c").unsqueeze(
                        2).to_broadcast([P, CC, NB]), ALU.add).then_inc(S["taps"], 1)
                    yield

                last = [0] * CC
                taps = conv_c()

                def some_taps(n):
                    for _ in range(n):
                        next(taps, None)

                for c in range(2 * CB):
                    evacuate(B["zab"] + c, ycat[:, c, :])
                    some_taps(4)
                    low_upto(dense_quarters(B["zab"] + c))
                    some_taps(3)
                dve.wait_ge(S["mean"], 1)
                dve.wait_ge(S["gelu"], CB)
                nc.vector.tensor_tensor(lnb[:, :, :], zb[:, 0:CB, :], bank[5][:, 0:T].unsqueeze(1).to_broadcast(
                    [P, CB, T]), ALU.subtract).then_inc(S["centred"], 1)

                wa = cols(l, "w_conv_a").rearrange("p (c k) -> p c k", k=TAPS_A)
                at = B["zab"] + 2 * CB
                dve.wait_ge(S["gelu"], 2 * CB)
                for c in range(CA):
                    evacuate(at + 2 * c, pp[:, 6, :])
                    some_taps(3)
                    low_upto(dense_quarters(at + 2 * c))
                    some_taps(3)
                    evacuate(at + 2 * c + 1, pp[:, 7, :])
                    dve.wait_ge(acc_evac, at + 2 * c + 2)
                    nc.vector.tensor_tensor(apad[:, c, TAPS_A - 1:], pp[:, 6, 0:SEQ], pp[:, 7, 0:SEQ], ALU.mult)
                    link(nc.vector.tensor_tensor(xa[:, c, :, TAPS_A - 1], pp[:, 6, SEQ:T], pp[:, 7, SEQ:T], ALU.mult))
                    some_taps(5)
                    if c:
                        low_upto(dense_quarters(at + 2 * c + 1))
                    if c == 0:
                        reciprocal_root((S["root_v"], 1), rstd2)
                        dve.wait_ge(S["centred"], 1)
                        nc.vector.tensor_tensor(lnb[:, :, :], lnb[:, :, :], rstd2[:, :].unsqueeze(1).to_broadcast(
                            [P, CB, T]), ALU.mult).then_inc(S["scaled"], 1)
                        low_upto(dense_quarters(at + 1))
                def mix_a(c):
                    evacuate(at + 2 * CA + c, ycat[:, c, :])
                    for k in range(TAPS_A):
                        src, dst = apad[:, c, k:k + SEQ], up[:, 0, 0:SEQ]
                        link(nc.vector.tensor_scalar(dst, src, wa[:, c, 0:1], None, ALU.mult) if k == 0 else
                             nc.vector.scalar_tensor_tensor(dst, src, wa[:, c, k:k + 1], dst, ALU.mult, ALU.add))
                    pv = prod[:, 0:NB * TAPS_A].rearrange("p (b k) -> p b k", k=TAPS_A)
                    link(nc.vector.tensor_tensor(pv, xa[:, c], wa[:, c, :].unsqueeze(1).to_broadcast([P, NB, TAPS_A]),
                                                 ALU.mult))
                    link(nc.vector.tensor_reduce(up[:, 0, SEQ:T], pv, AX_X, ALU.add))
                    dve.wait_ge(acc_evac, at + 2 * CA + c + 1)
                    i = nc.vector.tensor_tensor(ycat[:, c, :], ycat[:, c, :], up[:, 0, :], ALU.mult)
                    if c == CA - 1:
                        i.then_inc(S["y_a"], 1)
                    else:
                        link(i)
                    low_upto(dense_quarters(at + 2 * CA + c))

                some_taps(TAPS_C * CC)
                for c in range(CA - 1):
                    mix_a(c)
                dve.wait_ge(S["mean"], 2)
                nc.vector.tensor_tensor(cv[:, :, :], cv[:, :, :], bank[4][:, 0:T].unsqueeze(1).to_broadcast([P, CC, T]),
                                        ALU.subtract).then_inc(S["centred"], 1)
                dve.wait_ge(S["vt"], 1)
                nc.vector.tensor_copy(vtok[:, :, :], bank[5][:, :].rearrange("p (j d) -> p j d", j=CHUNKS)).then_inc(
                    S["vtok"], 1)
                low_upto(dense_quarters(B["pp"] + BANKS - 1))
                mix_a(CA - 1)
                low_upto(NEED[B["pp"] + KD - 1])
                dve.wait_ge(S["mixed"], 1)
                dve.wait_ge(S["ln_b"], CB)
                bs = cols(l, "b_s").rearrange("p (c t) -> p c t", t=P)
                for t in range(CHUNKS):
                    for j in range(2):
                        rows = slice(HEAD * j, HEAD * (j + 1))
                        src = bank[6 + t][rows, :].rearrange("p (c j t) -> p j c t", j=2, t=P)[:, j]
                        nc.vector.tensor_tensor(ycat[rows, CA:CA + CB, t * P:(t + 1) * P], src, bs[rows], ALU.add)
                for c in range(CB):
                    i = nc.vector.tensor_scalar(ycat[:, CA + c, SEQ:T], lnb[:, c, SEQ:T], col(l, "w00", c),
                                                bs[:, c, 0:1], ALU.mult, ALU.add)
                link(i)
                dve.wait_ge(S["gelu"], 2 * CB)
                nc.vector.tensor_tensor(ycat[:, CA:CA + CB, :], ycat[:, CA:CA + CB, :], zb[:, CB:2 * CB, :],
                                        ALU.mult).then_inc(S["y_b"], 1)
                reciprocal_root((S["root_v"], 2))
                dve.wait_ge(S["centred"], 2)
                nc.vector.tensor_tensor(cv[:, :, :], cv[:, :, :], rstd[:, :].unsqueeze(1).to_broadcast([P, CC, T]),
                                        ALU.mult).then_inc(S["scaled"], 1)

                dve.wait_ge(S["y_a"], 1)
                dve.wait_ge(S["y_b"], 1)
                groups = ((range(CA), rstd2, sig[:, 0, :]), (range(CA, CA + CB), rstd, sig[:, 1, :]),
                          (range(CA + CB, KD), rstd2, root[:, :]))

                def normed_rows(g):
                    rows, dst, _ = groups[g]
                    for c in rows:
                        nc.vector.scalar_tensor_tensor(ycat[:, c, :], ycat[:, c, :], col(l, "g_out", c), dst[:, :],
                                                       ALU.mult, ALU.mult).then_inc(S["y_normed"], 1)

                def low_rows(g):
                    for c in groups[g][0]:
                        dve.wait_ge(S["yn_hi"], c + 1)
                        nc.vector.tensor_tensor(hid_lo[:, c, :], ycat[:, c, :], hid_hi[:, c, :].bitcast(F32),
                                                ALU.subtract).then_inc(S["yn"], 1)

                for g in range(2):
                    reciprocal_root((S["y_root"], g + 1), *groups[g][1:])
                for g in range(2):
                    normed_rows(g)
                dve.wait_ge(S["y_normed"], CA)
                low_rows(0)
                reciprocal_root((S["y_root"], 3), *groups[2][1:])
                dve.wait_ge(S["y_c"], CC)
                normed_rows(2)
                low_rows(1)
                low_rows(2)
                dve.wait_ge(acc_evac, B["wo"])
                for k in range(KD):
                    add_to_h(B["wo"] + k, k)
                    if l == 0:
                        gain(l, "g_ffn", k, S["gh_ffn"])
                    low_upto(dense_quarters(B["wo"] + k))
                reciprocal_root((S["root"], 2))

                if l == 0:
                    def hidden_low(n):
                        dve.wait_ge(S["hid_hi"], n + 1)
                        f = n % KH
                        nc.vector.tensor_tensor(hid_lo[:, f, :], zb[:, 2 + n % 2, :], hid_hi[:, f, :].bitcast(F32),
                                                ALU.subtract).then_inc(S["hid2" if n >= KH else "hid"], 1)

                    for half, (ff, down) in enumerate((("ff", "down"), ("ff2", "down2"))):
                        for f in range(KH):
                            n = half * KH + f
                            if n >= 2:
                                dve.wait_ge(S["silu"], n - 1)
                            evacuate(B[ff] + 2 * f, up[:, n % 2, :])
                            if f:
                                hidden_low(n - 1)
                            low_upto(dense_quarters(B[ff] + 2 * f))
                            evacuate(B[ff] + 2 * f + 1, zb[:, n % 2, :])
                            dve.wait_ge(acc_evac, B[ff] + 2 * f + 2)
                            dve.wait_ge(S["silu"], n + 1)
                            nc.vector.tensor_tensor(zb[:, 2 + n % 2, :], zb[:, n % 2, :], sig[:, n % 2, :],
                                                    ALU.mult).then_inc(S["hid_f32"], 1)
                            if f < KH - 1:
                                low_upto(dense_quarters(B[ff] + 2 * f + 1))
                        hidden_low(half * KH + KH - 1)
                        low_upto(dense_quarters(B[ff] + KF - 1))
                        for k in range(KD):
                            add_to_h(B[down] + k, k)
                            if half:
                                gain(l, "g_ple", k, S["gh_ple"])
                            low_upto(dense_quarters(B[down] + k))
                else:
                    route_tokens(dve, link, S)
                    expert_rows(dve, M[0], N_EXP, 0)
                    dve.wait_ge(M[0]["lo"], N_EXP * UNIT_Q + AHEAD)
                    dve.wait_ge(flag_ready, 1)
                    some = dve.value_load(flag[0:1, 0:1], min_val=0, max_val=1)
                    with dve.If(some > 0):
                        for _ in range(AHEAD):
                            dve.nop().then_inc(M[1]["lo"], 1)
                        expert_rows(dve, M[1], UNITS - N_EXP, N_EXP)
                        dve.wait_ge(M[1]["lo"], (UNITS - N_EXP) * UNIT_Q + AHEAD)
                    for _ in range(AHEAD):
                        dve.nop().then_inc(tail["lo"], 1)
                    done_lo[0] = AHEAD
                    for k in range(KD):
                        gain(l, "g_ple", k, S["gh_ple"])

                reciprocal_root((S["root"], 3))
                for k in range(KD):
                    if k >= 2:
                        dve.wait_ge(S["sig_ple"], k - 1)
                    if l:
                        low_upto(k + 1, tail)
                    evacuate(B["ple"] + k, up[:, k % 2, :])
                    dve.wait_ge(S["sig_ple"], k + 1)
                    link(nc.vector.tensor_tensor(pp[:, k, :], pp[:, k, :], sig[:, k % 2, :], ALU.mult))
                    if l + 1 < DEPTH:
                        link(nc.vector.tensor_tensor(h[:, k, :], h[:, k, :], pp[:, k, :], ALU.add))
                        gain(l + 1, "g_mix", k, L[l + 1]["gh_mix"], hid_hi, hid_lo)
                        low_upto(dense_quarters(B["ple"] + k))
                    else:
                        nc.vector.tensor_tensor(h[:, k, :], h[:, k, :], pp[:, k, :], ALU.add).then_inc(S["y_fin_h"], 1)
                        low_upto(tail_quarters(k), tail)
            reciprocal_root((F["root_fin"], 1))
            dve.wait_ge(L[DEPTH - 1]["y_fin_h"], KD)
            for k in range(KD):
                nc.vector.scalar_tensor_tensor(ycat[:, k, :], h[:, k, :], col(0, "g_final", k), rstd[:, :], ALU.mult,
                                               ALU.mult).then_inc(F["y_fin"], 1)

def _blocks(w, order=None):
    import numpy as np
    k, n = w.shape
    b = w.reshape(k // P, P, n // P, P).transpose(2, 0, 1, 3)
    if order is not None:
        b = b[np.asarray(order)]
    return b.reshape(-1, P, P)


def _features(a):
    import numpy as np
    lead = a.shape[:-1]
    b = a.reshape(*lead, a.shape[-1] // P, P)
    return np.moveaxis(np.moveaxis(b, -1, 0), -1, 1)


def kernel(**inputs):
    import numpy as np
    import concourse.bacc as _bacc
    from concourse.bass_utils import run_bass_kernel_spmd as _run

    a = {k: np.asarray(v) for k, v in inputs.items()}
    ca = list(range(CA))
    o_gc, o_xa, o_b, o_c = CA, 2 * CA, 3 * CA, 3 * CA + 2 * CB
    in_order = [o_c + CC * j + c for c in range(CC) for j in range(2)]
    in_order += [o_b + CB + c for c in range(CB)] + [o_b + c for c in range(CB)]
    in_order += [o for c in ca for o in (o_gc + c, o_xa + c)] + ca

    def moving(w, n_group):
        k, n = w.shape
        return w.reshape(k // P, P, n // n_group, n_group // P, P).transpose(2, 0, 3, 1, 4).reshape(
            n // n_group, -1, P, P)

    def gate_up(g, u):
        b = np.stack([_blocks(g).reshape(-1, KD, P, P), _blocks(u).reshape(-1, KD, P, P)], axis=1)
        return b.reshape(-1, P, P)

    parts = []
    for l in range(DEPTH):
        parts += [_blocks(a["w_in"][l], in_order), _blocks(a["w_ple_proj"][l]), _blocks(a["w_o"][l])]
        if l == 0:
            n = D_FF // 2
            for c in (slice(0, n), slice(n, D_FF)):
                parts += [gate_up(a["w_ff_gate"][0][:, c], a["w_ff_up"][0][:, c]), _blocks(a["w_ff_down"][0][c])]
        else:
            for e in range(N_EXP):
                parts += [np.stack([moving(a["w_ex_gate"][0, e], 512), moving(a["w_ex_up"][0, e], 512)],
                                   axis=1).reshape(-1, P, P), moving(a["w_ex_down"][0, e], D_MODEL)[0]]
        parts.append(_blocks(a["w_ple_gate"][l]))
    blocks = np.concatenate(parts)
    assert len(blocks) == SLOTS * WBLOCKS
    wstream = np.ascontiguousarray(blocks.reshape(SLOTS, WBLOCKS, P, P).transpose(0, 2, 1, 3)).reshape(
        SLOTS, P, WBLOCKS * P)

    def tokens(prompt, sample):
        return _features(np.concatenate([prompt.reshape(SEQ, -1), sample.reshape(NB, -1)]))

    x = np.ascontiguousarray(tokens(a["x_prompt"], a["x_sample"]))
    p = np.stack([tokens(a["p_prompt"][l], a["p_sample"][l]) for l in range(DEPTH)])
    par = np.zeros((DEPTH, P, NPAR), x.dtype)
    state = []
    heads = np.arange(D_B) // HEAD
    for l in range(DEPTH):
        put = {n: a[n][l] for n in ("g_mix", "g_ln_b", "b_ln_b", "b_conv_c", "g_ln_c", "b_ln_c", "g_out", "g_ffn",
                                    "g_ple", "w_conv_a", "w_conv_c")}
        put["g_final"] = a["g_final"]
        put["b_s"] = a["b_s"][l].T[:, heads]
        put["w00"] = a["w_s"][l][:, 0, 0][heads]
        for n, v in put.items():
            o, size = PAR[n]
            par[l, :, o:o + size] = _features(v).reshape(P, size)
        o, size = PAR["w_sT"]
        par[l, :, o:o + size] = a["w_s"][l].transpose(2, 0, 1).reshape(P, size)
        o, size = PAR["w_router"]
        par[l, :, o:o + size] = a["w_router"][0].reshape(KD, P, N_EXP).transpose(1, 0, 2).reshape(P, size)
        state.append(np.concatenate([_features(a["state_conv_a"][l]).reshape(P, -1),
                                     _features(a["state_conv_c"][l]).reshape(P, -1)], axis=1))
    arrays = {"wstream": wstream, "x_in": x, "p_in": np.ascontiguousarray(p), "par_in": par,
              "state_in": np.ascontiguousarray(np.stack(state))}
    outs = {"y_out": (P, KD, T), "a_prompt": (DEPTH, P, CA, TAPS_A - 1), "a_sample": (DEPTH, P, CA, NB, TAPS_A),
            "c_prompt": (DEPTH, P, CC, TAPS_C - 1), "c_sample": (DEPTH, P, CC, NB, TAPS_C),
            "v_sample": (DEPTH, P, CB, NB)}
    nc = _bacc.Bacc("TRN2", target_bir_lowering=False, num_devices=1)
    aps = [nc.dram_tensor(n, v.shape, F32, kind="ExternalInput").ap() for n, v in arrays.items()]
    aps += [nc.dram_tensor(n, s, F32, kind="ExternalOutput").ap() for n, s in outs.items()]
    build(nc, *aps)
    r = _run(nc, [arrays], core_ids=[0]).results[0]

    def rows(v, lead):
        v = np.moveaxis(np.moveaxis(v, 1, -1), 0, -1)
        return np.ascontiguousarray(v.reshape(*lead, -1))

    y = rows(np.asarray(r["y_out"]), (T,))
    ap, as_, cp, cs, vs = (np.asarray(r[n]) for n in ("a_prompt", "a_sample", "c_prompt", "c_sample", "v_sample"))
    return (y[0:SEQ].reshape(1, SEQ, D_MODEL), y[SEQ:].reshape(NB, 1, D_MODEL),
            np.stack([rows(v, (1, TAPS_A - 1)) for v in ap]), np.stack([rows(v[:, :, :, 1:], (NB, TAPS_A - 1)) for v in as_]),
            np.stack([rows(v, (1, TAPS_C - 1)) for v in cp]), np.stack([rows(v[:, :, :, 1:], (NB, TAPS_C - 1)) for v in cs]),
            np.stack([rows(v, (NB, 1)) for v in vs]))
```
